# Optimizing a Trainium2 kernel written in Bass

```python
import math
import jax, jax.numpy as jnp
from jax import lax
import numpy as np

D_MODEL = 1024
BATCH = 1
SEQ = 256
DEPTH = 2

MEM_LEN = 256
BLOCK_Q = 128
H_A = 8
DH_A = 64
DC_A = 128
H_IDX = 8
DH_IDX = 64
TOPK_MAX = 256
H_SB = 8
DH_SB = 64
C_CONV = 512
CONV_W = 3
W_A = H_A * DH_A
W_SB = H_SB * DH_SB
W_BRANCH = 512
N_BRANCH = 3
H_X = 4
DH_X = 128
D_FF = 2816
N_BUCKETS = 32
MAX_DISTANCE = 128
DN_ALPHA = (2 * DEPTH) ** 0.25
DN_BETA = (8 * DEPTH) ** -0.25
LN_EPS = 1e-5
N_LN = 4
SPLITS = (W_A, DC_A, H_IDX * DH_IDX, DH_IDX, H_IDX, W_SB, W_SB, W_SB,
          C_CONV, C_CONV, C_CONV, D_MODEL, D_MODEL, D_MODEL)
P_TOTAL = sum(SPLITS)


def layer_norm(x, g, b):
    xf = x.astype(jnp.float32)
    mu = jnp.mean(xf, axis=-1, keepdims=True)
    var = jnp.mean(jnp.square(xf - mu), axis=-1, keepdims=True)
    y = (xf - mu) * lax.rsqrt(var + LN_EPS) * g.astype(jnp.float32) + b.astype(jnp.float32)
    return y.astype(x.dtype)

def rms_norm(x, g):
    xf = x.astype(jnp.float32)
    y = xf * lax.rsqrt(jnp.mean(jnp.square(xf), axis=-1, keepdims=True) + LN_EPS) * g.astype(jnp.float32)
    return y.astype(x.dtype)

def swiglu_ffn(x, w_in, w_out):
    a, b = jnp.split(x @ w_in, 2, axis=-1)
    return (jax.nn.silu(a) * b) @ w_out

def t5_bucket(n):
    max_exact = N_BUCKETS // 2
    n = jnp.maximum(n, 0)
    nf = jnp.maximum(n, 1).astype(jnp.float32)
    large = max_exact + (jnp.log(nf / max_exact) / math.log(MAX_DISTANCE / max_exact)
                         * (N_BUCKETS - max_exact)).astype(jnp.int32)
    large = jnp.minimum(large, N_BUCKETS - 1)
    return jnp.where(n < max_exact, n, large)

def dsa_branch(q, c_kv, iq, ik, iw, w_uk, w_uv, rel_bias):
    bsz, seq = q.shape[0], q.shape[1]
    k_top = min(TOPK_MAX, seq // 4)
    nblk = seq // BLOCK_Q
    q_lat = jnp.einsum('bshd,hdc->bshc', q, w_uk) * (DH_A ** -0.5)
    idx_scale = (H_IDX ** -0.5) * (DH_IDX ** -0.5)

    def to_blocks(a):
        return jnp.swapaxes(a.reshape((bsz, nblk, BLOCK_Q) + a.shape[2:]), 0, 1)

    starts = jnp.arange(nblk, dtype=jnp.int32) * BLOCK_Q
    key_pos = jnp.arange(seq, dtype=jnp.int32)

    def block(args):
        ql, iqb, iwb, start = args
        t = start + jnp.arange(BLOCK_Q, dtype=jnp.int32)
        causal = key_pos[None, :] <= t[:, None]
        dots = jnp.einsum('bqhd,bsd->bhqs', iqb, ik).astype(jnp.float32)
        score = jnp.einsum('bqh,bhqs->bqs', iwb.astype(jnp.float32) * idx_scale, jax.nn.relu(dots))
        score = jnp.where(causal[None], score, -jnp.inf)
        _, idx = lax.top_k(score, k_top)
        valid = idx <= t[None, :, None]
        kv_sel = jax.vmap(lambda c, i: c[i])(c_kv, idx)
        logits = jnp.einsum('bqhc,bqkc->bhqk', ql, kv_sel).astype(jnp.float32)
        bias = rel_bias[t5_bucket(t[None, :, None] - idx)]
        logits = logits + jnp.transpose(bias, (0, 3, 1, 2)).astype(jnp.float32)
        logits = jnp.where(valid[:, None], logits, -1e30)
        p = jax.nn.softmax(logits, axis=-1).astype(kv_sel.dtype)
        return jnp.einsum('bhqk,bqkc->bqhc', p, kv_sel)

    o_lat = lax.map(block, (to_blocks(q_lat), to_blocks(iq), to_blocks(iw), starts))
    o_lat = jnp.swapaxes(o_lat, 0, 1).reshape(bsz, seq, H_A, DC_A)
    o = jnp.einsum('bshc,hcd->bshd', o_lat, w_uv)
    return o.reshape(bsz, seq, W_A)

def stick_breaking_branch(q, k, v):
    bsz, seq = q.shape[0], q.shape[1]
    scale = DH_SB ** -0.5
    outs = []
    for i in range(seq // BLOCK_Q):
        q0 = i * BLOCK_Q
        end = q0 + BLOCK_Q
        z = jnp.einsum('bqhd,bshd->bhqs', q[:, q0:end], k[:, :end]).astype(jnp.float32) * scale
        t = q0 + jnp.arange(BLOCK_Q)
        s = jnp.arange(end)
        strict = (s[None, :] < t[:, None])[None, None]
        log_not = jnp.where(strict, jax.nn.log_sigmoid(-z), 0.0)
        later = lax.cumsum(log_not, axis=3, reverse=True) - log_not
        a = jnp.where(strict, jnp.exp(jax.nn.log_sigmoid(z) + later), 0.0)
        outs.append(jnp.einsum('bhqs,bshd->bqhd', a.astype(v.dtype), v[:, :end]))
    return jnp.concatenate(outs, axis=1).reshape(bsz, seq, W_SB)

def short_conv_branch(b_gate_in, c_gate_in, h, conv_w):
    z = c_gate_in * h
    y = lax.conv_general_dilated(z, conv_w[:, None, :].astype(z.dtype), window_strides=(1,),
                                 padding=((CONV_W - 1, 0),),
                                 dimension_numbers=('NWC', 'WIO', 'NWC'),
                                 feature_group_count=C_CONV)
    return b_gate_in * y

def mixer_sublayer(x, w_in, b_gate, kv_g, w_uk, w_uv, conv_w, w_branch, w_out, rel_bias):
    bsz, seq = x.shape[0], x.shape[1]
    offsets = [int(o) for o in np.cumsum(SPLITS)[:-1]]
    (qa, ckv, iq, ik, iw, qs, ks, vs, cb, cc, ch, ga, gb, gc) = jnp.split(x @ w_in, offsets, axis=-1)
    ckv = rms_norm(ckv, kv_g)
    y_a = dsa_branch(qa.reshape(bsz, seq, H_A, DH_A), ckv,
                     iq.reshape(bsz, seq, H_IDX, DH_IDX), ik, iw, w_uk, w_uv, rel_bias)
    hs = (bsz, seq, H_SB, DH_SB)
    y_b = stick_breaking_branch(qs.reshape(hs), ks.reshape(hs), vs.reshape(hs))
    y_c = short_conv_branch(cb, cc, ch, conv_w)
    merged = (jax.nn.sigmoid(ga + b_gate[0]) * (y_a @ w_branch[0])
              + jax.nn.sigmoid(gb + b_gate[1]) * (y_b @ w_branch[1])
              + jax.nn.sigmoid(gc + b_gate[2]) * (y_c @ w_branch[2]))
    return merged @ w_out

def memory_cross_attention(x, mem, wq, wkv, wo):
    bsz, seq = x.shape[0], x.shape[1]
    q = (x @ wq).reshape(bsz, seq, H_X, DH_X)
    k, v = jnp.split(mem @ wkv, 2, axis=-1)
    k = k.reshape(bsz, mem.shape[1], H_X, DH_X)
    v = v.reshape(bsz, mem.shape[1], H_X, DH_X)
    logits = jnp.einsum('bqhd,bmhd->bhqm', q, k).astype(jnp.float32) * (DH_X ** -0.5)
    p = jax.nn.softmax(logits, axis=-1).astype(v.dtype)
    o = jnp.einsum('bhqm,bmhd->bqhd', p, v).reshape(bsz, seq, H_X * DH_X)
    return o @ wo

def first_inputs(seed: int = 0) -> dict:
    key = jax.random.key(seed)
    ks = jax.random.split(key, 20)
    n = jax.random.normal
    f32 = jnp.float32
    return {
        "x": n(ks[0], (BATCH, SEQ, D_MODEL), f32),
        "mem": n(ks[1], (BATCH, MEM_LEN, D_MODEL), f32),
        "ln_g": 1.0 + 0.01 * n(ks[2], (DEPTH, N_LN, D_MODEL), f32),
        "ln_b": 0.01 * n(ks[3], (DEPTH, N_LN, D_MODEL), f32),
        "ffn_w_in": n(ks[4], (DEPTH, 2, D_MODEL, 2 * D_FF), f32) * D_MODEL ** -0.5,
        "ffn_w_out": n(ks[5], (DEPTH, 2, D_FF, D_MODEL), f32) * (D_FF ** -0.5 * DN_BETA),
        "w_mix_in": n(ks[6], (DEPTH, D_MODEL, P_TOTAL), f32) * D_MODEL ** -0.5,
        "b_gate": 0.01 * n(ks[7], (DEPTH, N_BRANCH, D_MODEL), f32),
        "kv_norm_g": 1.0 + 0.01 * n(ks[8], (DEPTH, DC_A), f32),
        "w_uk": n(ks[9], (DEPTH, H_A, DH_A, DC_A), f32) * DH_A ** -0.5,
        "w_uv": n(ks[10], (DEPTH, H_A, DC_A, DH_A), f32) * DC_A ** -0.5,
        "conv_w": n(ks[11], (DEPTH, CONV_W, C_CONV), f32) * CONV_W ** -0.5,
        "w_branch": n(ks[12], (DEPTH, N_BRANCH, W_BRANCH, D_MODEL), f32) * W_BRANCH ** -0.5,
        "w_mix_out": n(ks[13], (DEPTH, D_MODEL, D_MODEL), f32) * (D_MODEL ** -0.5 * DN_BETA),
        "xa_wq": n(ks[14], (DEPTH, D_MODEL, H_X * DH_X), f32) * D_MODEL ** -0.5,
        "xa_wkv": n(ks[15], (DEPTH, D_MODEL, 2 * H_X * DH_X), f32) * D_MODEL ** -0.5,
        "xa_wo": n(ks[16], (DEPTH, H_X * DH_X, D_MODEL), f32) * ((H_X * DH_X) ** -0.5 * DN_BETA),
        "rel_bias": 0.1 * n(ks[17], (N_BUCKETS, H_A), f32),
    }

def first_block(x, mem, ln_g, ln_b, ffn_w_in, ffn_w_out, w_mix_in, b_gate, kv_norm_g, w_uk, w_uv,
              conv_w, w_branch, w_mix_out, xa_wq, xa_wkv, xa_wo, rel_bias):
    for l in range(DEPTH):
        x = layer_norm(DN_ALPHA * x + 0.5 * swiglu_ffn(x, ffn_w_in[l, 0], ffn_w_out[l, 0]),
                       ln_g[l, 0], ln_b[l, 0])
        x = layer_norm(DN_ALPHA * x + mixer_sublayer(x, w_mix_in[l], b_gate[l], kv_norm_g[l], w_uk[l],
                                                     w_uv[l], conv_w[l], w_branch[l], w_mix_out[l],
                                                     rel_bias),
                       ln_g[l, 1], ln_b[l, 1])
        x = layer_norm(DN_ALPHA * x + memory_cross_attention(x, mem, xa_wq[l], xa_wkv[l], xa_wo[l]),
                       ln_g[l, 2], ln_b[l, 2])
        x = layer_norm(DN_ALPHA * x + 0.5 * swiglu_ffn(x, ffn_w_in[l, 1], ffn_w_out[l, 1]),
                       ln_g[l, 3], ln_b[l, 3])
    return x


GRID_W = 64
CTX_LEN = 256
N_EVEN = (DEPTH + 1) // 2
N_ODD = DEPTH // 2
MIX_WIDTH = D_MODEL
DA_HEADS = 4
DA_DK = 64
DA_DV = 2 * DA_DK
MLA_HEADS = 4
MLA_NOPE = 128
MLA_ROPE = 64
MLA_V = 128
MLA_Q_LORA = 256
MLA_KV_LORA = 128
EV_IN = 3 * DA_HEADS * 2 * DA_DK + MLA_Q_LORA + MLA_KV_LORA + MLA_ROPE
NA_HEADS = 16
NA_DH = 64
NA_KH = 8
NA_KW = 16
D_FF_2 = -(-8 * D_MODEL // (3 * 256)) * 256
ROPE_THETA = 10000.0
Q_BLOCK = 128
EPS = 1e-6
NEG_INF = -1e30


def rms_norm_2(x, g):
    xf = x.astype(jnp.float32)
    y = xf * lax.rsqrt(jnp.mean(xf * xf, axis=-1, keepdims=True) + EPS)
    return (y * g.astype(jnp.float32)).astype(x.dtype)

def softmax_f32(s):
    return jax.nn.softmax(s.astype(jnp.float32), axis=-1)

def adaln(cond, mod_w, mod_b):
    return jnp.split(jax.nn.silu(cond) @ mod_w + mod_b, 6, axis=-1)

def modulate(h, shift, scale):
    return h * (1 + scale) + shift

def swiglu(h, w_in, w_out):
    g, u = jnp.split(h @ w_in, 2, axis=-1)
    return (jax.nn.silu(g) * u) @ w_out

def axial_rope_tables(S, dim):
    t = jnp.arange(S)
    row = (t // GRID_W).astype(jnp.float32)
    col = (t % GRID_W).astype(jnp.float32)
    half = dim // 2
    inv = ROPE_THETA ** (-jnp.arange(0, half, 2, dtype=jnp.float32) / half)
    ar = row[:, None] * inv
    ac = col[:, None] * inv
    return (jnp.cos(ar), jnp.sin(ar), jnp.cos(ac), jnp.sin(ac))

def _rotate(x, cos, sin):
    x1, x2 = jnp.split(x, 2, axis=-1)
    return jnp.concatenate([x1 * cos - x2 * sin, x1 * sin + x2 * cos], axis=-1)

def apply_axial_rope(x, tables):
    cr, sr, cc, sc = tables
    xr, xc = jnp.split(x, 2, axis=-1)
    return jnp.concatenate([_rotate(xr, cr, sr), _rotate(xc, cc, sc)], axis=-1).astype(x.dtype)

def sweep_query_blocks(fn, *qs):
    S = qs[0].shape[-2]
    nb = S // Q_BLOCK
    blocks = tuple(jnp.moveaxis(q.reshape(q.shape[:-2] + (nb, Q_BLOCK, q.shape[-1])), -3, 0) for q in qs)
    out = lax.map(lambda a: fn(*a), blocks)
    out = jnp.moveaxis(out, 0, -3)
    return out.reshape(out.shape[:-3] + (S, out.shape[-1]))

def merge_heads(*outs):
    return jnp.concatenate([o.transpose(0, 2, 1, 3).reshape(o.shape[0], o.shape[2], -1) for o in outs], axis=-1)

def even_project(h, w_in, da_q_g, da_k_g, mla_q_a_g, mla_w_uq, mla_kv_a_g, mla_w_ukv, mla_q_g, mla_k_g, mla_kr_g):
    B, T, _ = h.shape
    n_dq = DA_HEADS * 2 * DA_DK
    idx = [n_dq, 2 * n_dq, 3 * n_dq, 3 * n_dq + MLA_Q_LORA, 3 * n_dq + MLA_Q_LORA + MLA_KV_LORA]
    dq, dk, dv, cq, ckv, kr = jnp.split(h @ w_in, idx, axis=-1)
    dq = rms_norm_2(dq.reshape(B, T, DA_HEADS, 2, DA_DK), da_q_g).transpose(0, 2, 3, 1, 4)
    dk = rms_norm_2(dk.reshape(B, T, DA_HEADS, 2, DA_DK), da_k_g).transpose(0, 2, 3, 1, 4)
    dv = dv.reshape(B, T, DA_HEADS, DA_DV).transpose(0, 2, 1, 3)
    q = (rms_norm_2(cq, mla_q_a_g) @ mla_w_uq).reshape(B, T, MLA_HEADS, MLA_NOPE + MLA_ROPE)
    q = rms_norm_2(q, mla_q_g).transpose(0, 2, 1, 3)
    qn, qr = q[..., :MLA_NOPE], q[..., MLA_NOPE:]
    kv = (rms_norm_2(ckv, mla_kv_a_g) @ mla_w_ukv).reshape(B, T, MLA_HEADS, MLA_NOPE + MLA_V)
    kn = rms_norm_2(kv[..., :MLA_NOPE], mla_k_g).transpose(0, 2, 1, 3)
    mv = kv[..., MLA_NOPE:].transpose(0, 2, 1, 3)
    kr = rms_norm_2(kr, mla_kr_g)
    return dq, dk, dv, qn, qr, kn, kr, mv

def diff_attend(q, k, v, lam, lam_init, out_g):
    s = jnp.einsum('bhiqd,bhikd->bhiqk', q, k) * (DA_DK ** -0.5)
    p = softmax_f32(s)
    a = p[:, :, 0] - lam * p[:, :, 1]
    o = jnp.einsum('bhqk,bhkd->bhqd', a.astype(v.dtype), v)
    return rms_norm_2(o, out_g) * (1.0 - lam_init)

def mla_attend(qn, qr, kn, kr, v):
    s = (jnp.einsum('bhqd,bhkd->bhqk', qn, kn) + jnp.einsum('bhqd,bkd->bhqk', qr, kr)) * ((MLA_NOPE + MLA_ROPE) ** -0.5)
    p = softmax_f32(s)
    return jnp.einsum('bhqk,bhkd->bhqd', p.astype(v.dtype), v)

def even_mixer(hx, hc, need_ctx, w_in, da_q_g, da_k_g, lam, lam_init, da_out_g,
               mla_q_a_g, mla_w_uq, mla_kv_a_g, mla_w_ukv, mla_q_g, mla_k_g, mla_kr_g):
    proj = lambda h: even_project(h, w_in, da_q_g, da_k_g, mla_q_a_g, mla_w_uq, mla_kv_a_g, mla_w_ukv,
                                  mla_q_g, mla_k_g, mla_kr_g)
    dq_x, dk_x, dv_x, qn_x, qr_x, kn_x, kr_x, mv_x = proj(hx)
    dq_c, dk_c, dv_c, qn_c, qr_c, kn_c, kr_c, mv_c = proj(hc)
    S = hx.shape[1]
    tab_da = axial_rope_tables(S, DA_DK)
    tab_mla = axial_rope_tables(S, MLA_ROPE)
    dq_x = apply_axial_rope(dq_x, tab_da)
    dk_x = apply_axial_rope(dk_x, tab_da)
    qr_x = apply_axial_rope(qr_x, tab_mla)
    kr_x = apply_axial_rope(kr_x, tab_mla)
    dk_all = jnp.concatenate([dk_c, dk_x], axis=-2)
    dv_all = jnp.concatenate([dv_c, dv_x], axis=-2)
    kn_all = jnp.concatenate([kn_c, kn_x], axis=-2)
    kr_all = jnp.concatenate([kr_c, kr_x], axis=-2)
    mv_all = jnp.concatenate([mv_c, mv_x], axis=-2)
    da_x = sweep_query_blocks(lambda q: diff_attend(q, dk_all, dv_all, lam, lam_init, da_out_g), dq_x)
    mla_x = sweep_query_blocks(lambda a, b: mla_attend(a, b, kn_all, kr_all, mv_all), qn_x, qr_x)
    y_x = merge_heads(da_x, mla_x)
    y_c = None
    if need_ctx:
        da_c = diff_attend(dq_c, dk_c, dv_c, lam, lam_init, da_out_g)
        mla_c = mla_attend(qn_c, qr_c, kn_c, kr_c, mv_c)
        y_c = merge_heads(da_c, mla_c)
    return y_x, y_c

def odd_project(h, w_in, q_g, k_g):
    B, T, _ = h.shape
    q, k, v = jnp.split((h @ w_in).reshape(B, T, 3 * NA_HEADS, NA_DH), 3, axis=2)
    q = rms_norm_2(q, q_g).transpose(0, 2, 1, 3)
    k = rms_norm_2(k, k_g).transpose(0, 2, 1, 3)
    return q, k, v.transpose(0, 2, 1, 3)

def dense_attend(q, k, v):
    p = softmax_f32(jnp.einsum('bhqd,bhkd->bhqk', q, k) * (NA_DH ** -0.5))
    return jnp.einsum('bhqk,bhkd->bhqd', p.astype(v.dtype), v)

def na_latent(q, k, v, kc, vc, rpb):
    B, H, S, d = q.shape
    rows = S // GRID_W
    kh = min(NA_KH, rows)
    kg = k.reshape(B, H, rows, GRID_W, d)
    vg = v.reshape(B, H, rows, GRID_W, d)
    qg = q.reshape(B, H, rows, GRID_W, d)
    cols = jnp.arange(GRID_W)
    col_start = jnp.clip(cols - NA_KW // 2, 0, GRID_W - NA_KW)
    col_valid = (cols[None, :] >= col_start[:, None]) & (cols[None, :] < col_start[:, None] + NA_KW)
    dc_idx = jnp.clip(cols[None, :] - cols[:, None], -(NA_KW - 1), NA_KW - 1) + NA_KW - 1
    rpb_c = rpb[:, :, dc_idx]
    scale = NA_DH ** -0.5

    def row_step(args):
        r, q_row = args
        rs = jnp.clip(r - kh // 2, 0, rows - kh)
        kb = lax.dynamic_slice_in_dim(kg, rs, kh, axis=2)
        vb = lax.dynamic_slice_in_dim(vg, rs, kh, axis=2)
        dr_idx = rs + jnp.arange(kh) - r + NA_KH - 1
        bias = jnp.take(rpb_c, dr_idx, axis=1).transpose(0, 2, 1, 3)
        s_loc = jnp.einsum('bhqd,bhiwd->bhqiw', q_row, kb).astype(jnp.float32) * scale + bias
        s_loc = jnp.where(col_valid[:, None, :], s_loc, NEG_INF).reshape(B, H, GRID_W, kh * GRID_W)
        s_ctx = jnp.einsum('bhqd,bhkd->bhqk', q_row, kc).astype(jnp.float32) * scale
        p = softmax_f32(jnp.concatenate([s_loc, s_ctx], axis=-1))
        p_loc = p[..., :kh * GRID_W].reshape(B, H, GRID_W, kh, GRID_W).astype(v.dtype)
        p_ctx = p[..., kh * GRID_W:].astype(v.dtype)
        return jnp.einsum('bhqiw,bhiwd->bhqd', p_loc, vb) + jnp.einsum('bhqk,bhkd->bhqd', p_ctx, vc)

    out = lax.map(row_step, (jnp.arange(rows), jnp.moveaxis(qg, 2, 0)))
    return jnp.moveaxis(out, 0, 2).reshape(B, H, S, d)

def odd_mixer(hx, hc, need_ctx, w_in, q_g, k_g, rpb):
    q_x, k_x, v_x = odd_project(hx, w_in, q_g, k_g)
    q_c, k_c, v_c = odd_project(hc, w_in, q_g, k_g)
    y_x = merge_heads(na_latent(q_x, k_x, v_x, k_c, v_c, rpb))
    y_c = merge_heads(dense_attend(q_c, k_c, v_c)) if need_ctx else None
    return y_x, y_c

def second_inputs(seed: int = 0) -> dict:
    key = jax.random.key(seed)
    ks = iter(jax.random.split(key, 40))
    nrm = lambda shape, s: jax.random.normal(next(ks), shape, jnp.float32) * s
    gain = lambda shape: 1.0 + 0.1 * jax.random.normal(next(ks), shape, jnp.float32)
    D = D_MODEL
    return {
        "x": nrm((BATCH, SEQ, D), 1.0),
        "c": nrm((BATCH, D), 1.0),
        "ctx": nrm((BATCH, CTX_LEN, D), 1.0),
        "c_ctx": nrm((D,), 1.0),
        "mod_w": nrm((DEPTH, D, 6 * D), 0.5 * D ** -0.5),
        "mod_b": nrm((DEPTH, 6 * D), 0.02),
        "norm_mix_g": gain((DEPTH, D)),
        "norm_ffn_g": gain((DEPTH, D)),
        "w_out": nrm((DEPTH, MIX_WIDTH, D), MIX_WIDTH ** -0.5),
        "ffn_w_in": nrm((DEPTH, D, 2 * D_FF_2), D ** -0.5),
        "ffn_w_out": nrm((DEPTH, D_FF_2, D), D_FF_2 ** -0.5),
        "ev_w_in": nrm((N_EVEN, D, EV_IN), D ** -0.5),
        "da_q_g": gain((N_EVEN, DA_DK)),
        "da_k_g": gain((N_EVEN, DA_DK)),
        "da_lq1": nrm((N_EVEN, DA_DK), 0.1),
        "da_lk1": nrm((N_EVEN, DA_DK), 0.1),
        "da_lq2": nrm((N_EVEN, DA_DK), 0.1),
        "da_lk2": nrm((N_EVEN, DA_DK), 0.1),
        "da_out_g": gain((N_EVEN, DA_DV)),
        "mla_q_a_g": gain((N_EVEN, MLA_Q_LORA)),
        "mla_w_uq": nrm((N_EVEN, MLA_Q_LORA, MLA_HEADS * (MLA_NOPE + MLA_ROPE)), MLA_Q_LORA ** -0.5),
        "mla_kv_a_g": gain((N_EVEN, MLA_KV_LORA)),
        "mla_w_ukv": nrm((N_EVEN, MLA_KV_LORA, MLA_HEADS * (MLA_NOPE + MLA_V)), MLA_KV_LORA ** -0.5),
        "mla_q_g": gain((N_EVEN, MLA_NOPE + MLA_ROPE)),
        "mla_k_g": gain((N_EVEN, MLA_NOPE)),
        "mla_kr_g": gain((N_EVEN, MLA_ROPE)),
        "od_w_in": nrm((N_ODD, D, 3 * NA_HEADS * NA_DH), D ** -0.5),
        "na_q_g": gain((N_ODD, NA_DH)),
        "na_k_g": gain((N_ODD, NA_DH)),
        "na_rpb": nrm((N_ODD, NA_HEADS, 2 * NA_KH - 1, 2 * NA_KW - 1), 0.5),
    }

def second_block(x, c, ctx, c_ctx, mod_w, mod_b, norm_mix_g, norm_ffn_g, w_out, ffn_w_in, ffn_w_out,
              ev_w_in, da_q_g, da_k_g, da_lq1, da_lk1, da_lq2, da_lk2, da_out_g,
              mla_q_a_g, mla_w_uq, mla_kv_a_g, mla_w_ukv, mla_q_g, mla_k_g, mla_kr_g,
              od_w_in, na_q_g, na_k_g, na_rpb):
    for l in range(DEPTH):
        need_ctx = l < DEPTH - 1
        sh_a, sc_a, g_a, sh_f, sc_f, g_f = [m[:, None, :] for m in adaln(c, mod_w[l], mod_b[l])]
        csh_a, csc_a, cg_a, csh_f, csc_f, cg_f = adaln(c_ctx, mod_w[l], mod_b[l])
        hx = modulate(rms_norm_2(x, norm_mix_g[l]), sh_a, sc_a)
        hc = modulate(rms_norm_2(ctx, norm_mix_g[l]), csh_a, csc_a)
        e = l // 2
        if l % 2 == 0:
            lam_init = 0.8 - 0.6 * math.exp(-0.3 * l)
            lam = (jnp.exp(jnp.sum(da_lq1[e] * da_lk1[e]).astype(jnp.float32))
                   - jnp.exp(jnp.sum(da_lq2[e] * da_lk2[e]).astype(jnp.float32)) + lam_init)
            y_x, y_c = even_mixer(hx, hc, need_ctx, ev_w_in[e], da_q_g[e], da_k_g[e], lam, lam_init, da_out_g[e],
                                  mla_q_a_g[e], mla_w_uq[e], mla_kv_a_g[e], mla_w_ukv[e],
                                  mla_q_g[e], mla_k_g[e], mla_kr_g[e])
        else:
            y_x, y_c = odd_mixer(hx, hc, need_ctx, od_w_in[e], na_q_g[e], na_k_g[e], na_rpb[e])
        x = x + g_a * (y_x @ w_out[l])
        x = x + g_f * swiglu(modulate(rms_norm_2(x, norm_ffn_g[l]), sh_f, sc_f), ffn_w_in[l], ffn_w_out[l])
        if need_ctx:
            ctx = ctx + cg_a * (y_c @ w_out[l])
            ctx = ctx + cg_f * swiglu(modulate(rms_norm_2(ctx, norm_ffn_g[l]), csh_f, csc_f), ffn_w_in[l], ffn_w_out[l])
    return x


def setup_inputs(seed=0):
    out = dict(first_inputs(seed))
    for name, value in second_inputs(seed + 1).items():
        if name != "x":
            out[name + "_2"] = value
    return out


def reference(
    x, mem, ln_g, ln_b, ffn_w_in, ffn_w_out, w_mix_in, b_gate, kv_norm_g, w_uk, w_uv, conv_w,
    w_branch, w_mix_out, xa_wq, xa_wkv, xa_wo, rel_bias, c_2, ctx_2, c_ctx_2, mod_w_2, mod_b_2,
    norm_mix_g_2, norm_ffn_g_2, w_out_2, ffn_w_in_2, ffn_w_out_2, ev_w_in_2, da_q_g_2, da_k_g_2,
    da_lq1_2, da_lk1_2, da_lq2_2, da_lk2_2, da_out_g_2, mla_q_a_g_2, mla_w_uq_2, mla_kv_a_g_2,
    mla_w_ukv_2, mla_q_g_2, mla_k_g_2, mla_kr_g_2, od_w_in_2, na_q_g_2, na_k_g_2, na_rpb_2,
):
    x = first_block(
        x, mem, ln_g, ln_b, ffn_w_in, ffn_w_out, w_mix_in, b_gate, kv_norm_g, w_uk, w_uv,
        conv_w, w_branch, w_mix_out, xa_wq, xa_wkv, xa_wo, rel_bias,
    )
    return second_block(
        x, c_2, ctx_2, c_ctx_2, mod_w_2, mod_b_2, norm_mix_g_2, norm_ffn_g_2, w_out_2,
        ffn_w_in_2, ffn_w_out_2, ev_w_in_2, da_q_g_2, da_k_g_2, da_lq1_2, da_lk1_2, da_lq2_2,
        da_lk2_2, da_out_g_2, mla_q_a_g_2, mla_w_uq_2, mla_kv_a_g_2, mla_w_ukv_2, mla_q_g_2,
        mla_k_g_2, mla_kr_g_2, od_w_in_2, na_q_g_2, na_k_g_2, na_rpb_2,
    )


_drawn_inputs = setup_inputs


def setup_inputs(seed=0):
    import zlib

    import numpy as np

    out = dict(_drawn_inputs(seed))
    spreads = {}
    factors = {'b_gate': 8.0,
     'kv_norm_g': 8.0,
     'rel_bias': 8.0,
     'norm_mix_g_2': 3.995,
     'da_q_g_2': 6.94,
     'da_k_g_2': 8.0,
     'da_lq1_2': 64.0,
     'da_lk1_2': 64.0,
     'da_lq2_2': 8.0,
     'da_lk2_2': 8.0,
     'da_out_g_2': 3.253,
     'mla_q_a_g_2': 8.0,
     'mla_kv_a_g_2': 8.0,
     'mla_q_g_2': 8.0,
     'mla_k_g_2': 8.0,
     'mla_kr_g_2': 8.0,
     'na_q_g_2': 8.0,
     'na_k_g_2': 8.0,
     'na_rpb_2': 6.785}
    for name, (base, spread) in spreads.items():
        noise = np.random.default_rng([zlib.crc32(name.encode()), seed]).standard_normal(out[name].shape)
        drawn = base * np.exp(spread * noise) if base else spread * noise
        out[name] = __import__('jax').numpy.asarray(drawn.astype(out[name].dtype))
    for name, factor in factors.items():
        out[name] = (out[name] * factor).astype(out[name].dtype)
    return out
```

```python
from contextlib import ExitStack
import math

import numpy as np

import concourse.bass as bass
from concourse import mybir

F32 = mybir.dt.float32
F32R = mybir.dt.float32r
ALU = mybir.AluOpType
ACT = mybir.ActivationFunctionType
AX = mybir.AxisListType.X
P = 128
HP = [0, 2, 4, 6, 1, 3, 5, 7]
D = 1024
F = 2816
BIG = 1e30
ALPHA = 4 ** 0.25

NRAW, NSPL, AHEAD = 3, 3, 2
UW = 2048

C_ID, C_TRI, C_ONE, C_NEG, C_SM, C_SN, C_HALF, C_S0, C_S1, C_NA, C_END = (
    0, 128, 256, 384, 640, 768, 896, 928, 1056, 1184, 1440)


def constants():
    c = np.zeros((P, C_END), np.float32)
    p = np.arange(P)[:, None]
    c[:, C_ID:C_ID + P] = np.eye(P)
    c[:, C_TRI:C_TRI + P] = p >= np.arange(P)[None]
    c[:, C_ONE:C_ONE + P] = 1
    c[:, C_NEG:C_NEG + 256] = np.where(np.arange(256)[None] > 128 + p, -3e38, 0)
    c[:, C_SM:C_SM + P] = p < np.arange(P)[None]
    c[:, C_SN:C_SN + P] = np.where(p < np.arange(P)[None], 0, -BIG)
    c[:, C_HALF:C_HALF + 32] = -0.5
    c[0, C_S0:C_S0 + P] = 1
    c[64, C_S1:C_S1 + P] = 1
    col = p % 64
    start = np.clip(col - 8, 0, 48)
    w = np.arange(256)[None] % 64
    c[:, C_NA:C_NA + 256] = np.where((w >= start) & (w < start + 16), 0, -BIG)
    return c


def bucket_table():
    n = np.maximum(255 - np.arange(512), 0)
    nf = np.maximum(n, 1).astype(np.float32)
    large = 16 + (np.log(nf / np.float32(16)) / np.float32(math.log(8.0)) * np.float32(16)).astype(np.int32)
    b = np.where(n < 16, n, np.minimum(large, 31))
    return (b[None] == np.arange(32)[:, None]).astype(np.float32)


def rope_table():
    t = np.arange(256)
    inv = (10000.0 ** (-np.arange(0, 32, 2, dtype=np.float32) / np.float32(32))).astype(np.float32)
    ar = (t // 64).astype(np.float32)[:, None] * inv
    ac = (t % 64).astype(np.float32)[:, None] * inv
    out = np.zeros((256, 2, 2, 2, 16), np.float32)
    for a, ang in enumerate((ar, ac)):
        out[:, 0, a, :] = np.cos(ang)[:, None]
        out[:, 1, a, 0] = -np.sin(ang)
        out[:, 1, a, 1] = np.sin(ang)
    return out.reshape(2, 128, 128).transpose(1, 0, 2).copy()


class Count:

    def __init__(self, sem):
        self.sem, self.n = sem, 0

    def mark(self, back=0):
        return (self, self.n - back)


class Step:

    def __init__(self, make):
        self.make, self.inc = make, None

    def then_inc(self, count, when=True, by=1):
        if not when:
            return None
        self.inc = (count.sem, by)
        count.n += by
        return count.mark()

    def play(self, e):
        ins = self.make(e)
        if self.inc:
            ins.then_inc(*self.inc)


class Wait:
    inc = True

    def __init__(self, sem, value):
        self.sem, self.value = sem, value

    def play(self, e):
        e.wait_ge(self.sem, self.value)


class Queue:

    def __init__(self):
        self.steps = []

    def step(self, make):
        self.steps.append(Step(make))
        return self.steps[-1]

    def wait_ge(self, *marks):
        for m in marks:
            if isinstance(m, (list, tuple)) and not (m and isinstance(m[0], Count)):
                self.wait_ge(*m)
            elif m is not None and m[1] > 0:
                self.steps.append(Wait(m[0].sem, m[1]))

    def dma_start(self, out, in_):
        return self.step(lambda e: e.dma_start(out, in_))

    def tensor_tensor(self, out, a, b, op):
        return self.step(lambda e: e.tensor_tensor(out, a, b, op))

    def play(self, e):
        for s in self.steps:
            s.play(e)


class VectorQueue(Queue):
    def tensor_scalar(self, out, a, s1, s2, op0, op1=None):
        if op1 is None:
            return self.step(lambda e: e.tensor_scalar(out, a, s1, None, op0))
        return self.step(lambda e: e.tensor_scalar(out, a, s1, s2, op0, op1))

    def scalar_tensor_tensor(self, out, a, s, b, op0, op1):
        return self.step(lambda e: e.scalar_tensor_tensor(out, a, s, b, op0, op1))

    def tensor_copy(self, out, a):
        return self.step(lambda e: e.tensor_copy(out, a))

    def tensor_reduce(self, out, a, axis, op):
        return self.step(lambda e: e.tensor_reduce(out, a, axis, op))

    def reciprocal(self, out, a):
        return self.step(lambda e: e.reciprocal(out, a))

    def bn_stats(self, out, a):
        return self.step(lambda e: e.bn_stats(out, a))

    def bn_aggr(self, out, a):
        return self.step(lambda e: e.bn_aggr(out, a))

    def max(self, out, a):
        return self.step(lambda e: e.max(out, a))

    def match_replace(self, out, eight, a, v):
        return self.step(lambda e: e.match_replace(out, eight, a, v))

    def memset(self, out, v):
        return self.step(lambda e: e.memset(out, v))

    copy = tensor_copy


class ScalarQueue(Queue):
    def activation(self, out, a, f, **k):
        return self.step(lambda e: e.activation(out, a, f, **k))

    def copy(self, out, a):
        return self.activation(out, a, ACT.Copy)


class TensorQueue(Queue):
    def matmul(self, out, lhs, rhs, **k):
        return self.step(lambda e: e.matmul(out, lhs, rhs, **k))

    def transpose(self, out, a, ident):
        return self.step(lambda e: e.transpose(out, a, ident))


def blocks(w, c0, n, kts=None):
    kts = kts or w.shape[0] // P
    return [(w, k0, min(4, kts - k0), c0, n) for k0 in range(0, kts, 4)]


def same(a, b):
    return a[0].tensor.name == b[0].tensor.name and a[0].offset == b[0].offset and a[1:] == b[1:]


def ffn_blocks(w_in, w_out):
    out = []
    for c in range(0, F, 512):
        n = min(512, F - c)
        out += blocks(w_in, c, n) + blocks(w_in, F + c, n)
    return out + blocks(w_out, 0, 512) + blocks(w_out, 512, 512)


def first_plan(A):
    out = []
    for l in range(2):
        out += ffn_blocks(A["ffn_w_in"][l, 0], A["ffn_w_out"][l, 0])
        for c, n in [(0, 512), (512, 512), (1024, 200), (3272, 512), (3784, 512), (2760, 512), (1224, 512),
                     (1736, 512), (2248, 512)] + [(4296 + i * 512, 512) for i in range(6)]:
            out += blocks(A["w_mix_in"][l], c, n)
        for i in (0, 2, 1):
            for c in (0, 512):
                out += blocks(A["w_branch"][l, i], c, 512)
        for w in ("w_mix_out", "xa_wkv"):
            for c in (0, 512):
                out += blocks(A[w][l], c, 512)
        out += blocks(A["xa_wq"][l], 0, 512)
        for c in (0, 512):
            out += blocks(A["xa_wo"][l], c, 512)
        out += ffn_blocks(A["ffn_w_in"][l, 1], A["ffn_w_out"][l, 1])
    return out


def second_plan(A):
    def mod(l):
        return [b for j in range(12) for b in blocks(A["mod_w_2"][l], j * 512, 512)]

    def w_out(l):
        return blocks(A["w_out_2"][l], 0, 512) + blocks(A["w_out_2"][l], 512, 512)

    def ffn(l):
        return ffn_blocks(A["ffn_w_in_2"][l], A["ffn_w_out_2"][l])

    ev, od, ukv, uq = A["ev_w_in_2"][0], A["od_w_in_2"][0], A["mla_w_ukv_2"][0], A["mla_w_uq_2"][0]
    out = mod(0)
    for s in range(2):
        out += blocks(ev, 1536, 448) + blocks(ev, 512, 512) + blocks(ev, 1024, 512)
        out += blocks(ukv, 0, 512) + blocks(ukv, 512, 512) + blocks(ev, 0, 512)
        out += blocks(uq, 0, 384) + blocks(uq, 384, 384) + w_out(0)
    out += ffn(0) + ffn(0) + mod(1)
    for s in range(2):
        for c in (0, 512):
            out += blocks(od, 1024 + c, 512) + blocks(od, 2048 + c, 512)
    return out + blocks(od, 0, 512) + blocks(od, 512, 512) + w_out(1) + ffn(1)


class Bank:
    def __init__(self, ap):
        self.ap, self.drained, self.held = ap[:, :], None, False


class Core:
    pass


def new_core(nc, A, ctx, plan):
    co = Core()
    co.nc, co.A, co.ctx, co.plan = nc, A, ctx, plan
    sem = lambda n: Count(ctx.enter_context(nc.semaphore(n)))
    co.pe, co.dv, co.ac, co.po, co.sp = TensorQueue(), VectorQueue(), ScalarQueue(), Queue(), Queue()
    co.s_pe, co.s_dv, co.s_ac, co.s_po = sem("s_pe"), sem("s_dv"), sem("s_ac"), sem("s_po")
    co.s_hi, co.s_lo, co.s_use = sem("s_hi"), sem("s_lo"), sem("s_use")
    co.s_out = sem("s_out")
    co.s_raw = [sem(f"s_raw{i}") for i in range(NRAW)]
    co.s_par = [sem(f"s_par{i}") for i in range(12)]
    co.npar = 0
    co.nuse = 0
    co.bg = []
    co.base = 16512
    co.top = 229344
    co.y = nc.alloc_sbuf_tensor_at("y", [P, 2, D], F32, offset=co.top - 8192)
    co.names = 0
    co.raw = [alloc(co, [P, UW]) for _ in range(NRAW)]
    co.whi = [alloc(co, [P, UW], F32R) for _ in range(NSPL)]
    co.wlo = [alloc(co, [P, UW], F32R) for _ in range(NSPL)]
    co.banks = [Bank(ctx.enter_context(nc.psum_tensor(f"bank{i}", [P, 512], F32))) for i in range(8)]
    co.bi = 0
    for u in range(AHEAD):
        stage(co, u)
    return co




def alloc(co, shape, dt=F32):
    n = 4
    for s in shape[1:]:
        n *= s
    n = (n + 31) // 32 * 32
    co.names += 1
    assert co.base + n <= co.top, (co.base, n, co.top)
    t = co.nc.alloc_sbuf_tensor_at(f"m{co.names}", shape, dt, offset=co.base)
    co.base += n
    return t


def counts(co):
    return (pe_mark(co), co.s_dv.mark(), co.s_ac.mark(), co.s_po.mark(),
            tuple(s.mark() for s in co.s_par if s.n))


def pe_mark(co):
    assert not co.pe.steps or co.pe.steps[-1].inc
    return (co.s_pe.mark(), co.s_use.mark())


def next_bank(co, hold=False):
    while co.banks[co.bi].held:
        co.bi = (co.bi + 1) % 8
    b = co.banks[co.bi]
    co.bi = (co.bi + 1) % 8
    b.held = hold
    return b




def load_small(co, out, in_):
    s = co.s_par[co.npar % len(co.s_par)]
    co.npar += 1
    if s.n:
        co.po.wait_ge(s.mark())
    return co.po.dma_start(out, in_).then_inc(s, by=16)


def ident(co, a):
    n = a.shape[0]
    return co.cst[0:n, C_ID:C_ID + n]


def minus_half(co, v):
    return co.cst[:, C_HALF:C_HALF + v.shape[-1]]




def spawn(co, gen):
    if next(gen, StopIteration) is not StopIteration:
        co.bg.append(gen)


def advance(co):
    co.bg = [g for g in co.bg if next(g, StopIteration) is not StopIteration]


def flush(co):
    while co.bg:
        advance(co)




def slot(co, ring, u, nk, n):
    return ring[u % len(ring)][:, 0:nk * n].rearrange("p (k n) -> p k n", k=nk)


def stage(co, u):
    if u >= len(co.plan):
        return
    w, k0, nk, c0, n = co.plan[u]
    raw, hi, lo = (slot(co, r, u, nk, n) for r in (co.raw, co.whi, co.wlo))
    landed = co.s_raw[u % NRAW]
    if u >= NRAW:
        co.sp.wait_ge((co.s_hi, u - NRAW + 1))
        co.sp.wait_ge((co.s_lo, u - NRAW + 1))
    co.sp.dma_start(raw, w[k0 * P:(k0 + nk) * P, c0:c0 + n].rearrange("(k p) n -> p k n", p=P))\
        .then_inc(landed, by=16)

    co.ac.wait_ge(landed.mark())
    if u >= NSPL:
        co.ac.wait_ge((co.s_use, u - NSPL + 1))
    co.ac.activation(hi, raw, ACT.Copy).then_inc(co.s_hi)

    co.dv.wait_ge(landed.mark())
    co.dv.wait_ge((co.s_hi, u + 1))
    if u >= NSPL:
        co.dv.wait_ge((co.s_use, u - NSPL + 1))
    co.dv.tensor_tensor(lo, raw, hi.bitcast(F32), ALU.subtract).then_inc(co.s_lo)


def gemm(co, xt, xdep, w, c0, n, evac, kt0=0, kts=None, tt=2, quiet=False):
    hi, lo = xt
    kts = kts or w.shape[0] // P
    banks = [next_bank(co, hold=True) for _ in range(tt)]
    per = 4
    done = 0
    while done < kts:
        nk = min(per, kts - done)
        u = co.nuse
        co.nuse += 1
        assert same(co.plan[u], (w, done, nk, c0, n)), u
        stage(co, u + AHEAD)
        wh, wl = slot(co, co.whi, u, nk, n), slot(co, co.wlo, u, nk, n)
        co.pe.wait_ge((co.s_hi, u + 1))
        co.pe.wait_ge((co.s_lo, u + 1))
        co.pe.wait_ge(xdep[done // 2:(done + nk + 1) // 2] if isinstance(xdep, list) else xdep)
        for t in range(tt):
            out = banks[t].ap[:, 0:n]
            co.pe.wait_ge(banks[t].drained)
            for k in range(nk):
                kk = kt0 + done + k
                xh = hi[:, kk, t * P:(t + 1) * P]
                xl = lo[:, kk, t * P:(t + 1) * P]
                first = done == 0 and k == 0
                last = done + k == kts - 1
                co.pe.matmul(out, xh, wh[:, k, :], start=first, stop=False, skip_group_check=True)
                co.pe.matmul(out, xh, wl[:, k, :], start=False, stop=False, skip_group_check=True)
                used = co.pe.matmul(out, xl, wh[:, k, :], start=False, stop=last, skip_group_check=True)\
                    .then_inc(co.s_use, t == tt - 1 and k == nk - 1)
        done += nk
        if not quiet:
            advance(co)
    evac(banks, used)
    for b in banks:
        b.held = False


def finish_out(co, out):
    co.sp.wait_ge(co.xready)
    done = co.sp.dma_start(out.rearrange("(t p) d -> p t d", p=P), co.x[:, :, :]).then_inc(co.s_out, by=16)
    co.sp.wait_ge(done)
    co.sp.wait_ge([s.mark() for s in co.s_par if s.n])


def emit(co):
    block = co.ctx.enter_context(co.nc.Block())

    @block.sync
    def _(e):
        co.sp.play(e)

    @block.scalar
    def _(e):
        co.ac.play(e)

    @block.gpsimd
    def _(e):
        co.po.play(e)

    @block.vector
    def _(e):
        co.dv.play(e)

    @block.tensor
    def _(e):
        co.pe.play(e)




def to_t(co, src, kt, dst, dep, free=None):
    hi, lo = dst
    out = []
    for k0 in range(0, kt, 2):
        nk = min(2, kt - k0)
        b = next_bank(co)
        co.pe.wait_ge(dep, b.drained)
        for k in range(nk):
            for t in range(2):
                tok = co.pe.transpose(b.ap[:, k * 256 + t * P:k * 256 + (t + 1) * P], src(t, k0 + k), ident(co, src(t, k0 + k))).then_inc(co.s_pe, k == nk - 1 and t == 1)
        ps = b.ap[:, 0:nk * 256].rearrange("p (k n) -> p k n", k=nk)
        co.ac.wait_ge(tok, free)
        a = co.ac.activation(hi[:, k0:k0 + nk, :], ps, ACT.Copy).then_inc(co.s_ac)
        co.dv.wait_ge(tok, a, free)
        v = co.dv.tensor_tensor(lo[:, k0:k0 + nk, :], ps, hi[:, k0:k0 + nk, :].bitcast(F32), ALU.subtract).then_inc(co.s_dv)
        b.drained = (a, v)
        out.append((a, v))
    return out


def t32(co, src, n, dst, dep, free=None, scale=1.0):
    toks = []
    for k0 in range(0, n, 2):
        nk = min(2, n - k0)
        b = next_bank(co)
        for k in range(nk):
            for t in range(2):
                s = src(k0 + k, t)
                m = s.shape[-1]
                co.pe.wait_ge(dep, b.drained)
                tok = co.pe.transpose(b.ap[0:m, k * 256 + t * P:k * 256 + (t + 1) * P], s, ident(co, s)).then_inc(co.s_pe, k == nk - 1 and t == 1)
        m = dst.shape[0]
        ps = b.ap[0:m, 0:nk * 256].rearrange("p (k n) -> p k n", k=nk)
        co.ac.wait_ge(tok, free)
        a = co.ac.activation(dst[:, k0:k0 + nk, :], ps, ACT.Copy, scale=scale).then_inc(co.s_ac)
        b.drained = a
        toks.append(a)
    return tuple(toks)


def load_ln(co, l, i, *deps):
    A = co.A
    co.po.wait_ge(deps)
    co.lnpar = (load_small(co, co.lg[:, :], A["ln_g"][l, i:i + 1, :].to_broadcast([P, D])),
                  load_small(co, co.lb[:, :], A["ln_b"][l, i:i + 1, :].to_broadcast([P, D])))


def layer_norm(co, y, ydep, eps, nxt):
    st, mv, rs, par = co.st, co.mv, co.rs, co.lnpar
    norm = []
    for t in range(2):
        tok = ydep
        for c in range(2):
            a, o = y[:, t, c * 512:(c + 1) * 512], st[:, t, c, :]
            co.dv.wait_ge(ydep, co.rsfree)
            tok = co.dv.bn_stats(o, a).then_inc(co.s_dv)
        m, sv = mv[:, t, :], st[:, t, :, :].rearrange("p c s -> p (c s)")
        co.dv.wait_ge(tok)
        tok = co.dv.bn_aggr(m, sv).then_inc(co.s_dv)
        co.dv.wait_ge(tok)
        tok = co.dv.tensor_scalar(rs[:, t, 0:1], mv[:, t, 1:2], eps, None, ALU.add).then_inc(co.s_dv)
        co.po.wait_ge(tok)
        norm.append(co.po.tensor_tensor(rs[:, t, 1:2], rs[:, t, 0:1], minus_half(co, rs[:, t, 0:1]), ALU.pow).then_inc(co.s_po))
    yield
    out = []
    for t in range(2):
        co.dv.wait_ge(norm[t])
        tok = co.dv.tensor_scalar(y[:, t, :], y[:, t, :], mv[:, t, 0:1], rs[:, t, 1:2], ALU.subtract, ALU.mult).then_inc(co.s_dv)
        co.dv.wait_ge(tok, par)
        tok = co.dv.tensor_tensor(y[:, t, :], y[:, t, :], co.lg[:, :], ALU.mult).then_inc(co.s_dv)
        co.dv.wait_ge(tok, co.xfree, par)
        tok = co.dv.tensor_tensor(co.x[:, t, :], y[:, t, :], co.lb[:, :], ALU.add).then_inc(co.s_dv)
        out.append(tok)
    if nxt is not None:
        load_ln(co, nxt[0], nxt[1], tok)
    co.rsfree = tok
    co.xready = tuple(out)
    yield
    co.xdep = to_t(co, lambda t, k: co.x[:, t, k * P:(k + 1) * P], 8, (co.xh, co.xl), co.xready,
                          co.xtfree)
    co.xfree = pe_mark(co)


def residual(co, y, scale, got, fe):
    def make(c0, n):
        def evac(banks, tok):
            for t in range(2):
                o = y[:, t, c0:c0 + n]
                co.dv.wait_ge(tok, co.xready, fe)
                r = co.dv.scalar_tensor_tensor(o, co.x[:, t, c0:c0 + n], scale, banks[t].ap[:, 0:n], ALU.mult, ALU.add).then_inc(co.s_dv)
                banks[t].drained = r
                got.append(r)
        return evac
    return make


def ffn(co, w_in, w_out, resid):
    xt, xdep = (co.xh, co.xl), co.xdep
    base = co.base
    uh, ul = alloc(co, [P, 22, 256], F32R), alloc(co, [P, 22, 256], F32R)
    sa = alloc(co, [P, 2, 512])
    ut = [alloc(co, [P, 2, 512]) for _ in range(2)]
    fe = counts(co)
    free = {"sa": fe, 0: fe, 1: fe}
    udep = []
    for j in range(6):
        c, n = j * 512, min(512, F - j * 512)
        hold = {}

        def evac_a(banks, tok):
            hold["sa"] = []
            co.ac.wait_ge(tok, free['sa'])
            for t in range(2):
                a = co.ac.activation(sa[:, t, 0:n], banks[t].ap[:, 0:n], ACT.Silu).then_inc(co.s_ac)
                banks[t].drained = a
                hold["sa"].append(a)

        def evac_b(banks, tok):
            spawn(co, rest(banks, tok, j, n, hold["sa"]))

        def rest(banks, tok, j, n, sat):
            u = ut[j % 2]
            co.dv.wait_ge(tok, free[j % 2])
            for t in range(2):
                co.dv.wait_ge(sat[t])
                v = co.dv.tensor_tensor(u[:, t, 0:n], banks[t].ap[:, 0:n], sa[:, t, 0:n], ALU.mult).then_inc(co.s_dv)
                banks[t].drained = v
            free["sa"] = v
            yield
            got = to_t(co, lambda t, k: u[:, t, k * P:(k + 1) * P], n // P,
                            (uh[:, 4 * j:, :], ul[:, 4 * j:, :]), v, fe)
            free[j % 2] = pe_mark(co)
            udep.extend(got)

        gemm(co, xt, xdep, w_in, c, n, evac_a)
        gemm(co, xt, xdep, w_in, F + c, n, evac_b)
    flush(co)
    co.xtfree = pe_mark(co)
    for c in range(2):
        gemm(co, (uh, ul), udep, w_out, c * 512, 512, resid(c * 512, 512))
    co.base = base


"""The first block's sublayers."""


def setup(co):
    A = co.A
    co.cst = alloc(co, [P, C_END])
    co.x = alloc(co, [P, 2, D])
    co.xh, co.xl = alloc(co, [P, 8, 256], F32R), alloc(co, [P, 8, 256], F32R)
    co.st, co.mv, co.rs = alloc(co, [P, 2, 2, 6]), alloc(co, [P, 2, 2]), alloc(co, [P, 2, 2])
    co.lgbase = co.base
    co.lg, co.lb = alloc(co, [P, D]), alloc(co, [P, D])
    co.xfree = co.rsfree = co.xtfree = None
    cdep = load_small(co, co.cst[:, :], A["consts"][:, :])
    co.xready = load_small(co, co.x[:, :, :], A["x"][0].rearrange("(t p) d -> p t d", p=P))
    load_ln(co, 0, 0)
    co.xdep = to_t(co, lambda t, k: co.x[:, t, k * P:(k + 1) * P], 8, (co.xh, co.xl),
                          (co.xready, cdep))
    mark = co.base
    e, rb, rep, row = alloc(co, [32, 512]), alloc(co, [32, 8]), alloc(co, [32, 8, P]), alloc(co, [P, 8, 512])
    d = (load_small(co, e[:, :], A["buckets"][:, :]), load_small(co, rb[:, :], A["rel_bias"][:, :]))
    outs = []
    co.dv.wait_ge(d, cdep)
    for h in range(8):
        t = co.dv.tensor_scalar(rep[:, h, :], co.cst[0:32, C_ONE:C_ONE + P], rb[:, HP[h]:HP[h] + 1], None, ALU.mult).then_inc(co.s_dv)
        b = next_bank(co)
        co.pe.wait_ge(t, b.drained)
        t = co.pe.matmul(b.ap[:, :], rep[:, h, :], e[:, :], skip_group_check=True, start=True, stop=True).then_inc(co.s_pe)
        co.ac.wait_ge(t)
        b.drained = co.ac.activation(row[:, h, :], b.ap[:, :], ACT.Copy).then_inc(co.s_ac)
        outs.append(b.drained)
    co.po.wait_ge(tuple(outs))
    co.t5 = load_small(co, A["t5"].rearrange("h p s -> p h s"), row[:, :, :])
    co.base = mark


def ffn1(co, l, i, nxt):
    A = co.A
    flush(co)
    w = 0 if i == 0 else 1
    mark = co.base
    got = []
    y = co.y
    fe = counts(co)
    ffn(co, A["ffn_w_in"][l, w], A["ffn_w_out"][l, w], residual(co, y, 2 * ALPHA, got, fe))
    spawn(co, layer_norm(co, y, tuple(got), 4e-5, nxt))
    co.base = mark


def pair(co, dst, banks, tok, a, n, *deps):
    co.ac.wait_ge(tok, deps)
    t0 = co.ac.activation(dst[:, 0, :], banks[0].ap[:, a:a + n], ACT.Copy).then_inc(co.s_ac)
    co.dv.wait_ge(tok, deps)
    t1 = co.dv.tensor_copy(dst[:, 1, :], banks[1].ap[:, a:a + n]).then_inc(co.s_dv)
    banks[0].drained, banks[1].drained = (banks[0].drained, t0), (banks[1].drained, t1)
    return (t0, t1)


def mixer(co, l, nxt):
    A = co.A
    flush(co)
    w = A["w_mix_in"][l]
    xt = (co.xh, co.xl)
    start = co.base
    yt = {i: (alloc(co, [P, 4, 256], F32R), alloc(co, [P, 4, 256], F32R)) for i in (0, 2)}
    tk = [alloc(co, [P, 2, 512]) for _ in range(2)]
    fe = counts(co)
    tkfree = [fe, fe]
    ydep = {}
    turn = [0]

    def tokens_of(banks, tok, n, then):
        i = turn[0] % 2
        turn[0] += 1

        def gen():
            s = pair(co, tk[i][:, :, 0:n], banks, tok, 0, n, tkfree[i])
            yield
            tkfree[i] = then(tk[i], s)
        spawn(co, gen())

    qst, kst, vs = alloc(co, [P, 4, 256]), alloc(co, [P, 4, 256]), alloc(co, [P, 2, 512])
    low = co.base
    qat, iqt, ikt = alloc(co, [P, 4, 256]), alloc(co, [P, 4, 256]), alloc(co, [P, 1, 256])
    ckv, ckvt, iw = alloc(co, [P, 2, P]), alloc(co, [P, 1, 256]), alloc(co, [P, 2, 8])
    ik2, kvg, sq, ss = alloc(co, [P, 2, P]), alloc(co, [P, P]), alloc(co, [P, P]), alloc(co, [P, 2, 2])
    wuk, wuv = alloc(co, [P, 4, P]), alloc(co, [P, 8, 64])
    b1, L, pt, olt, qlt = (alloc(co, [P, 8, 256]), alloc(co, [P, 8, 256]), alloc(co, [P, 2, 4, P]),
                           alloc(co, [P, 4, P]), alloc(co, [P, 8, P]))
    sc, m8, mx, sm, ya = (alloc(co, [P, 2, 256]), alloc(co, [P, 8]), alloc(co, [P, 8]), alloc(co, [P, 2, 8]),
                          alloc(co, [P, 2, 512]))
    zt = alloc(co, [P, 4, 258])
    cw = alloc(co, [12, P])
    cwt = alloc(co, [P, 12])
    dep = {}
    co.po.wait_ge(fe)
    dep["w"] = (load_small(co, wuk[:, :, :], A["w_uk"][l].rearrange("(a b) d c -> (b d) a c", b=2)),
                load_small(co, wuv[:, :, :], A["w_uv"][l].rearrange("h c d -> c h d")),
                load_small(co, kvg[:, :], A["kv_norm_g"][l:l + 1, :].to_broadcast([P, P])),
                load_small(co, cw[:, :], A["conv_w"][l].rearrange("w (k p) -> (w k) p", p=P)))
    skew = bass.AP(tensor=A["t5"].tensor, offset=A["t5"].offset + 127, ap=[[511, P], [P * 512, 8], [1, 256]])
    co.po.wait_ge(fe, co.t5)
    dep["b1"] = load_small(co, b1[:, :, :], skew)

    def on_qa(s, tok):
        dep["qa"] = t32(co, lambda k, t: s[:, t, k * P:(k + 1) * P], 4, qat[:, :, :], tok, fe)
        return pe_mark(co)

    def on_mid(s, tok):
        dep["iq0"] = t32(co, lambda k, t: s[:, t, P + k * P:P + (k + 1) * P], 3, iqt[:, :, :], tok, fe)
        p = pe_mark(co)
        done = []
        co.ac.wait_ge(tok, fe)
        for t in range(2):
            co.ac.wait_ge(done)
            a = co.ac.activation(sq[:, :], s[:, t, 0:P], ACT.Square, accum_out=ss[:, t, 0:1]).then_inc(co.s_ac)
            done = a
            co.dv.wait_ge(a)
            a = co.dv.tensor_scalar(ss[:, t, 0:1], ss[:, t, 0:1], 1.0 / P, 1e-5, ALU.mult, ALU.add).then_inc(co.s_dv)
            co.po.wait_ge(a)
            a = co.po.tensor_tensor(ss[:, t, 1:2], ss[:, t, 0:1], minus_half(co, ss[:, t, 0:1]), ALU.pow).then_inc(co.s_po)
            co.dv.wait_ge(a, dep["w"])
            a = co.dv.scalar_tensor_tensor(ckv[:, t, :], s[:, t, 0:P], ss[:, t, 1:2], kvg[:, :], ALU.mult, ALU.mult).then_inc(co.s_dv)
        dep["ckv"] = a
        return (p, a)

    def on_last(s, tok):
        dep["iq1"] = t32(co, lambda k, t: s[:, t, 0:P], 1, iqt[:, 3:4, :], tok, fe)
        p = pe_mark(co)
        co.dv.wait_ge(tok, fe)
        a = co.dv.tensor_scalar(iw[:, :, :], s[:, :, 192:200], (8 ** -0.5) * (64 ** -0.5), None, ALU.mult).then_inc(co.s_dv)
        co.dv.wait_ge(tok, fe)
        for r in range(2):
            b = co.dv.tensor_copy(ik2[:, :, r * 64:(r + 1) * 64], s[:, :, 128:192]).then_inc(co.s_dv)
        dep["iw"] = a
        dep["ik"] = t32(co, lambda k, t: ik2[:, t, :], 1, ikt[:, :, :], b, fe)
        dep["ckvt"] = t32(co, lambda k, t: ckv[:, t, :], 1, ckvt[:, :, :], dep["ckv"], fe)
        return (p, b)

    def ev(then, n=512):
        return lambda banks, tok: tokens_of(banks, tok, n, then)

    gemm(co, xt, co.xdep, w, 0, 512, ev(on_qa))
    gemm(co, xt, co.xdep, w, 512, 512, ev(on_mid))
    gemm(co, xt, co.xdep, w, 1024, 200, ev(on_last, 200))

    def dsa():
        yield
        yield
        Lfree = scfree = ptfree = olfree = qlfree = smfree = None
        for t in range(2):
            nk = (t + 1) * P
            ts_ = slice(t * P, (t + 1) * P)
            ql = []
            for g in range(2):
                b = next_bank(co)
                co.pe.wait_ge(dep['qa'], dep['w'], b.drained)
                for i in range(4):
                    tok = co.pe.matmul(b.ap[:, i * P:(i + 1) * P], wuk[64 * g:64 * g + 64, i, :], qat[64 * g:64 * g + 64, i, ts_], skip_group_check=True, start=True, stop=True).then_inc(co.s_pe, i == 3)
                co.ac.wait_ge(tok, qlfree, fe)
                b.drained = co.ac.activation(qlt[:, 4 * g:4 * g + 4, :], b.ap.rearrange("p (h n) -> p h n", h=4), ACT.Copy, scale=0.125).then_inc(co.s_ac)
                ql.append(b.drained)
            rel = []
            for g in range(4):
                b = next_bank(co)
                r = slice(64 * (g // 2), 64 * (g // 2) + 64)
                co.pe.wait_ge(dep['iq0'], dep['iq1'], dep['ik'], b.drained)
                for i in range(2):
                    tok = co.pe.matmul(b.ap[:, i * nk:(i + 1) * nk], iqt[r, HP[2 * g + i] // 2, ts_], ikt[r, 0, 0:nk], skip_group_check=True, start=True, stop=True).then_inc(co.s_pe, i == 1)
                co.ac.wait_ge(tok, Lfree, fe)
                b.drained = co.ac.activation(L[:, 2 * g:2 * g + 2, 0:nk], b.ap[:, 0:2 * nk].rearrange("p (h n) -> p h n", h=2), ACT.Relu).then_inc(co.s_ac)
                rel.append(b.drained)
            yield
            neg = co.cst[:, C_NEG + 256 - nk:C_NEG + 256]
            tok = scfree
            co.dv.wait_ge(dep['iw'], fe)
            for h in range(8):
                co.dv.wait_ge(rel[h // 2], tok)
                tok = co.dv.scalar_tensor_tensor(sc[:, 0, 0:nk], L[:, h, 0:nk], iw[:, t, HP[h]:HP[h] + 1], neg if h == 0 else sc[:, 0, 0:nk], ALU.mult, ALU.add).then_inc(co.s_dv)
            yield
            for r in range(8):
                v, o = sc[:, r % 2, 0:nk], sc[:, (r + 1) % 2, 0:nk]
                co.dv.wait_ge(tok)
                tok = co.dv.max(m8[:, :], v).then_inc(co.s_dv)
                co.dv.wait_ge(tok)
                tok = co.dv.match_replace(o, m8[:, :], v, -3.3e38).then_inc(co.s_dv)
                if r == 3:
                    yield
            s0 = sc[:, 0, 0:nk]
            co.dv.wait_ge(tok)
            tok = co.dv.tensor_scalar(s0, s0, -3.2e38, -BIG, ALU.is_gt, ALU.mult).then_inc(co.s_dv)
            co.dv.wait_ge(tok)
            tok = co.dv.tensor_tensor(s0, s0, neg, ALU.min).then_inc(co.s_dv)
            Lv = L[:, :, 0:nk]
            co.dv.wait_ge(tok, dep["b1"], fe)
            tok = co.dv.tensor_tensor(Lv, b1[:, :, 256 - nk:256], s0.unsqueeze(1).to_broadcast([P, 8, nk]), ALU.add).then_inc(co.s_dv)
            yield
            lt = []
            for g in range(4):
                b = next_bank(co)
                co.pe.wait_ge(dep['ckvt'], b.drained)
                for h in (2 * g, 2 * g + 1):
                    co.pe.wait_ge(ql[h // 4])
                    m = co.pe.matmul(b.ap[:, (h % 2) * nk:(h % 2 + 1) * nk], qlt[:, h, :], ckvt[:, 0, 0:nk], skip_group_check=True, start=True, stop=True).then_inc(co.s_pe, h % 2 == 1)
                v = L[:, 2 * g:2 * g + 2, 0:nk]
                co.dv.wait_ge(m, tok)
                b.drained = co.dv.tensor_tensor(v, b.ap[:, 0:2 * nk].rearrange("p (h n) -> p h n", h=2), v, ALU.add).then_inc(co.s_dv)
                lt.append(b.drained)
            qlfree = m
            co.dv.wait_ge(tuple(lt))
            tok = co.dv.tensor_reduce(mx[:, :], Lv, AX, ALU.max).then_inc(co.s_dv)
            co.dv.wait_ge(tok)
            tok = co.dv.tensor_scalar(mx[:, :], mx[:, :], -1.0, None, ALU.mult).then_inc(co.s_dv)
            yield
            es = []
            co.ac.wait_ge(tok, smfree, fe)
            for h in range(8):
                es.append(co.ac.activation(L[:, h, 0:nk], L[:, h, 0:nk], ACT.Exp, bias=mx[:, h:h + 1], accum_out=sm[:, t, h:h + 1]).then_inc(co.s_ac))
            co.dv.wait_ge(tuple(es))
            rc = co.dv.reciprocal(sm[:, t, :], sm[:, t, :]).then_inc(co.s_dv)
            yb = next_bank(co, hold=True)
            for g in range(2):
                cps = []
                for s in range(t + 1):
                    b = next_bank(co)
                    co.pe.wait_ge(b.drained)
                    for h in range(4):
                        co.pe.wait_ge(es[4 * g + h])
                        m = co.pe.transpose(b.ap[:, h * P:(h + 1) * P], L[:, 4 * g + h, s * P:(s + 1) * P], ident(co, L[:, 4 * g + h, s * P:(s + 1) * P])).then_inc(co.s_pe, h == 3)
                    o, i = pt[:, s, :, :], b.ap.rearrange("p (h n) -> p h n", h=4)
                    q = co.ac if s == 0 else co.dv
                    q.wait_ge(m, ptfree, fe)
                    b.drained = q.copy(o, i).then_inc(co.s_ac if q is co.ac else co.s_dv)
                    cps.append(b.drained)
                yield
                b = next_bank(co)
                co.pe.wait_ge(dep['ckv'], b.drained)
                for s in range(t + 1):
                    co.pe.wait_ge(cps[s])
                    m = co.pe.matmul(b.ap, ckv[:, s, :], pt[:, s, :, :].rearrange("p h n -> p (h n)"), start=s == 0, stop=s == t, skip_group_check=True).then_inc(co.s_pe, s == t)
                ptfree = m
                co.dv.wait_ge(m, olfree, fe)
                b.drained = c = co.dv.tensor_copy(olt[:, :, :], b.ap.rearrange("p (h n) -> p h n", h=4)).then_inc(co.s_dv)
                yield
                for h in range(4):
                    hh = 4 * g + h
                    co.pe.wait_ge(c, yb.drained, dep["w"])
                    m = co.pe.matmul(yb.ap[:, hh * 64:(hh + 1) * 64], olt[:, h, :], wuv[:, HP[hh], :], skip_group_check=True, start=True, stop=True).then_inc(co.s_pe, h == 3)
                olfree = m
            Lfree = m
            scfree = m
            co.dv.wait_ge(m, rc, fe)
            for g in range(2):
                yb.drained = co.dv.tensor_tensor(ya[:, t, :].rearrange("p (a b d) -> p b a d", a=4, b=2)[:, g], yb.ap.rearrange("p (b a d) -> p b a d", a=4, b=2)[:, g], sm[:, t, 4 * g:4 * g + 4].unsqueeze(2).to_broadcast([P, 4, 64]), ALU.mult).then_inc(co.s_dv)
            yb.held = False
            dep[f"ya{t}"] = yb.drained
            yield
        ydep[0] = to_t(co, lambda t, k: ya[:, t, k * P:(k + 1) * P], 4, yt[0], (dep["ya0"], dep["ya1"]), fe)

    spawn(co, dsa())

    def on_cc(s, tok):
        dep["cc"] = (s, tok)
        return None

    def conv_z(banks, tok):
        s, ctok = dep["cc"]
        i = turn[0] % 2
        turn[0] += 1
        z = tk[i]

        def gen():
            co.dv.wait_ge(tok, ctok, tkfree[i])
            for t in range(2):
                m = co.dv.tensor_tensor(z[:, t, :], banks[t].ap[:, :], s[:, t, :], ALU.mult).then_inc(co.s_dv)
                banks[t].drained = m
            tkfree[1 - i] = m
            co.dv.wait_ge(fe)
            a = co.dv.memset(zt[:, :, 0:2], 0.0).then_inc(co.s_dv)
            yield
            got = t32(co, lambda k, t: z[:, t, k * P:(k + 1) * P], 4, zt[:, :, 2:258], m, fe)
            tkfree[i] = pe_mark(co)
            b = next_bank(co)
            co.pe.wait_ge(dep["w"], b.drained)
            m = co.pe.transpose(b.ap[:, 0:12], cw[:, :], ident(co, cw[:, :])).then_inc(co.s_pe)
            co.dv.wait_ge(m, fe)
            b.drained = m = co.dv.tensor_copy(cwt[:, :], b.ap[:, 0:12]).then_inc(co.s_dv)
            dep["z"] = (got, a, m)
        spawn(co, gen())

    def conv_b(s, tok):
        c = conv_y
        bt = dep["y"]
        hi, lo = yt[2]
        out = []
        for k0 in (0, 2):
            b = next_bank(co)
            co.pe.wait_ge(tok, b.drained)
            for k in (k0, k0 + 1):
                for t in range(2):
                    m = co.pe.transpose(b.ap[:, (k - k0) * 256 + t * P:(k - k0) * 256 + (t + 1) * P], s[:, t, k * P:(k + 1) * P], ident(co, s[:, t, k * P:(k + 1) * P])).then_inc(co.s_pe, t == 1)
            v = c[:, k0:k0 + 2, :]
            co.dv.wait_ge(m, bt)
            b.drained = m = co.dv.tensor_tensor(v, b.ap.rearrange("p (k n) -> p k n", k=2), v, ALU.mult).then_inc(co.s_dv)
            co.ac.wait_ge(m, fe)
            a = co.ac.activation(hi[:, k0:k0 + 2, :], v, ACT.Copy).then_inc(co.s_ac)
            co.dv.wait_ge(a)
            out.append((a, co.dv.tensor_tensor(lo[:, k0:k0 + 2, :], v, hi[:, k0:k0 + 2, :].bitcast(F32), ALU.subtract).then_inc(co.s_dv)))
        ydep[2] = out
        return pe_mark(co)

    conv_y = alloc(co, [P, 4, 256])

    def conv():
        yield
        co.dv.wait_ge(dep['z'], fe)
        for k in range(4):
            a = co.dv.tensor_scalar(conv_y[:, k, :], zt[:, k, 2:258], cwt[:, 8 + k:9 + k], None, ALU.mult).then_inc(co.s_dv)
            co.dv.wait_ge(a)
            a = co.dv.scalar_tensor_tensor(conv_y[:, k, :], zt[:, k, 1:257], cwt[:, 4 + k:5 + k], conv_y[:, k, :], ALU.mult, ALU.add).then_inc(co.s_dv)
            co.dv.wait_ge(a)
            a = co.dv.scalar_tensor_tensor(conv_y[:, k, :], zt[:, k, 0:256], cwt[:, k:k + 1], conv_y[:, k, :], ALU.mult, ALU.add).then_inc(co.s_dv)
        dep["y"] = a

    gemm(co, xt, co.xdep, w, 3272, 512, ev(on_cc))
    gemm(co, xt, co.xdep, w, 3784, 512, conv_z)
    spawn(co, conv())
    gemm(co, xt, co.xdep, w, 2760, 512, ev(conv_b))

    def on_qs(s, tok):
        dep["qs"] = t32(co, lambda k, t: s[:, t, k * P:(k + 1) * P], 4, qst[:, :, :], tok, fe, scale=0.125)
        return pe_mark(co)

    def on_ks(s, tok):
        dep["ks"] = t32(co, lambda k, t: s[:, t, k * P:(k + 1) * P], 4, kst[:, :, :], tok, fe)
        return pe_mark(co)

    def on_vs(banks, tok):
        dep["vs"] = pair(co, vs[:, :, :], banks, tok, 0, 512, fe)

    gemm(co, xt, co.xdep, w, 1224, 512, ev(on_qs))
    gemm(co, xt, co.xdep, w, 1736, 512, ev(on_ks))
    gemm(co, xt, co.xdep, w, 2248, 512, on_vs)
    flush(co)
    co.base = low
    yt[1] = (alloc(co, [P, 4, 256], F32R), alloc(co, [P, 4, 256], F32R))
    sg = alloc(co, [P, 2, 3, D])
    bb = [alloc(co, [P, 512]) for _ in range(2)]
    low = co.base
    fe2 = counts(co)
    zs = [alloc(co, [P, 8, P]) for _ in range(2)]
    sp11, sp0, tmp = alloc(co, [P, 8, P]), alloc(co, [P, 8, P]), alloc(co, [P, 2, 512])
    cs = co.cst

    def stick():
        sp_done = {}
        zfree = {0: fe2, 1: fe2}
        tfree = {0: fe2, 1: fe2}
        spfree = fe2
        yb = {}
        for i, (s, t) in enumerate(((0, 0), (1, 1), (0, 1))):
            z = zs[i % 2]
            sp = sp11 if (s, t) == (1, 1) else sp0
            toks = []
            for g in range(2):
                b = next_bank(co)
                r = slice(64 * g, 64 * g + 64)
                co.pe.wait_ge(dep['qs'], dep['ks'], b.drained)
                for h in range(4):
                    m = co.pe.matmul(b.ap[:, h * P:(h + 1) * P], kst[r, h, s * P:(s + 1) * P], qst[r, h, t * P:(t + 1) * P], skip_group_check=True, start=True, stop=True).then_inc(co.s_pe, h == 3)
                zg, spg, tg = z[:, 4 * g:4 * g + 4, :], sp[:, 4 * g:4 * g + 4, :], tmp[:, g, :].rearrange(
                    "p (h n) -> p h n", h=4)
                co.ac.wait_ge(m, zfree[i % 2])
                b.drained = c = co.ac.activation(zg, b.ap.rearrange("p (h n) -> p h n", h=4), ACT.Copy).then_inc(co.s_ac)
                co.dv.wait_ge(c, tfree[g])
                a = co.dv.scalar_tensor_tensor(tg, zg, -1.0, zg, ALU.mult, ALU.max).then_inc(co.s_dv)
                co.ac.wait_ge(a)
                a = co.ac.activation(tg, tg, ACT.Exp, scale=-1.0).then_inc(co.s_ac)
                co.ac.wait_ge(a)
                a = co.ac.activation(tg, tg, ACT.Ln, bias=1.0).then_inc(co.s_ac)
                co.dv.wait_ge(a, spfree)
                a = co.dv.scalar_tensor_tensor(spg, zg, 0.0, tg, ALU.max, ALU.add).then_inc(co.s_dv)
                tfree[g] = a
                if s == t:
                    co.dv.wait_ge(a)
                    a = co.dv.tensor_tensor(spg, spg, cs[:, C_SM:C_SM + P].unsqueeze(1).to_broadcast([P, 4, P]), ALU.mult).then_inc(co.s_dv)
                    co.dv.wait_ge(c, a)
                    c = co.dv.tensor_tensor(zg, zg, cs[:, C_SN:C_SN + P].unsqueeze(1).to_broadcast([P, 4, P]), ALU.add).then_inc(co.s_dv)
                toks.append((a, c))
            sp_done[(s, t)] = toks
            yield
            yield
            at = []
            for g in range(2):
                b = next_bank(co)
                f = lambda v: v[:, 4 * g:4 * g + 4, :].rearrange("p h n -> p (h n)")
                co.pe.wait_ge(toks[g], b.drained)
                m = co.pe.matmul(b.ap, cs[:, C_TRI:C_TRI + P], f(sp), stop=s == t, skip_group_check=True, start=True).then_inc(co.s_pe)
                if s != t:
                    co.pe.wait_ge(sp_done[(1, 1)][g])
                    m = co.pe.matmul(b.ap, cs[:, C_ONE:C_ONE + P], f(sp11), start=False, skip_group_check=True, stop=True).then_inc(co.s_pe)
                spfree = m
                zg = z[:, 4 * g:4 * g + 4, :]
                co.dv.wait_ge(m, toks[g])
                b.drained = a = co.dv.tensor_tensor(zg, zg, b.ap.rearrange("p (h n) -> p h n", h=4), ALU.subtract).then_inc(co.s_dv)
                co.ac.wait_ge(a)
                at.append(co.ac.activation(zg, zg, ACT.Exp).then_inc(co.s_ac))
            yield
            if t not in yb:
                yb[t] = next_bank(co, hold=True)
            first = s == t
            last = (s, t) != (1, 1)
            co.pe.wait_ge(dep['vs'], yb[t].drained)
            for h in range(8):
                co.pe.wait_ge(at[h // 4])
                m = co.pe.matmul(yb[t].ap[:, HP[h] * 64:(HP[h] + 1) * 64], z[:, h, :], vs[:, s, HP[h] * 64:(HP[h] + 1) * 64], start=first and h == 0, stop=last, skip_group_check=True).then_inc(co.s_pe, h == 7)
            zfree[i % 2] = m
            if last:
                o = tk[0][:, t, :]
                co.ac.wait_ge(m, tkfree[0])
                yb[t].drained = c = co.ac.activation(o, yb[t].ap, ACT.Copy).then_inc(co.s_ac)
                yb[t].held = False
                dep[f"yb{t}"] = c
            yield
        ydep[1] = to_t(co, lambda t, k: tk[0][:, t, k * P:(k + 1) * P], 4, yt[1], (dep["yb0"], dep["yb1"]), fe2)

    spawn(co, stick())
    bfree = [fe2, fe2]
    sgd = {}
    for i in range(3):
        for c in range(2):
            n = 2 * i + c
            co.po.wait_ge(bfree[n % 2])
            bd = load_small(co, bb[n % 2][:, :], A["b_gate"][l, i:i + 1, c * 512:(c + 1) * 512].to_broadcast([P, 512]))

            def evac(banks, tok):
                for t in range(2):
                    o = sg[:, t, i, c * 512:(c + 1) * 512]
                    co.dv.wait_ge(tok, bd, fe2)
                    banks[t].drained = a = co.dv.tensor_tensor(o, banks[t].ap, bb[n % 2][:, :], ALU.add).then_inc(co.s_dv)
                    co.ac.wait_ge(a)
                    sgd[(i, c, t)] = co.ac.activation(o, o, ACT.Sigmoid).then_inc(co.s_ac)
                bfree[n % 2] = a
            gemm(co, xt, co.xdep, w, 4296 + n * 512, 512, evac)
    flush(co)
    co.xtfree = pe_mark(co)
    co.base = low
    mg, y = alloc(co, [P, 2, D]), co.y
    fe3 = counts(co)
    mgd = [[None, None], [None, None]]
    for i in (0, 2, 1):
        for c in range(2):
            def evac(banks, tok):
                for t in range(2):
                    s, o = sg[:, t, i, c * 512:(c + 1) * 512], mg[:, t, c * 512:(c + 1) * 512]
                    co.dv.wait_ge(tok, sgd[(i, c, t)], fe3)
                    a = co.dv.tensor_tensor(o if i == 0 else s, banks[t].ap, s, ALU.mult).then_inc(co.s_dv)
                    banks[t].drained = a
                    if i:
                        co.dv.wait_ge(a, mgd[c][t])
                        a = co.dv.tensor_tensor(o, o, s, ALU.add).then_inc(co.s_dv)
                    mgd[c][t] = a
            gemm(co, yt[i], ydep[i], A["w_branch"][l, i], c * 512, 512, evac)
    mdep = to_t(co, lambda t, k: mg[:, t, k * P:(k + 1) * P], 8, xt, tuple(mgd[0] + mgd[1]), co.xtfree)
    got = []
    res = residual(co, y, ALPHA, got, fe3)
    for c in range(2):
        gemm(co, xt, mdep, A["w_mix_out"][l], c * 512, 512, res(c * 512, 512))
    co.xtfree = pe_mark(co)
    spawn(co, layer_norm(co, y, tuple(got), 1e-5, nxt))
    co.base = start


def cross(co, l, nxt):
    A = co.A
    start = co.base
    kt, v = alloc(co, [P, 4, 256]), alloc(co, [P, 2, 512])
    kept = co.base
    mem, mh, ml = alloc(co, [P, 2, D]), alloc(co, [P, 8, 256], F32R), alloc(co, [P, 8, 256], F32R)
    fe = counts(co)
    co.po.wait_ge(fe)
    md = load_small(co, mem[:, :, :], A["mem"][0].rearrange("(t p) d -> p t d", p=P))
    mdep = to_t(co, lambda t, k: mem[:, t, k * P:(k + 1) * P], 8, (mh, ml), md, fe)
    dep = {}
    w = A["xa_wkv"][l]

    def on_k(banks, tok):
        def gen():
            s = pair(co, mem[:, :, 0:512], banks, tok, 0, 512, md, mdep)
            yield
            dep["k"] = t32(co, lambda k, t: mem[:, t, k * P:(k + 1) * P], 4, kt[:, :, :], s, fe)
        spawn(co, gen())

    def on_v(banks, tok):
        dep["v"] = pair(co, v[:, :, :], banks, tok, 0, 512, fe)

    gemm(co, (mh, ml), mdep, w, 0, 512, on_k)
    gemm(co, (mh, ml), mdep, w, 512, 512, on_v)
    flush(co)
    co.base = kept
    qt, L, pt = alloc(co, [P, 4, 256]), alloc(co, [P, 2, 4, 256]), alloc(co, [P, 2, 4, 256])
    q, y, mx, sm = alloc(co, [P, 2, 512]), co.y, alloc(co, [P, 2, 4]), alloc(co, [P, 2, 4])
    oh, ol = alloc(co, [P, 4, 256], F32R), alloc(co, [P, 4, 256], F32R)
    fe = counts(co)

    def on_q(banks, tok):
        dep["qs"] = pair(co, q[:, :, :], banks, tok, 0, 512, fe)

    gemm(co, (co.xh, co.xl), co.xdep, A["xa_wq"][l], 0, 512, on_q)
    co.xtfree = pe_mark(co)
    dep["q"] = t32(co, lambda k, t: q[:, t, k * P:(k + 1) * P], 4, qt[:, :, :], dep["qs"], fe)
    cps = {}
    for t in range(2):
        lt = []
        for g in range(2):
            b = next_bank(co)
            co.pe.wait_ge(dep['q'], dep['k'], b.drained)
            for h in (2 * g, 2 * g + 1):
                m = co.pe.matmul(b.ap[:, (h % 2) * 256:(h % 2 + 1) * 256], qt[:, h, t * P:(t + 1) * P], kt[:, h, :], skip_group_check=True, start=True, stop=True).then_inc(co.s_pe, h % 2 == 1)
            co.ac.wait_ge(m, fe)
            b.drained = co.ac.activation(L[:, t, 2 * g:2 * g + 2, :], b.ap.rearrange("p (h n) -> p h n", h=2), ACT.Copy, scale=128 ** -0.5).then_inc(co.s_ac)
            lt.append(b.drained)
        co.dv.wait_ge(tuple(lt))
        a = co.dv.tensor_reduce(mx[:, t, :], L[:, t, :, :], AX, ALU.max).then_inc(co.s_dv)
        co.dv.wait_ge(a)
        a = co.dv.tensor_scalar(mx[:, t, :], mx[:, t, :], -1.0, None, ALU.mult).then_inc(co.s_dv)
        co.ac.wait_ge(a)
        es = [co.ac.activation(L[:, t, h, :], L[:, t, h, :], ACT.Exp, bias=mx[:, t, h:h + 1], accum_out=sm[:, t, h:h + 1]).then_inc(co.s_ac)
              for h in range(4)]
        co.dv.wait_ge(tuple(es))
        a = co.dv.reciprocal(sm[:, t, :], sm[:, t, :]).then_inc(co.s_dv)
        co.dv.wait_ge(a)
        nm = [co.dv.tensor_scalar(L[:, t, h, :], L[:, t, h, :], sm[:, t, h:h + 1], None, ALU.mult).then_inc(co.s_dv) for h in range(4)]
        for s in range(2):
            b = next_bank(co)
            co.pe.wait_ge(b.drained)
            for h in range(4):
                co.pe.wait_ge(nm[h])
                m = co.pe.transpose(b.ap[:, h * P:(h + 1) * P], L[:, t, h, s * P:(s + 1) * P], ident(co, L[:, t, h, s * P:(s + 1) * P])).then_inc(co.s_pe, h == 3)
            q = co.ac if s == 0 else co.dv
            q.wait_ge(m, fe)
            b.drained = q.copy(pt[:, s, :, t * P:(t + 1) * P], b.ap.rearrange("p (h n) -> p h n", h=4)).then_inc(co.s_ac if q is co.ac else co.s_dv)
            cps[(s, t)] = b.drained
    odep = []
    for g in range(2):
        b = next_bank(co)
        co.pe.wait_ge(dep['v'], b.drained)
        for h in (2 * g, 2 * g + 1):
            for s in range(2):
                co.pe.wait_ge(cps[s, 0], cps[s, 1])
                m = co.pe.matmul(b.ap[:, (h % 2) * 256:(h % 2 + 1) * 256], v[:, s, h * P:(h + 1) * P], pt[:, s, h, :], start=s == 0, stop=s == 1, skip_group_check=True).then_inc(co.s_pe, s == 1)
        ps = b.ap.rearrange("p (h n) -> p h n", h=2)
        co.ac.wait_ge(m, fe)
        a = co.ac.activation(oh[:, 2 * g:2 * g + 2, :], ps, ACT.Copy).then_inc(co.s_ac)
        co.dv.wait_ge(m, a)
        c = co.dv.tensor_tensor(ol[:, 2 * g:2 * g + 2, :], ps, oh[:, 2 * g:2 * g + 2, :].bitcast(F32), ALU.subtract).then_inc(co.s_dv)
        b.drained = (a, c)
        odep.append((a, c))
    got = []
    res = residual(co, y, ALPHA, got, fe)
    for c in range(2):
        gemm(co, (oh, ol), odep, A["xa_wo"][l], c * 512, 512, res(c * 512, 512))
    spawn(co, layer_norm(co, y, tuple(got), 1e-5, nxt))
    co.base = start


"""The second block. A stream is one of x and ctx: its tile, when it stands, who read it last."""


def begin(co):
    A = co.A
    co.base = co.lgbase
    co.top -= 8192
    co.ctx_t = alloc(co, [P, 2, D])
    co.mc = [alloc(co, [P, 6, 8, 2])] * 2
    co.gt = [alloc(co, [P, 2, D])] * 2
    co.gb = alloc(co, [P, D])
    co.ac_, co.gcol = alloc(co, [P, 2, 8, 2]), alloc(co, [P, 32])
    fe = counts(co)
    co.gbfree = fe
    co.yfree = fe
    co.po.wait_ge(fe)
    co.cready = load_small(co, co.ctx_t[:, :, :], A["ctx_2"][0].rearrange("(t p) d -> p t d", p=P))
    co.tile = [co.x, co.ctx_t]
    co.ready = [co.xready, co.cready]
    co.afree = fe


def modulation(co, l):
    A = co.A
    start = co.base
    rows, cs = alloc(co, [32, P]), alloc(co, [P, 16])
    ch, cl = alloc(co, [P, 8, P], F32R), alloc(co, [P, 8, P], F32R)
    mb = [alloc(co, [P, 512]) for _ in range(2)]
    rt = [alloc(co, [P, 512]) for _ in range(2)]
    mc, gt = co.mc[l], co.gt[l]
    fe = counts(co)
    co.po.wait_ge(fe)
    d = (load_small(co, rows[0:8, :], A["c_2"][0].rearrange("(k p) -> k p", p=P)),
         load_small(co, rows[8:16, :], A["c_ctx_2"].rearrange("(k p) -> k p", p=P)),
         load_small(co, rows[16:24, :], A["norm_mix_g_2"][l].rearrange("(k p) -> k p", p=P)),
         load_small(co, rows[24:32, :], A["norm_ffn_g_2"][l].rearrange("(k p) -> k p", p=P)))
    b = next_bank(co)
    co.pe.wait_ge(d, b.drained)
    m = co.pe.transpose(b.ap[:, 0:32], rows[:, :], ident(co, rows[:, :])).then_inc(co.s_pe)
    co.dv.wait_ge(m, fe)
    g = co.dv.tensor_copy(co.gcol[:, :], b.ap[:, 0:32]).then_inc(co.s_dv)
    co.ac.wait_ge(g, fe)
    s = co.ac.activation(cs[:, :], b.ap[:, 0:16], ACT.Silu).then_inc(co.s_ac)
    b.drained = (g, s)
    toks = []
    for i in range(2):
        src = cs[:, 8 * i:8 * i + 8].unsqueeze(2).to_broadcast([P, 8, 64])
        o, q = ch[:, :, 64 * i:64 * i + 64], cl[:, :, 64 * i:64 * i + 64]
        co.ac.wait_ge(s, fe)
        a = co.ac.activation(o, src, ACT.Copy).then_inc(co.s_ac)
        co.dv.wait_ge(a, fe)
        toks.append(co.dv.tensor_tensor(q, src, o.bitcast(F32), ALU.subtract).then_inc(co.s_dv))
    dep = tuple(toks)
    free = [fe, fe]
    bfree = [fe, fe]
    out = []
    for j in range(12):
        co.po.wait_ge(bfree[j % 2])
        bd = load_small(co, mb[j % 2][:, :], A["mod_b_2"][l:l + 1, j * 512:(j + 1) * 512].to_broadcast([P, 512]))

        def evac(banks, tok):
            blk, half = j // 2, j % 2
            gate = blk in (2, 5)
            o = gt[:, blk // 3, half * 512:(half + 1) * 512] if gate else rt[j % 2][:, :]
            co.dv.wait_ge(tok, bd, fe if gate else free[j % 2])
            a = co.dv.tensor_tensor(o, banks[0].ap, mb[j % 2][:, :], ALU.add).then_inc(co.s_dv)
            banks[0].drained = bfree[j % 2] = a
            if gate:
                out.append(a)
                return

            def gen(jj, r):
                yield
                b = next_bank(co)
                co.pe.wait_ge(a, b.drained)
                for k in range(4):
                    m = co.pe.transpose(b.ap[:, k * P:(k + 1) * P], r[:, k * P:(k + 1) * P], ident(co, r[:, k * P:(k + 1) * P])).then_inc(co.s_pe, k == 3)
                free[jj] = m
                co.dv.wait_ge(m, fe)
                b.drained = co.dv.tensor_copy(mc[:, blk, 4 * half:4 * half + 4, :], b.ap.rearrange("p (k a n) -> p k a n", k=4, a=2)[:, :, :, 0]).then_inc(co.s_dv)
                out.append(b.drained)
            spawn(co, gen(j % 2, rt[j % 2]))
        gemm(co, (ch, cl), dep, A["mod_w_2"][l], j * 512, 512, evac, tt=1)
    flush(co)
    for i in range(2):
        v = co.ac_[:, i, :, :]
        co.dv.wait_ge(tuple(out), co.afree)
        a = co.dv.tensor_scalar(v, mc[:, 1 + 3 * i, :, :], 1.0, None, ALU.add).then_inc(co.s_dv)
        co.dv.wait_ge(a, g)
        a = co.dv.tensor_tensor(v, v, co.gcol[:, 16 + 8 * i:24 + 8 * i].unsqueeze(2).to_broadcast([P, 8, 2]), ALU.mult).then_inc(co.s_dv)
    co.moddep = (a, tuple(out))
    co.base = start


def prenorm(co, l, s, f):
    src, y, rs = co.tile[s], co.y, co.rs
    norm = []
    co.ac.wait_ge(co.ready[s], co.yfree, co.rsfree)
    for t in range(2):
        a = co.ac.activation(y[:, t, :], src[:, t, :], ACT.Square, accum_out=rs[:, t, 0:1]).then_inc(co.s_ac)
        co.dv.wait_ge(a)
        a = co.dv.tensor_scalar(rs[:, t, 0:1], rs[:, t, 0:1], 1.0 / D, 1e-6, ALU.mult, ALU.add).then_inc(co.s_dv)
        co.po.wait_ge(a)
        a = co.po.tensor_tensor(rs[:, t, 1:2], rs[:, t, 0:1], minus_half(co, rs[:, t, 0:1]), ALU.pow).then_inc(co.s_po)
        co.dv.wait_ge(a)
        norm.append(co.dv.tensor_scalar(y[:, t, :], src[:, t, :], rs[:, t, 1:2], None, ALU.mult).then_inc(co.s_dv))
    co.rsfree = norm[1]
    yield
    out = []
    hi, lo, tmp = co.xh, co.xl, co.gb
    wfree = [co.gbfree, co.gbfree]
    for k0 in range(0, 8, 2):
        b = next_bank(co)
        co.pe.wait_ge(b.drained)
        for k in (0, 1):
            for t in range(2):
                co.pe.wait_ge(norm[t])
                m = co.pe.transpose(b.ap[:, k * 256 + t * P:k * 256 + (t + 1) * P], y[:, t, (k0 + k) * P:(k0 + k + 1) * P], ident(co, y[:, t, (k0 + k) * P:(k0 + k + 1) * P])).then_inc(co.s_pe, k == 1 and t == 1)
        j = k0 // 2 % 2
        w = tmp[:, 512 * j:512 * j + 512]
        for k in (0, 1):
            sc, sh = co.ac_[:, f, k0 + k, s:s + 1], co.mc[l][:, 3 * f, k0 + k, s:s + 1]
            co.dv.wait_ge(m, co.moddep, wfree[j])
            v = co.dv.tensor_scalar(w[:, k * 256:(k + 1) * 256], b.ap[:, k * 256:(k + 1) * 256], sc, sh, ALU.mult, ALU.add).then_inc(co.s_dv)
        b.drained = v
        w2 = w.rearrange("p (k n) -> p k n", k=2)
        co.ac.wait_ge(v, co.xtfree)
        a = co.ac.activation(hi[:, k0:k0 + 2, :], w2, ACT.Copy).then_inc(co.s_ac)
        co.dv.wait_ge(a, co.xtfree)
        v = co.dv.tensor_tensor(lo[:, k0:k0 + 2, :], w2, hi[:, k0:k0 + 2, :].bitcast(F32), ALU.subtract).then_inc(co.s_dv)
        wfree[j] = v
        out.append(v)
    co.gbfree = v
    co.yfree = pe_mark(co)
    co.xdep = out
    co.afree = v


def gate_rows(co, l, s, f):
    sel = co.cst[:, (C_S1 if s else C_S0):(C_S1 if s else C_S0) + P]
    out = []
    for c in range(2):
        b = next_bank(co)
        co.pe.wait_ge(co.moddep, b.drained)
        m = co.pe.matmul(b.ap, sel, co.gt[l][:, f, c * 512:(c + 1) * 512], skip_group_check=True, start=True, stop=True).then_inc(co.s_pe)
        co.ac.wait_ge(m, co.gbfree)
        b.drained = co.ac.activation(co.gb[:, c * 512:(c + 1) * 512], b.ap, ACT.Copy).then_inc(co.s_ac)
        out.append(b.drained)
    co.gbdep = tuple(out)


def gated(co, s):
    got = []
    x = co.tile[s]

    def make(c0, n):
        def evac(banks, tok):
            for t in range(2):
                g, p = co.gb[:, c0:c0 + n], banks[t].ap[:, 0:n]
                w, o = co.y[:, t, c0:c0 + n], x[:, t, c0:c0 + n]
                co.dv.wait_ge(tok, co.gbdep, co.yfree)
                a = co.dv.tensor_tensor(w, p, g, ALU.mult).then_inc(co.s_dv)
                banks[t].drained = a
                co.dv.wait_ge(a, co.ready[s])
                got.append(co.dv.tensor_tensor(o, o, w, ALU.add).then_inc(co.s_dv))
        return evac
    return make, got


def ffn2(co, l, s):
    A = co.A
    start = co.base
    spawn(co, prenorm(co, l, s, 1))
    flush(co)
    gate_rows(co, l, s, 1)
    make, got = gated(co, s)
    ffn(co, A["ffn_w_in_2"][l], A["ffn_w_out_2"][l], make)
    co.yfree = co.gbfree = tuple(got)
    co.ready[s] = tuple(got)
    co.base = start


def out_proj(co, l, s, ydep):
    flush(co)
    dep = to_t(co, lambda t, k: co.y[:, t, k * P:(k + 1) * P], 8, (co.xh, co.xl), ydep, co.xtfree)
    co.yfree = pe_mark(co)
    gate_rows(co, l, s, 0)
    make, got = gated(co, s)
    for c in range(2):
        gemm(co, (co.xh, co.xl), dep, co.A["w_out_2"][l], c * 512, 512, make(c * 512, 512))
    co.xtfree = pe_mark(co)
    co.yfree = co.gbfree = tuple(got)
    co.ready[s] = tuple(got)


def groups(co, v, w, n, g, gain, dep, wfree):
    a = v.shape[1]
    ss, ss2 = co.gs[:, 0, 0:a * g], co.gs[:, 1, 0:a * g]
    v3 = ss.rearrange("p (a g) -> p a g", a=a)
    co.dv.wait_ge(dep, wfree)
    tok = co.dv.tensor_tensor(w, v, v, ALU.mult).then_inc(co.s_dv)
    co.dv.wait_ge(tok, co.gsfree)
    tok = co.dv.tensor_reduce(v3, w, AX, ALU.add).then_inc(co.s_dv)
    co.dv.wait_ge(tok)
    tok = co.dv.tensor_scalar(ss, ss, 1.0 / n, 1e-6, ALU.mult, ALU.add).then_inc(co.s_dv)
    co.po.wait_ge(tok)
    tok = co.po.tensor_tensor(ss2, ss, minus_half(co, ss), ALU.pow).then_inc(co.s_po)
    r3 = ss2.rearrange("p (a g) -> p a g", a=a)
    co.dv.wait_ge(tok)
    for i in range(a):
        b = co.dv.tensor_tensor(v[:, i], v[:, i], r3[:, i].unsqueeze(2).to_broadcast([P, g, n]), ALU.mult).then_inc(co.s_dv)
        co.dv.wait_ge(b)
        b = co.dv.tensor_tensor(v[:, i], v[:, i], gain.unsqueeze(1).to_broadcast([P, g, n]), ALU.mult).then_inc(co.s_dv)
    co.gsfree = b
    return b


def rope(co, v, w, w2, g, dep):
    for t in range(2):
        c = co.rt[:, t, 0:64].unsqueeze(1).to_broadcast([P, g, 64])
        co.dv.wait_ge(dep)
        a = co.dv.tensor_tensor(w[:, t], v[:, t], c, ALU.mult).then_inc(co.s_dv)
        for h in range(2):
            o = w2[:, t].rearrange("p g (a h n) -> p g a h n", a=2, h=2)[:, :, :, h]
            i = v[:, t].rearrange("p g (a h n) -> p g a h n", a=2, h=2)[:, :, :, 1 - h]
            s = co.rt[:, t, 64:128].rearrange("p (a h n) -> p a h n", a=2, h=2)[:, :, h].unsqueeze(1)\
                .to_broadcast([P, g, 2, 16])
            co.dv.wait_ge(dep)
            b = co.dv.tensor_tensor(o, i, s, ALU.mult).then_inc(co.s_dv)
        co.dv.wait_ge(a, b)
        a = co.dv.tensor_tensor(v[:, t], w[:, t], w2[:, t], ALU.add).then_inc(co.s_dv)
    return a


def even(co):
    A, l = co.A, 0
    start = co.base
    W = A["ev_w_in_2"][0]
    dkt, dv = alloc(co, [P, 4, 512]), alloc(co, [P, 4, 512])
    knt, krt, mv = alloc(co, [P, 4, 512]), alloc(co, [64, 512]), alloc(co, [P, 4, 512])
    dqt, qnt, qrt = alloc(co, [P, 4, 256]), alloc(co, [P, 4, 256]), alloc(co, [64, 4, 256])
    co.rt, co.gs = alloc(co, [P, 2, P]), alloc(co, [P, 2, 32])
    gn = alloc(co, [P, 1152])
    lam = alloc(co, [P, 4])
    low = co.base
    tk, w1, w2 = alloc(co, [P, 2, 512]), alloc(co, [P, 2, 512]), alloc(co, [P, 2, 512])
    cqh, cql = alloc(co, [P, 2, 256], F32R), alloc(co, [P, 2, 256], F32R)
    ckh, ckl = alloc(co, [P, 1, 256], F32R), alloc(co, [P, 1, 256], F32R)
    lv = alloc(co, [P, 4, 64])
    fe = counts(co)
    co.gsfree = fe
    co.po.wait_ge(fe)
    gd, at = [load_small(co, co.rt[:, :, :], A["rope"][:, :, :])], 0
    gains = {}
    for n, w in (("da_q_g_2", 64), ("da_k_g_2", 64), ("mla_q_a_g_2", 256), ("mla_kv_a_g_2", 128),
                 ("mla_q_g_2", 192), ("mla_k_g_2", 128), ("mla_kr_g_2", 64), ("da_out_g_2", 128)):
        gains[n] = gn[:, at:at + w]
        co.po.wait_ge(fe)
        gd.append(load_small(co, gn[:, at:at + w], A[n].to_broadcast([P, w])))
        at += w
    co.po.wait_ge(fe)
    for i, n in enumerate(("da_lq1_2", "da_lk1_2", "da_lq2_2", "da_lk2_2")):
        gd.append(load_small(co, lv[:, i, :], A[n].to_broadcast([P, 64])))
    gd = tuple(gd)
    co.dv.wait_ge(gd)
    a = co.dv.tensor_scalar(gains["da_out_g_2"], gains["da_out_g_2"], 1.0 - (0.8 - 0.6 * math.exp(0.0)), None, ALU.mult).then_inc(co.s_dv)
    co.dv.wait_ge(gd)
    for i in range(2):
        a = co.dv.tensor_tensor(lv[:, 2 * i, :], lv[:, 2 * i, :], lv[:, 2 * i + 1, :], ALU.mult).then_inc(co.s_dv)
        co.dv.wait_ge(a, fe)
        a = co.dv.tensor_reduce(lam[:, i:i + 1], lv[:, 2 * i, :], AX, ALU.add).then_inc(co.s_dv)
    co.ac.wait_ge(a)
    a = co.ac.activation(lam[:, 0:2], lam[:, 0:2], ACT.Exp).then_inc(co.s_ac)
    co.dv.wait_ge(a)
    a = co.dv.tensor_tensor(lam[:, 2:3], lam[:, 1:2], lam[:, 0:1], ALU.subtract).then_inc(co.s_dv)
    co.dv.wait_ge(a)
    lamd = co.dv.tensor_scalar(lam[:, 2:3], lam[:, 2:3], -(0.8 - 0.6 * math.exp(0.0)), None, ALU.add).then_inc(co.s_dv)
    free = {"tk": fe}
    dep = {}

    def view(v, n, w):
        return v[:, :, 0:n * w].rearrange("p t (g n) -> p t g n", n=w)

    def project(s):
        xt = (co.xh, co.xl)
        roped = s == 0
        k0 = 256 if s == 0 else 0
        ks = slice(k0, k0 + 256)
        kfree = None if s == 1 else ()

        def on_heads(gname, dst, key, cols):
            def evac(banks, tok):
                def gen():
                    a = pair(co, tk[:, :, :], banks, tok, 0, 512, free["tk"])
                    yield
                    a = groups(co, view(tk, 8, 64), view(w1, 8, 64), 64, 8, gains[gname], (a, gd), fe)
                    if roped:
                        a = rope(co, view(tk, 8, 64), view(w1, 8, 64), view(w2, 8, 64), 8, a)
                    yield
                    dep[key, s] = t32(co, lambda k, t: tk[:, t, k * P:(k + 1) * P], 4, dst[:, :, cols], a,
                                           (fe, dep.get("qfree")))
                    free["tk"] = pe_mark(co)
                flush(co)
                spawn(co, gen())
            return evac

        def on_dv(banks, tok):
            for t in range(2):
                o = dv[:, k0 // P + t, :]
                q = co.ac if t else co.dv
                q.wait_ge(tok, fe)
                banks[t].drained = q.copy(o, banks[t].ap).then_inc(co.s_ac if q is co.ac else co.s_dv)
                dep["dv", s, t] = banks[t].drained

        def on_mla(banks, tok):
            def gen():
                a = pair(co, tk[:, :, 0:448], banks, tok, 0, 448, free["tk"])
                yield
                c = groups(co, tk[:, :, 0:256].unsqueeze(2), w1[:, :, 0:256].unsqueeze(2), 256, 1,
                                gains["mla_q_a_g_2"], (a, gd), fe)
                d = groups(co, tk[:, :, 256:384].unsqueeze(2), w1[:, :, 256:384].unsqueeze(2), 128, 1,
                                gains["mla_kv_a_g_2"], (a, gd), fe)
                kr = tk[:, :, 384:448].unsqueeze(2)
                e = groups(co, kr, w1[:, :, 384:448].unsqueeze(2), 64, 1, gains["mla_kr_g_2"], (a, gd), fe)
                if roped:
                    e = rope(co, kr, w1[:, :, 384:448].unsqueeze(2), w2[:, :, 384:448].unsqueeze(2), 1, e)
                yield
                dep["cq"] = to_t(co, lambda t, k: tk[:, t, k * P:(k + 1) * P], 2, (cqh, cql), c,
                                      (fe, dep.get("cqfree")))
                dep["ck"] = to_t(co, lambda t, k: tk[:, t, 256:384], 1, (ckh, ckl), d, (fe, dep.get("cqfree")))
                dep["kr", s] = t32(co, lambda k, t: tk[:, t, 384:448], 1, krt[:, ks].unsqueeze(1), e, fe)
                free["tk"] = pe_mark(co)
            flush(co)
            spawn(co, gen())

        def on_kv(c):
            def evac(banks, tok):
                def gen():
                    a = pair(co, tk[:, :, :], banks, tok, 0, 512, free["tk"])
                    yield
                    kn = tk[:, :, :].rearrange("p t (g n) -> p t g n", n=256)[:, :, :, 0:128]
                    k1 = w1[:, :, :].rearrange("p t (g n) -> p t g n", n=256)[:, :, :, 0:128]
                    e = groups(co, kn, k1, 128, 2, gains["mla_k_g_2"], (a, gd), fe)
                    for t in range(2):
                        v = tk[:, t, :].rearrange("p (g n) -> p g n", n=256)[:, :, 128:256]
                        o = mv[:, k0 // P + t, 256 * c:256 * c + 256].rearrange("p (g n) -> p g n", n=128)
                        co.ac.wait_ge(a, fe)
                        m = co.ac.activation(o, v, ACT.Copy).then_inc(co.s_ac)
                    dep["mv", s, c] = m
                    yield
                    dep["kn", s, c] = t32(co, lambda k, t: tk[:, t, 256 * k:256 * k + 128], 2,
                                               knt[:, 2 * c:2 * c + 2, ks], e, fe)
                    free["tk"] = (pe_mark(co), m)
                flush(co)
                spawn(co, gen())
            return evac

        def on_q(c):
            def evac(banks, tok):
                def gen():
                    a = pair(co, tk[:, :, 0:384], banks, tok, 0, 384, free["tk"])
                    yield
                    e = groups(co, view(tk, 2, 192), view(w1, 2, 192), 192, 2, gains["mla_q_g_2"], (a, gd), fe)
                    if roped:
                        e = rope(co, *(view(v, 2, 192)[:, :, :, 128:192] for v in (tk, w1, w2)), 2, e)
                    yield
                    qf = (fe, dep.get("qfree"))
                    dep["qn", s, c] = t32(co, lambda k, t: tk[:, t, 192 * k:192 * k + 128], 2,
                                               qnt[:, 2 * c:2 * c + 2, :], e, qf)
                    dep["qr", s, c] = t32(co, lambda k, t: tk[:, t, 192 * k + 128:192 * k + 192], 2,
                                               qrt[:, 2 * c:2 * c + 2, :], e, qf)
                    free["tk"] = pe_mark(co)
                flush(co)
                spawn(co, gen())
            return evac

        gemm(co, xt, co.xdep, W, 1536, 448, on_mla)
        gemm(co, xt, co.xdep, W, 512, 512, on_heads("da_k_g_2", dkt, "dk", ks))
        gemm(co, xt, co.xdep, W, 1024, 512, on_dv)
        gemm(co, (ckh, ckl), dep["ck"], A["mla_w_ukv_2"][0], 0, 512, on_kv(0))
        flush(co)
        gemm(co, (ckh, ckl), dep["ck"], A["mla_w_ukv_2"][0], 512, 512, on_kv(1))
        flush(co)
        gemm(co, xt, co.xdep, W, 0, 512, on_heads("da_q_g_2", dqt, "dq", slice(0, 256)))
        co.xtfree = pe_mark(co)
        gemm(co, (cqh, cql), dep["cq"], A["mla_w_uq_2"][0], 0, 384, on_q(0))
        flush(co)
        gemm(co, (cqh, cql), dep["cq"], A["mla_w_uq_2"][0], 384, 384, on_q(1))
        dep["cqfree"] = pe_mark(co)
        flush(co)

    def attend(s, pr, at_, sm, mx, fe, done):
        nk = 512 if s == 0 else 256
        ns = nk // P
        streams = (1, 0) if s == 0 else (1,)
        y = co.y
        kdep = tuple(v for k, v in dep.items() if isinstance(k, tuple) and k[0] in ("dk", "dv", "kn", "kr", "mv")
                     and k[1] in streams)
        qdep = tuple(v for k, v in dep.items() if isinstance(k, tuple) and k[0] in ("dq", "qn", "qr")
                     and k[1] == s)
        pfree, afree, smfree = [fe, fe], [fe, fe], [fe, fe]
        items = [(t, h) for t in range(2) for h in range(8)]
        yb = {}
        st = {}
        rdep = {}
        for i in range(len(items) + 2):
            if i < len(items):
                t, h = items[i]
                ts_ = slice(t * P, (t + 1) * P)
                p, r = pr[i % 2], i % 2
                es = []
                for j in range(2 if h < 4 else 1):
                    b = next_bank(co)
                    if h < 4:
                        co.pe.wait_ge(kdep, qdep, b.drained)
                        m = co.pe.matmul(b.ap[:, 0:nk], dqt[64 * j:64 * j + 64, h, ts_], dkt[64 * j:64 * j + 64, h, 0:nk], skip_group_check=True, start=True, stop=True).then_inc(co.s_pe)
                        sc = 64 ** -0.5
                    else:
                        co.pe.wait_ge(kdep, qdep, b.drained)
                        co.pe.matmul(b.ap[:, 0:nk], qnt[:, h - 4, ts_], knt[:, h - 4, 0:nk], stop=False, skip_group_check=True, start=True)
                        m = co.pe.matmul(b.ap[:, 0:nk], qrt[:, h - 4, ts_], krt[:, 0:nk], start=False, skip_group_check=True, stop=True).then_inc(co.s_pe)
                        sc = 192 ** -0.5
                    co.dv.wait_ge(m, smfree[r])
                    a = co.dv.tensor_reduce(mx[:, r, j:j + 1], b.ap[:, 0:nk], AX, ALU.max).then_inc(co.s_dv)
                    co.dv.wait_ge(a)
                    a = co.dv.tensor_scalar(mx[:, r, j:j + 1], mx[:, r, j:j + 1], -sc, None, ALU.mult).then_inc(co.s_dv)
                    acc = sm[:, t, h - 4:h - 3] if h >= 4 else mx[:, r, 2 + j:3 + j]
                    co.ac.wait_ge(a, pfree[r])
                    b.drained = co.ac.activation(p[:, j, 0:nk], b.ap[:, 0:nk], ACT.Exp, scale=sc, bias=mx[:, r, j:j + 1], accum_out=acc).then_inc(co.s_ac)
                    es.append(b.drained)
                st[i] = tuple(es)
            if 1 <= i <= len(items):
                t, h = items[i - 1]
                r = (i - 1) % 2
                p, es = pr[r], st[i - 1]
                if h < 4:
                    co.dv.wait_ge(es)
                    a = co.dv.reciprocal(mx[:, r, 2:4], mx[:, r, 2:4]).then_inc(co.s_dv)
                    co.dv.wait_ge(a, lamd)
                    a = co.dv.tensor_scalar(mx[:, r, 3:4], mx[:, r, 3:4], lam[:, 2:3], None, ALU.mult).then_inc(co.s_dv)
                    co.dv.wait_ge(a)
                    b = co.dv.tensor_scalar(p[:, 0, 0:nk], p[:, 0, 0:nk], mx[:, r, 2:3], None, ALU.mult).then_inc(co.s_dv)
                    co.dv.wait_ge(b)
                    a = co.dv.scalar_tensor_tensor(p[:, 0, 0:nk], p[:, 1, 0:nk], mx[:, r, 3:4], p[:, 0, 0:nk], ALU.mult, ALU.add).then_inc(co.s_dv)
                    es = a
                b = next_bank(co)
                co.pe.wait_ge(es, b.drained)
                for k in range(ns):
                    m = co.pe.transpose(b.ap[:, k * P:(k + 1) * P], p[:, 0, k * P:(k + 1) * P], ident(co, p[:, 0, k * P:(k + 1) * P])).then_inc(co.s_pe, k == ns - 1)
                pfree[r] = m
                smfree[r] = (m, es)
                co.ac.wait_ge(m, afree[r])
                b.drained = co.ac.activation(at_[r][:, 0:ns, :], b.ap[:, 0:nk].rearrange("p (k n) -> p k n", n=P), ACT.Copy).then_inc(co.s_ac)
                st[i - 1] = b.drained
            yield
            if i >= 2:
                t, h = items[i - 2]
                r = i % 2
                if h % 4 == 0:
                    yb[h // 4] = next_bank(co, hold=True)
                b = yb[h // 4]
                v = dv if h < 4 else mv
                hh = h % 4
                co.pe.wait_ge(st[i - 2], b.drained)
                for k in range(ns):
                    m = co.pe.matmul(b.ap[:, hh * P:(hh + 1) * P], at_[r][:, k, :], v[:, k, hh * P:(hh + 1) * P], start=k == 0, stop=k == ns - 1, skip_group_check=True).then_inc(co.s_pe, k == ns - 1)
                afree[r] = m
                if h == 3:
                    o = y[:, t, 0:512]
                    co.ac.wait_ge(m, co.yfree)
                    b.drained = a = co.ac.activation(o, b.ap, ACT.Copy).then_inc(co.s_ac)
                    b.held = False
                    ov = y[:, t:t + 1, 0:512].rearrange("p t (g n) -> p t g n", n=P)
                    wv = co.gb[:, 0:512].unsqueeze(1).rearrange("p t (g n) -> p t g n", n=P)
                    a = groups(co, ov, wv, 128, 4, gains["da_out_g_2"], (a, gd), co.gbfree)
                    co.gbfree = a
                    done.append(a)
                if h == 7:
                    co.dv.wait_ge(m)
                    a = co.dv.reciprocal(sm[:, t, :], sm[:, t, :]).then_inc(co.s_dv)
                    co.dv.wait_ge(a, co.yfree)
                    b.drained = a = co.dv.tensor_tensor(y[:, t, 512:1024].rearrange("p (g n) -> p g n", n=P), b.ap.rearrange("p (g n) -> p g n", n=P), sm[:, t, :].unsqueeze(2).to_broadcast([P, 4, P]), ALU.mult).then_inc(co.s_dv)
                    b.held = False
                    done.append(a)
        dep["qfree"] = pe_mark(co)

    for s in (1, 0):
        spawn(co, prenorm(co, l, s, 0))
        flush(co)
        fe = counts(co)
        free["tk"] = fe
        project(s)
        mark = co.base
        co.base = low
        pr = [alloc(co, [P, 2, 512]) for _ in range(2)]
        at_ = [alloc(co, [P, 4, P]) for _ in range(2)]
        sm, mx = alloc(co, [P, 2, 4]), alloc(co, [P, 2, 4])
        fa = counts(co)
        done = []
        spawn(co, attend(s, pr, at_, sm, mx, fa, done))
        flush(co)
        co.base = mark
        out_proj(co, l, s, tuple(done))
    co.base = start


def rpb_scratch(co):
    A = co.A
    mark = co.base
    z = alloc(co, [P, 1792])
    fe = counts(co)
    co.dv.wait_ge(fe)
    a = co.dv.memset(z[:, :], 0.0).then_inc(co.s_dv)
    flat = A["na"].rearrange("c r h w -> (c r h w)").rearrange("(q p n) -> q p n", p=P, n=1792)
    co.po.wait_ge(a)
    d = tuple(load_small(co, flat[q], z[:, :]) for q in range(4))
    out = []
    for r in range(7):
        src = A["na_rpb_2"][0, :, r + 4, :]
        src = bass.AP(tensor=src.tensor, offset=src.offset, ap=[[0, 64]] + [list(v) for v in src.ap])
        co.po.wait_ge(d)
        out.append(load_small(co, A["na"][:, r, :, 48:79], src))
    co.nadep = tuple(out)
    co.nafree = d
    co.base = mark


def odd(co):
    A, l = co.A, 1
    start = co.base
    W = A["od_w_in_2"][0]
    kt, v, qt = alloc(co, [P, 8, 512]), alloc(co, [P, 4, D]), alloc(co, [P, 8, 256])
    co.gs = alloc(co, [P, 2, 32])
    gn = alloc(co, [P, 2, 64])
    low = co.base
    tk, w1 = alloc(co, [P, 2, 512]), alloc(co, [P, 2, 512])
    fe = counts(co)
    co.gsfree = fe
    co.po.wait_ge(fe)
    gd = (load_small(co, gn[:, 0, :], A["na_q_g_2"].to_broadcast([P, 64])),
          load_small(co, gn[:, 1, :], A["na_k_g_2"].to_broadcast([P, 64])))
    free = {"tk": fe}
    dep = {"k": [], "v": [], "q": []}

    def on_heads(which, dst, c, cols):
        def evac(banks, tok):
            def gen():
                a = pair(co, tk[:, :, :], banks, tok, 0, 512, free["tk"])
                yield
                f = lambda t: t[:, :, :].rearrange("p t (g n) -> p t g n", n=64)
                a = groups(co, f(tk), f(w1), 64, 8, gn[:, which, :], (a, gd), fe)
                yield
                dep["qk"[which]].append(t32(co, lambda k, t: tk[:, t, k * P:(k + 1) * P], 4,
                                                 dst[:, 4 * c:4 * c + 4, cols], a, fe))
                free["tk"] = pe_mark(co)
            flush(co)
            spawn(co, gen())
        return evac

    def on_v(c, s0):
        def evac(banks, tok):
            for t in range(2):
                q = co.ac if t else co.dv
                q.wait_ge(tok, fe)
                banks[t].drained = q.copy(v[:, s0 + t, c * 512:(c + 1) * 512], banks[t].ap).then_inc(co.s_ac if q is co.ac else co.s_dv)
                dep["v"].append(banks[t].drained)
        return evac

    for s in (1, 0):
        spawn(co, prenorm(co, l, s, 0))
        flush(co)
        xt = (co.xh, co.xl)
        for c in range(2):
            gemm(co, xt, co.xdep, W, 1024 + c * 512, 512, on_heads(1, kt, c, slice(256 * s, 256 * s + 256)))
            gemm(co, xt, co.xdep, W, 2048 + c * 512, 512, on_v(c, 2 * s))
        if s == 0:
            for c in range(2):
                gemm(co, xt, co.xdep, W, c * 512, 512, on_heads(0, qt, c, slice(0, 256)))
        co.xtfree = pe_mark(co)
        flush(co)
    co.base = low
    nb = [alloc(co, [P, 16, 256]) for _ in range(1)]
    pr = [alloc(co, [P, 512]) for _ in range(3)]
    at_ = [alloc(co, [P, 4, P]) for _ in range(2)]
    sm, mx = alloc(co, [P, 2, 16]), alloc(co, [P, 3, 1])
    fa = counts(co)
    nbfree = fa
    kd, done = tuple(dep["k"] + dep["v"] + dep["q"]), []

    def attend():
        nbf = fa
        pfree, afree, mfree = [fa] * 3, [fa] * 2, [fa] * 3
        for t in range(2):
            ld = []
            for r2 in range(2):
                for i in range(4):
                    src = A["na"][:, 3 - (2 * t + r2) + i, :, :]
                    src = bass.AP(tensor=src.tensor, offset=src.offset + 63, ap=[[7 * 16 * P - 1, 64], [P, 16], [1, 64]])
                    co.po.wait_ge(co.nadep, nbf)
                    ld.append(load_small(co, nb[0][64 * r2:64 * r2 + 64, :, 64 * i:64 * i + 64], src))
            o = nb[0][:, :, :]
            na = co.cst[:, C_NA:C_NA + 256].unsqueeze(1).to_broadcast([P, 16, 256])
            co.dv.wait_ge(tuple(ld))
            nd = co.dv.tensor_tensor(o, o, na, ALU.add).then_inc(co.s_dv)
            yb = [next_bank(co, hold=True) for _ in range(2)]
            st = {}
            for i in range(18):
                if i < 16:
                    h, r = i, (16 * t + i) % 3
                    p = pr[r]
                    b = next_bank(co)
                    rr = slice(64 * (h % 2), 64 * (h % 2) + 64)
                    co.pe.wait_ge(kd, b.drained)
                    m = co.pe.matmul(b.ap, qt[rr, h // 2, t * P:(t + 1) * P], kt[rr, h // 2, :], skip_group_check=True, start=True, stop=True).then_inc(co.s_pe)
                    co.dv.wait_ge(m, nd, pfree[r])
                    a = co.dv.scalar_tensor_tensor(p[:, 0:256], b.ap[:, 0:256], 0.125, nb[0][:, h, :], ALU.mult, ALU.add).then_inc(co.s_dv)
                    co.ac.wait_ge(a, pfree[r])
                    c = co.ac.activation(p[:, 256:512], b.ap[:, 256:512], ACT.Copy, scale=0.125).then_inc(co.s_ac)
                    b.drained = (a, c)
                    co.dv.wait_ge(a, c, mfree[r])
                    a = co.dv.tensor_reduce(mx[:, r, :], p[:, :], AX, ALU.max).then_inc(co.s_dv)
                    co.dv.wait_ge(a)
                    a = co.dv.tensor_scalar(mx[:, r, :], mx[:, r, :], -1.0, None, ALU.mult).then_inc(co.s_dv)
                    co.ac.wait_ge(a, fa)
                    st[i] = mfree[r] = co.ac.activation(p[:, :], p[:, :], ACT.Exp, bias=mx[:, r, :], accum_out=sm[:, t, h:h + 1]).then_inc(co.s_ac)
                if 1 <= i <= 16:
                    h, r = i - 1, (16 * t + i - 1) % 3
                    p, q = pr[r], (i - 1) % 2
                    b = next_bank(co)
                    co.pe.wait_ge(st[h], b.drained)
                    for k in range(4):
                        m = co.pe.transpose(b.ap[:, k * P:(k + 1) * P], p[:, k * P:(k + 1) * P], ident(co, p[:, k * P:(k + 1) * P])).then_inc(co.s_pe, k == 3)
                    pfree[r] = m
                    co.ac.wait_ge(m, afree[q])
                    b.drained = co.ac.activation(at_[q][:, :, :], b.ap.rearrange("p (k n) -> p k n", n=P), ACT.Copy).then_inc(co.s_ac)
                    st[h] = b.drained
                yield
                if i >= 2:
                    h, q = i - 2, i % 2
                    b = yb[h // 8]
                    co.pe.wait_ge(st[h], b.drained)
                    for k in range(4):
                        m = co.pe.matmul(b.ap[:, (h % 8) * 64:(h % 8 + 1) * 64], at_[q][:, k, :], v[:, k, h * 64:(h + 1) * 64], start=k == 0, stop=k == 3, skip_group_check=True).then_inc(co.s_pe, k == 3)
                    afree[q] = m
            nbf = a
            co.dv.wait_ge(m)
            a = co.dv.reciprocal(sm[:, t, :], sm[:, t, :]).then_inc(co.s_dv)
            co.dv.wait_ge(a, co.yfree)
            for c in range(2):
                yb[c].drained = e = co.dv.tensor_tensor(co.y[:, t, c * 512:(c + 1) * 512].rearrange("p (g n) -> p g n", n=64), yb[c].ap.rearrange("p (g n) -> p g n", n=64), sm[:, t, 8 * c:8 * c + 8].unsqueeze(2).to_broadcast([P, 8, 64]), ALU.mult).then_inc(co.s_dv)
                yb[c].held = False
                done.append(e)
    spawn(co, attend())
    flush(co)
    co.base = start
    out_proj(co, l, 0, tuple(done))


def first_and_second_block(nc, A, out):
    A["t5"] = nc.dram_tensor("t5_rows", [8, P, 512], F32).ap()
    A["na"] = nc.dram_tensor("rpb_rows", [64, 7, 16, P], F32).ap()
    with ExitStack() as ctx:
        co = new_core(nc, A, ctx, first_plan(A) + second_plan(A))
        setup(co)
        for l in range(2):
            ffn1(co, l, 0, (l, 1))
            mixer(co, l, (l, 2))
            cross(co, l, (l, 3))
            ffn1(co, l, 1, (1, 0) if l == 0 else None)
        flush(co)
        begin(co)
        rpb_scratch(co)
        modulation(co, 0)
        even(co)
        ffn2(co, 0, 1)
        ffn2(co, 0, 0)
        modulation(co, 1)
        odd(co)
        ffn2(co, 1, 0)
        flush(co)
        co.xready = co.ready[0]
        finish_out(co, out)
        emit(co)


_INS = ["x", "mem", "ln_g", "ln_b", "ffn_w_in", "ffn_w_out", "w_mix_in", "b_gate", "kv_norm_g", "w_uk", "w_uv",
        "conv_w", "w_branch", "w_mix_out", "xa_wq", "xa_wkv", "xa_wo", "rel_bias", "c_2", "ctx_2", "c_ctx_2",
        "mod_w_2", "mod_b_2", "norm_mix_g_2", "norm_ffn_g_2", "w_out_2", "ffn_w_in_2", "ffn_w_out_2", "ev_w_in_2",
        "da_q_g_2", "da_k_g_2", "da_lq1_2", "da_lk1_2", "da_lq2_2", "da_lk2_2", "da_out_g_2", "mla_q_a_g_2",
        "mla_w_uq_2", "mla_kv_a_g_2", "mla_w_ukv_2", "mla_q_g_2", "mla_k_g_2", "mla_kr_g_2", "od_w_in_2",
        "na_q_g_2", "na_k_g_2", "na_rpb_2"]


def kernel(**inputs):
    import concourse.bacc as _bacc
    from concourse.bass_utils import run_bass_kernel_spmd as _run

    nc = _bacc.Bacc("TRN2", target_bir_lowering=False, num_devices=1)
    arrays, aps = {}, {}
    given = {n: np.ascontiguousarray(inputs[n]) for n in _INS}
    given["consts"], given["buckets"], given["rope"] = constants(), bucket_table(), rope_table()
    for name, a in given.items():
        arrays[f"in_{name}"] = a
        aps[name] = nc.dram_tensor(f"in_{name}", a.shape, mybir.dt.from_np(a.dtype), kind="ExternalInput").ap()
    out = nc.dram_tensor("out_0", (1, 256, D), F32, kind="ExternalOutput").ap()
    first_and_second_block(nc, aps, out[0])
    r = _run(nc, [arrays], core_ids=[0])
    return r.results[0]["out_0"]
```

```python
from contextlib import ExitStack
import math

import numpy as np

import concourse.bass as bass
from concourse import mybir

F32 = mybir.dt.float32
F32R = mybir.dt.float32r
ALU = mybir.AluOpType
ACT = mybir.ActivationFunctionType
AX = mybir.AxisListType.X
P = 128
HP = [0, 2, 4, 6, 1, 3, 5, 7]
D = 1024
F = 2816
BIG = 1e30
ALPHA = 4 ** 0.25

NRAW, NSPL, AHEAD = 3, 3, 2
UW = 2048

C_ID, C_TRI, C_ONE, C_NEG, C_SM, C_SN, C_HALF, C_S0, C_S1, C_NA, C_END = (
    0, 128, 256, 384, 640, 768, 896, 928, 1056, 1184, 1440)


def constants():
    c = np.zeros((P, C_END), np.float32)
    p = np.arange(P)[:, None]
    c[:, C_ID:C_ID + P] = np.eye(P)
    c[:, C_TRI:C_TRI + P] = p >= np.arange(P)[None]
    c[:, C_ONE:C_ONE + P] = 1
    c[:, C_NEG:C_NEG + 256] = np.where(np.arange(256)[None] > 128 + p, -3e38, 0)
    c[:, C_SM:C_SM + P] = p < np.arange(P)[None]
    c[:, C_SN:C_SN + P] = np.where(p < np.arange(P)[None], 0, -BIG)
    c[:, C_HALF:C_HALF + 32] = -0.5
    c[0, C_S0:C_S0 + P] = 1
    c[64, C_S1:C_S1 + P] = 1
    col = p % 64
    start = np.clip(col - 8, 0, 48)
    w = np.arange(256)[None] % 64
    c[:, C_NA:C_NA + 256] = np.where((w >= start) & (w < start + 16), 0, -BIG)
    return c


def bucket_table():
    n = np.maximum(255 - np.arange(512), 0)
    nf = np.maximum(n, 1).astype(np.float32)
    large = 16 + (np.log(nf / np.float32(16)) / np.float32(math.log(8.0)) * np.float32(16)).astype(np.int32)
    b = np.where(n < 16, n, np.minimum(large, 31))
    return (b[None] == np.arange(32)[:, None]).astype(np.float32)


def rope_table():
    t = np.arange(256)
    inv = (10000.0 ** (-np.arange(0, 32, 2, dtype=np.float32) / np.float32(32))).astype(np.float32)
    ar = (t // 64).astype(np.float32)[:, None] * inv
    ac = (t % 64).astype(np.float32)[:, None] * inv
    out = np.zeros((256, 2, 2, 2, 16), np.float32)
    for a, ang in enumerate((ar, ac)):
        out[:, 0, a, :] = np.cos(ang)[:, None]
        out[:, 1, a, 0] = -np.sin(ang)
        out[:, 1, a, 1] = np.sin(ang)
    return out.reshape(2, 128, 128).transpose(1, 0, 2).copy()


class Count:

    def __init__(self, sem):
        self.sem, self.n = sem, 0

    def mark(self, back=0):
        return (self, self.n - back)


class Step:

    def __init__(self, make):
        self.make, self.inc = make, None

    def then_inc(self, count, when=True, by=1):
        if not when:
            return None
        self.inc = (count.sem, by)
        count.n += by
        return count.mark()

    def play(self, e):
        ins = self.make(e)
        if self.inc:
            ins.then_inc(*self.inc)


class Wait:
    inc = True

    def __init__(self, sem, value):
        self.sem, self.value = sem, value

    def play(self, e):
        e.wait_ge(self.sem, self.value)


class Queue:

    def __init__(self):
        self.steps = []

    def step(self, make):
        self.steps.append(Step(make))
        return self.steps[-1]

    def wait_ge(self, *marks):
        for m in marks:
            if isinstance(m, (list, tuple)) and not (m and isinstance(m[0], Count)):
                self.wait_ge(*m)
            elif m is not None and m[1] > 0:
                self.steps.append(Wait(m[0].sem, m[1]))

    def dma_start(self, out, in_):
        return self.step(lambda e: e.dma_start(out, in_))

    def tensor_tensor(self, out, a, b, op):
        return self.step(lambda e: e.tensor_tensor(out, a, b, op))

    def play(self, e):
        for s in self.steps:
            s.play(e)


class VectorQueue(Queue):
    def tensor_scalar(self, out, a, s1, s2, op0, op1=None):
        if op1 is None:
            return self.step(lambda e: e.tensor_scalar(out, a, s1, None, op0))
        return self.step(lambda e: e.tensor_scalar(out, a, s1, s2, op0, op1))

    def scalar_tensor_tensor(self, out, a, s, b, op0, op1):
        return self.step(lambda e: e.scalar_tensor_tensor(out, a, s, b, op0, op1))

    def tensor_copy(self, out, a):
        return self.step(lambda e: e.tensor_copy(out, a))

    def tensor_reduce(self, out, a, axis, op):
        return self.step(lambda e: e.tensor_reduce(out, a, axis, op))

    def reciprocal(self, out, a):
        return self.step(lambda e: e.reciprocal(out, a))

    def bn_stats(self, out, a):
        return self.step(lambda e: e.bn_stats(out, a))

    def bn_aggr(self, out, a):
        return self.step(lambda e: e.bn_aggr(out, a))

    def max(self, out, a):
        return self.step(lambda e: e.max(out, a))

    def match_replace(self, out, eight, a, v):
        return self.step(lambda e: e.match_replace(out, eight, a, v))

    def memset(self, out, v):
        return self.step(lambda e: e.memset(out, v))

    copy = tensor_copy


class ScalarQueue(Queue):
    def activation(self, out, a, f, **k):
        return self.step(lambda e: e.activation(out, a, f, **k))

    def copy(self, out, a):
        return self.activation(out, a, ACT.Copy)


class TensorQueue(Queue):
    def matmul(self, out, lhs, rhs, **k):
        return self.step(lambda e: e.matmul(out, lhs, rhs, **k))

    def transpose(self, out, a, ident):
        return self.step(lambda e: e.transpose(out, a, ident))


def blocks(w, c0, n, kts=None):
    kts = kts or w.shape[0] // P
    return [(w, k0, min(4, kts - k0), c0, n) for k0 in range(0, kts, 4)]


def same(a, b):
    return a[0].tensor.name == b[0].tensor.name and a[0].offset == b[0].offset and a[1:] == b[1:]


def ffn_blocks(w_in, w_out):
    out = []
    for c in range(0, F, 512):
        n = min(512, F - c)
        out += blocks(w_in, c, n) + blocks(w_in, F + c, n)
    return out + blocks(w_out, 0, 512) + blocks(w_out, 512, 512)


MOD_EARLY = [(l, j) for l in range(2) for j in range(12)][:16]
MOD_LATE = [(1, j) for j in range(4, 12)]


def mod_blocks(A, groups):
    return [b for l, j in groups for b in blocks(A["mod_w_2"][l], j * 512, 512)]


def first_plan(A):
    out = []
    for l in range(2):
        early = MOD_EARLY[8 * l:8 * l + 8]
        out += ffn_blocks(A["ffn_w_in"][l, 0], A["ffn_w_out"][l, 0]) + mod_blocks(A, early[0:2])
        for c, n in [(0, 512), (512, 512), (1024, 200), (3272, 512), (3784, 512), (2760, 512), (1224, 512),
                     (1736, 512), (2248, 512)] + [(4296 + i * 512, 512) for i in range(6)]:
            out += blocks(A["w_mix_in"][l], c, n)
        for i in (0, 2, 1):
            for c in (0, 512):
                out += blocks(A["w_branch"][l, i], c, 512)
        for w in ("w_mix_out", "xa_wkv"):
            for c in (0, 512):
                out += blocks(A[w][l], c, 512)
        out += blocks(A["xa_wq"][l], 0, 512) + mod_blocks(A, early[2:4])
        for c in (0, 512):
            out += blocks(A["xa_wo"][l], c, 512)
        out += mod_blocks(A, early[4:6]) + ffn_blocks(A["ffn_w_in"][l, 1], A["ffn_w_out"][l, 1])
        out += mod_blocks(A, early[6:8])
    return out


def second_plan(A):
    def w_out(l):
        return blocks(A["w_out_2"][l], 0, 512) + blocks(A["w_out_2"][l], 512, 512)

    def ffn(l):
        return ffn_blocks(A["ffn_w_in_2"][l], A["ffn_w_out_2"][l])

    ev, od, ukv, uq = A["ev_w_in_2"][0], A["od_w_in_2"][0], A["mla_w_ukv_2"][0], A["mla_w_uq_2"][0]
    out = []
    for s in range(2):
        out += blocks(ev, 1536, 448) + blocks(ev, 512, 512) + blocks(ev, 1024, 512)
        out += blocks(ukv, 0, 512) + blocks(ukv, 512, 512) + blocks(ev, 0, 512)
        out += blocks(uq, 0, 384) + blocks(uq, 384, 384) + w_out(0)
    out += ffn(0) + ffn(0)
    for s in range(2):
        for c in (0, 512):
            out += blocks(od, 1024 + c, 512) + blocks(od, 2048 + c, 512)
    out += blocks(od, 0, 512) + blocks(od, 512, 512) + mod_blocks(A, MOD_LATE)
    return out + w_out(1) + ffn(1)


class Bank:
    def __init__(self, ap):
        self.ap, self.drained, self.held = ap[:, :], None, False


class Core:
    pass


def new_core(nc, A, ctx, plan):
    co = Core()
    co.nc, co.A, co.ctx, co.plan = nc, A, ctx, plan
    sem = lambda n: Count(ctx.enter_context(nc.semaphore(n)))
    co.pe, co.dv, co.ac, co.po, co.sp = TensorQueue(), VectorQueue(), ScalarQueue(), Queue(), Queue()
    co.s_pe, co.s_dv, co.s_ac, co.s_po = sem("s_pe"), sem("s_dv"), sem("s_ac"), sem("s_po")
    co.s_hi, co.s_lo, co.s_use = sem("s_hi"), sem("s_lo"), sem("s_use")
    co.s_out = sem("s_out")
    co.s_raw = [sem(f"s_raw{i}") for i in range(NRAW)]
    co.s_par = [sem(f"s_par{i}") for i in range(12)]
    co.npar = 0
    co.nuse = 0
    co.bg = []
    co.base = 16512
    co.top = 229344
    co.y = nc.alloc_sbuf_tensor_at("y", [P, 2, D], F32, offset=co.top - 8192)
    co.names = 0
    co.raw = [alloc(co, [P, UW]) for _ in range(NRAW)]
    co.whi = [alloc(co, [P, UW], F32R) for _ in range(NSPL)]
    co.wlo = [alloc(co, [P, UW], F32R) for _ in range(NSPL)]
    co.banks = [Bank(ctx.enter_context(nc.psum_tensor(f"bank{i}", [P, 512], F32))) for i in range(8)]
    co.bi = 0
    for u in range(AHEAD):
        stage(co, u)
    return co




def alloc(co, shape, dt=F32):
    n = 4
    for s in shape[1:]:
        n *= s
    n = (n + 31) // 32 * 32
    co.names += 1
    assert co.base + n <= co.top, (co.base, n, co.top)
    t = co.nc.alloc_sbuf_tensor_at(f"m{co.names}", shape, dt, offset=co.base)
    co.base += n
    return t


def counts(co):
    return (pe_mark(co), co.s_dv.mark(), co.s_ac.mark(), co.s_po.mark(),
            tuple(s.mark() for s in co.s_par if s.n))


def pe_mark(co):
    assert not co.pe.steps or co.pe.steps[-1].inc
    return (co.s_pe.mark(), co.s_use.mark())


def next_bank(co, hold=False):
    while co.banks[co.bi].held:
        co.bi = (co.bi + 1) % 8
    b = co.banks[co.bi]
    co.bi = (co.bi + 1) % 8
    b.held = hold
    return b




def load_small(co, out, in_):
    s = co.s_par[co.npar % len(co.s_par)]
    co.npar += 1
    if s.n:
        co.po.wait_ge(s.mark())
    return co.po.dma_start(out, in_).then_inc(s, by=16)


def ident(co, a):
    n = a.shape[0]
    return co.cst[0:n, C_ID:C_ID + n]


def minus_half(co, v):
    return co.cst[:, C_HALF:C_HALF + v.shape[-1]]




def spawn(co, gen):
    if next(gen, StopIteration) is not StopIteration:
        co.bg.append(gen)


def advance(co):
    co.bg = [g for g in co.bg if next(g, StopIteration) is not StopIteration]


def flush(co):
    while co.bg:
        advance(co)




def slot(co, ring, u, nk, n):
    return ring[u % len(ring)][:, 0:nk * n].rearrange("p (k n) -> p k n", k=nk)


def stage(co, u):
    if u >= len(co.plan):
        return
    w, k0, nk, c0, n = co.plan[u]
    raw, hi, lo = (slot(co, r, u, nk, n) for r in (co.raw, co.whi, co.wlo))
    landed = co.s_raw[u % NRAW]
    if u >= NRAW:
        co.sp.wait_ge((co.s_hi, u - NRAW + 1))
        co.sp.wait_ge((co.s_lo, u - NRAW + 1))
    co.sp.dma_start(raw, w[k0 * P:(k0 + nk) * P, c0:c0 + n].rearrange("(k p) n -> p k n", p=P))\
        .then_inc(landed, by=16)

    co.ac.wait_ge(landed.mark())
    if u >= NSPL:
        co.ac.wait_ge((co.s_use, u - NSPL + 1))
    co.ac.activation(hi, raw, ACT.Copy).then_inc(co.s_hi)

    co.dv.wait_ge(landed.mark())
    co.dv.wait_ge((co.s_hi, u + 1))
    if u >= NSPL:
        co.dv.wait_ge((co.s_use, u - NSPL + 1))
    co.dv.tensor_tensor(lo, raw, hi.bitcast(F32), ALU.subtract).then_inc(co.s_lo)


def gemm(co, xt, xdep, w, c0, n, evac, kt0=0, kts=None, tt=2, quiet=False):
    hi, lo = xt
    kts = kts or w.shape[0] // P
    banks = [next_bank(co, hold=True) for _ in range(tt)]
    per = 4
    done = 0
    while done < kts:
        nk = min(per, kts - done)
        u = co.nuse
        co.nuse += 1
        assert same(co.plan[u], (w, done, nk, c0, n)), u
        stage(co, u + AHEAD)
        wh, wl = slot(co, co.whi, u, nk, n), slot(co, co.wlo, u, nk, n)
        co.pe.wait_ge((co.s_hi, u + 1))
        co.pe.wait_ge((co.s_lo, u + 1))
        co.pe.wait_ge(xdep[done // 2:(done + nk + 1) // 2] if isinstance(xdep, list) else xdep)
        for t in range(tt):
            out = banks[t].ap[:, 0:n]
            co.pe.wait_ge(banks[t].drained)
            for k in range(nk):
                kk = kt0 + done + k
                xh = hi[:, kk, t * P:(t + 1) * P]
                xl = lo[:, kk, t * P:(t + 1) * P]
                first = done == 0 and k == 0
                last = done + k == kts - 1
                co.pe.matmul(out, xh, wh[:, k, :], start=first, stop=False, skip_group_check=True)
                co.pe.matmul(out, xh, wl[:, k, :], start=False, stop=False, skip_group_check=True)
                used = co.pe.matmul(out, xl, wh[:, k, :], start=False, stop=last, skip_group_check=True)\
                    .then_inc(co.s_use, t == tt - 1 and k == nk - 1)
        done += nk
        if not quiet:
            advance(co)
    evac(banks, used)
    for b in banks:
        b.held = False


def finish_out(co, out):
    co.sp.wait_ge(co.xready)
    done = co.sp.dma_start(out.rearrange("(t p) d -> p t d", p=P), co.x[:, :, :]).then_inc(co.s_out, by=16)
    co.sp.wait_ge(done)
    co.sp.wait_ge([s.mark() for s in co.s_par if s.n])


def emit(co):
    block = co.ctx.enter_context(co.nc.Block())

    @block.sync
    def _(e):
        co.sp.play(e)

    @block.scalar
    def _(e):
        co.ac.play(e)

    @block.gpsimd
    def _(e):
        co.po.play(e)

    @block.vector
    def _(e):
        co.dv.play(e)

    @block.tensor
    def _(e):
        co.pe.play(e)




def to_t(co, src, kt, dst, dep, free=None):
    hi, lo = dst
    out = []
    for k0 in range(0, kt, 2):
        nk = min(2, kt - k0)
        b = next_bank(co)
        co.pe.wait_ge(dep, b.drained)
        for k in range(nk):
            for t in range(2):
                tok = co.pe.transpose(b.ap[:, k * 256 + t * P:k * 256 + (t + 1) * P], src(t, k0 + k), ident(co, src(t, k0 + k))).then_inc(co.s_pe, k == nk - 1 and t == 1)
        ps = b.ap[:, 0:nk * 256].rearrange("p (k n) -> p k n", k=nk)
        co.ac.wait_ge(tok, free)
        a = co.ac.activation(hi[:, k0:k0 + nk, :], ps, ACT.Copy).then_inc(co.s_ac)
        co.dv.wait_ge(tok, a, free)
        v = co.dv.tensor_tensor(lo[:, k0:k0 + nk, :], ps, hi[:, k0:k0 + nk, :].bitcast(F32), ALU.subtract).then_inc(co.s_dv)
        b.drained = (a, v)
        out.append((a, v))
    return out


def t32(co, src, n, dst, dep, free=None, scale=1.0):
    toks = []
    for k0 in range(0, n, 2):
        nk = min(2, n - k0)
        b = next_bank(co)
        for k in range(nk):
            for t in range(2):
                s = src(k0 + k, t)
                m = s.shape[-1]
                co.pe.wait_ge(dep, b.drained)
                tok = co.pe.transpose(b.ap[0:m, k * 256 + t * P:k * 256 + (t + 1) * P], s, ident(co, s)).then_inc(co.s_pe, k == nk - 1 and t == 1)
        m = dst.shape[0]
        ps = b.ap[0:m, 0:nk * 256].rearrange("p (k n) -> p k n", k=nk)
        co.ac.wait_ge(tok, free)
        a = co.ac.activation(dst[:, k0:k0 + nk, :], ps, ACT.Copy, scale=scale).then_inc(co.s_ac)
        b.drained = a
        toks.append(a)
    return tuple(toks)


def load_ln(co, l, i, *deps):
    A = co.A
    co.po.wait_ge(deps)
    co.lnpar = (load_small(co, co.lg[:, :], A["ln_g"][l, i:i + 1, :].to_broadcast([P, D])),
                  load_small(co, co.lb[:, :], A["ln_b"][l, i:i + 1, :].to_broadcast([P, D])))


def norm_stats(co, y, t, c, dep):
    co.dv.wait_ge(dep, co.rsfree)
    return co.dv.bn_stats(co.st[:, t, c, :], y[:, t, c * 512:(c + 1) * 512]).then_inc(co.s_dv)


def layer_norm(co, y, ydep, stats, eps, nxt):
    st, mv, rs, par = co.st, co.mv, co.rs, co.lnpar
    norm, cen = [], []
    for t in range(2):
        co.dv.wait_ge(stats[t])
        tok = co.dv.bn_aggr(mv[:, t, :], st[:, t, :, :].rearrange("p c s -> p (c s)")).then_inc(co.s_dv)
        co.dv.wait_ge(tok)
        tok = co.dv.tensor_scalar(rs[:, t, 0:1], mv[:, t, 1:2], eps, None, ALU.add).then_inc(co.s_dv)
        co.po.wait_ge(tok)
        norm.append(co.po.tensor_tensor(rs[:, t, 1:2], rs[:, t, 0:1], minus_half(co, rs[:, t, 0:1]), ALU.pow).then_inc(co.s_po))
        co.dv.wait_ge(tok, ydep[t], par)
        cen.append(co.dv.scalar_tensor_tensor(y[:, t, :], y[:, t, :], mv[:, t, 0:1], co.lg[:, :], ALU.subtract, ALU.mult).then_inc(co.s_dv))
    yield
    out = {}
    co.dv.wait_ge(co.xfree, par)
    for c in range(2):
        for t in range(2):
            cs = slice(c * 512, (c + 1) * 512)
            co.dv.wait_ge(norm[t], cen[t])
            out[t, c] = co.dv.scalar_tensor_tensor(co.x[:, t, cs], y[:, t, cs], rs[:, t, 1:2], co.lb[:, cs], ALU.mult, ALU.add).then_inc(co.s_dv)
    tok = out[1, 1]
    if nxt is not None:
        load_ln(co, nxt[0], nxt[1], tok)
    co.rsfree = tok
    co.xready = (out[0, 1], tok)
    yield
    hi, lo = co.xh, co.xl
    co.xdep = []
    for c in range(2):
        co.xdep += to_t(co, lambda t, k: co.x[:, t, (4 * c + k) * P:(4 * c + k + 1) * P], 4,
                        (hi[:, 4 * c:, :], lo[:, 4 * c:, :]), (out[0, c], out[1, c]), co.xtfree)
    co.xfree = pe_mark(co)


def mod_setup(co):
    A = co.A
    rows, cs = alloc(co, [48, P]), alloc(co, [P, 16])
    d = [load_small(co, rows[0:8, :], A["c_2"][0].rearrange("(k p) -> k p", p=P)),
         load_small(co, rows[8:16, :], A["c_ctx_2"].rearrange("(k p) -> k p", p=P)),
         load_small(co, rows[16:32, :], A["norm_mix_g_2"].rearrange("l (k p) -> (l k) p", p=P)),
         load_small(co, rows[32:48, :], A["norm_ffn_g_2"].rearrange("l (k p) -> (l k) p", p=P))]
    b = next_bank(co)
    co.pe.wait_ge(d, co.cdep, b.drained)
    m = co.pe.transpose(b.ap[:, 0:48], rows[:, :], ident(co, rows[:, :])).then_inc(co.s_pe)
    co.dv.wait_ge(m)
    g = co.dv.tensor_copy(co.gcol[:, :], b.ap[:, 0:48]).then_inc(co.s_dv)
    co.ac.wait_ge(g)
    s = co.ac.activation(cs[:, :], b.ap[:, 0:16], ACT.Silu).then_inc(co.s_ac)
    b.drained = (g, s)
    co.chdep, co.gcdep = [], g
    for i in range(2):
        src = cs[:, 8 * i:8 * i + 8].unsqueeze(2).to_broadcast([P, 8, 64])
        hi, lo = (v[:, :, 64 * i:64 * i + 64] for v in co.chl)
        co.ac.wait_ge(s)
        a = co.ac.activation(hi, src, ACT.Copy).then_inc(co.s_ac)
        co.dv.wait_ge(a)
        co.chdep.append(co.dv.tensor_tensor(lo, src, hi.bitcast(F32), ALU.subtract).then_inc(co.s_dv))
    co.chdep = tuple(co.chdep)


def mod_tiles(co):
    t = [alloc(co, [P, 512]) for _ in range(4)]
    fe = counts(co)
    return t[0:2], t[2:4], [fe, fe], [fe, fe]


def mod_groups(co, groups, tiles, quiet=True):
    A = co.A
    mb, rt, bfree, rfree = tiles
    for l, j in groups:
        blk, half, i = j // 2, j % 2, j % len(rfree)
        co.po.wait_ge(bfree[i])
        bd = load_small(co, mb[i][:, :], A["mod_b_2"][l:l + 1, j * 512:(j + 1) * 512].to_broadcast([P, 512]))

        def evac(banks, tok):
            co.dv.wait_ge(tok, bd, rfree[i])
            a = co.dv.tensor_tensor(rt[i][:, :], banks[0].ap, mb[i][:, :], ALU.add).then_inc(co.s_dv)
            banks[0].drained = bfree[i] = a
            if blk in (2, 5):
                co.po.wait_ge(a)
                rfree[i] = co.gated_at[l, blk // 3, half] = load_small(
                    co, A["gates"][l, blk // 3, :, half * 512:(half + 1) * 512], rt[i][0:65:64, :])
            else:
                spawn(co, columns(l, blk, half, i, a))

        def columns(l, blk, half, i, a):
            yield
            b = next_bank(co)
            co.pe.wait_ge(a, b.drained)
            for k in range(4):
                m = co.pe.transpose(b.ap[:, k * P:(k + 1) * P], rt[i][:, k * P:(k + 1) * P], ident(co, rt[i][:, k * P:(k + 1) * P])).then_inc(co.s_pe, k == 3)
            rfree[i] = m
            co.dv.wait_ge(m)
            b.drained = co.mcd[l, blk, half] = co.dv.tensor_copy(co.mc[:, l, blk, 4 * half:4 * half + 4, :], b.ap.rearrange("p (k a n) -> p k a n", k=4, a=2)[:, :, :, 0]).then_inc(co.s_dv)

        gemm(co, co.chl, co.chdep, A["mod_w_2"][l], j * 512, 512, evac, tt=1, quiet=quiet)
        if quiet and (l, j) != groups[-1]:
            advance(co)


def mod_gain(co, l, f):
    v = co.mgain[:, l, f, :, :]
    c = 16 + 16 * f + 8 * l
    shift, scale = (co.mcd[l, 3 * f, 0], co.mcd[l, 3 * f, 1]), (co.mcd[l, 3 * f + 1, 0], co.mcd[l, 3 * f + 1, 1])
    co.dv.wait_ge(scale, co.gcdep)
    a = co.dv.tensor_scalar(v, co.mc[:, l, 3 * f + 1, :, :], 1.0, None, ALU.add).then_inc(co.s_dv)
    co.dv.wait_ge(a)
    a = co.dv.tensor_tensor(v, v, co.gcol[:, c:c + 8].unsqueeze(2).to_broadcast([P, 8, 2]), ALU.mult).then_inc(co.s_dv)
    return (a, shift)


def residual(co, y, scale, got, fe):
    def make(c0, n):
        def evac(banks, tok):
            for t in range(2):
                o = y[:, t, c0:c0 + n]
                co.dv.wait_ge(tok, co.xready, fe)
                r = co.dv.scalar_tensor_tensor(o, co.x[:, t, c0:c0 + n], scale, banks[t].ap[:, 0:n], ALU.mult, ALU.add).then_inc(co.s_dv)
                banks[t].drained = r
                got[t] = r
            for t in range(2):
                got[2 + t] = norm_stats(co, y, t, c0 // 512, got[t])
        return evac
    return make


def ffn(co, w_in, w_out, resid):
    xt, xdep = (co.xh, co.xl), co.xdep
    base = co.base
    uh, ul = alloc(co, [P, 22, 256], F32R), alloc(co, [P, 22, 256], F32R)
    sa = alloc(co, [P, 2, 512])
    ut = [alloc(co, [P, 2, 512]) for _ in range(2)]
    fe = counts(co)
    free = {"sa": fe, 0: fe, 1: fe}
    udep = []
    for j in range(6):
        c, n = j * 512, min(512, F - j * 512)
        hold = {}

        def evac_a(banks, tok):
            hold["sa"] = []
            co.ac.wait_ge(tok, free['sa'])
            for t in range(2):
                a = co.ac.activation(sa[:, t, 0:n], banks[t].ap[:, 0:n], ACT.Silu).then_inc(co.s_ac)
                banks[t].drained = a
                hold["sa"].append(a)

        def evac_b(banks, tok):
            spawn(co, rest(banks, tok, j, n, hold["sa"]))

        def rest(banks, tok, j, n, sat):
            u = ut[j % 2]
            co.dv.wait_ge(tok, free[j % 2])
            for t in range(2):
                co.dv.wait_ge(sat[t])
                v = co.dv.tensor_tensor(u[:, t, 0:n], banks[t].ap[:, 0:n], sa[:, t, 0:n], ALU.mult).then_inc(co.s_dv)
                banks[t].drained = v
            free["sa"] = v
            yield
            got = to_t(co, lambda t, k: u[:, t, k * P:(k + 1) * P], n // P,
                            (uh[:, 4 * j:, :], ul[:, 4 * j:, :]), v, fe)
            free[j % 2] = pe_mark(co)
            udep.extend(got)

        gemm(co, xt, xdep, w_in, c, n, evac_a)
        gemm(co, xt, xdep, w_in, F + c, n, evac_b)
    flush(co)
    co.xtfree = pe_mark(co)
    for c in range(2):
        gemm(co, (uh, ul), udep, w_out, c * 512, 512, resid(c * 512, 512))
    co.base = base


"""The first block's sublayers."""


def setup(co):
    A = co.A
    co.cst = alloc(co, [P, C_END])
    co.x = alloc(co, [P, 2, D])
    co.xh, co.xl = alloc(co, [P, 8, 256], F32R), alloc(co, [P, 8, 256], F32R)
    co.st, co.mv, co.rs = alloc(co, [P, 2, 2, 6]), alloc(co, [P, 2, 2]), alloc(co, [P, 2, 2])
    co.chl = (alloc(co, [P, 8, P], F32R), alloc(co, [P, 8, P], F32R))
    co.gcol, co.mc, co.mgain = alloc(co, [P, 48]), alloc(co, [P, 2, 6, 8, 2]), alloc(co, [P, 2, 2, 8, 2])
    co.mcd, co.gated_at = {}, {}
    co.lgbase = co.base
    co.lg, co.lb = alloc(co, [P, D]), alloc(co, [P, D])
    co.xfree = co.rsfree = co.xtfree = None
    cdep = co.cdep = load_small(co, co.cst[:, :], A["consts"][:, :])
    co.xready = load_small(co, co.x[:, :, :], A["x"][0].rearrange("(t p) d -> p t d", p=P))
    load_ln(co, 0, 0)
    co.xdep = to_t(co, lambda t, k: co.x[:, t, k * P:(k + 1) * P], 8, (co.xh, co.xl),
                          (co.xready, cdep))
    mark = co.base
    mod_setup(co)
    e, rb, rep, row = alloc(co, [32, 512]), alloc(co, [32, 8]), alloc(co, [32, 8, P]), alloc(co, [P, 8, 512])
    d = (load_small(co, e[:, :], A["buckets"][:, :]), load_small(co, rb[:, :], A["rel_bias"][:, :]))
    outs = []
    co.dv.wait_ge(d, cdep)
    for h in range(8):
        t = co.dv.tensor_scalar(rep[:, h, :], co.cst[0:32, C_ONE:C_ONE + P], rb[:, HP[h]:HP[h] + 1], None, ALU.mult).then_inc(co.s_dv)
        b = next_bank(co)
        co.pe.wait_ge(t, b.drained)
        t = co.pe.matmul(b.ap[:, :], rep[:, h, :], e[:, :], skip_group_check=True, start=True, stop=True).then_inc(co.s_pe)
        co.ac.wait_ge(t)
        b.drained = co.ac.activation(row[:, h, :], b.ap[:, :], ACT.Copy).then_inc(co.s_ac)
        outs.append(b.drained)
    co.po.wait_ge(tuple(outs))
    co.t5 = load_small(co, A["t5"].rearrange("h p s -> p h s"), row[:, :, :])
    co.base = mark


def ffn1(co, l, i, nxt):
    A = co.A
    flush(co)
    w = 0 if i == 0 else 1
    mark = co.base
    got = [None] * 4
    y = co.y
    mt = mod_tiles(co)
    fe = counts(co)
    if (l, i) == (0, 1):
        rpb_scratch(co)
    ffn(co, A["ffn_w_in"][l, w], A["ffn_w_out"][l, w], residual(co, y, 2 * ALPHA, got, fe))
    spawn(co, layer_norm(co, y, got[0:2], got[2:4], 4e-5, nxt))
    mod_groups(co, MOD_EARLY[8 * l + (6 if i else 0):][:2], mt)
    co.base = mark


def pair(co, dst, banks, tok, a, n, *deps):
    co.ac.wait_ge(tok, deps)
    t0 = co.ac.activation(dst[:, 0, :], banks[0].ap[:, a:a + n], ACT.Copy).then_inc(co.s_ac)
    co.dv.wait_ge(tok, deps)
    t1 = co.dv.tensor_copy(dst[:, 1, :], banks[1].ap[:, a:a + n]).then_inc(co.s_dv)
    banks[0].drained, banks[1].drained = (banks[0].drained, t0), (banks[1].drained, t1)
    return (t0, t1)


def mixer(co, l, nxt):
    A = co.A
    flush(co)
    w = A["w_mix_in"][l]
    xt = (co.xh, co.xl)
    start = co.base
    yt = {i: (alloc(co, [P, 4, 256], F32R), alloc(co, [P, 4, 256], F32R)) for i in (0, 2)}
    tk = [alloc(co, [P, 2, 512]) for _ in range(2)]
    fe = counts(co)
    tkfree = [fe, fe]
    ydep = {}
    turn = [0]

    def tokens_of(banks, tok, n, then):
        i = turn[0] % 2
        turn[0] += 1

        def gen():
            s = pair(co, tk[i][:, :, 0:n], banks, tok, 0, n, tkfree[i])
            yield
            tkfree[i] = then(tk[i], s)
        spawn(co, gen())

    qst, kst, vs = alloc(co, [P, 4, 256]), alloc(co, [P, 4, 256]), alloc(co, [P, 2, 512])
    low = co.base
    qat, iqt, ikt = alloc(co, [P, 4, 256]), alloc(co, [P, 4, 256]), alloc(co, [P, 1, 256])
    ckv, ckvt, iw = alloc(co, [P, 2, P]), alloc(co, [P, 1, 256]), alloc(co, [P, 2, 8])
    ik2, kvg, sq, ss = alloc(co, [P, 2, P]), alloc(co, [P, P]), alloc(co, [P, P]), alloc(co, [P, 2, 2])
    wuk, wuv = alloc(co, [P, 4, P]), alloc(co, [P, 8, 64])
    b1, L, pt, olt, qlt = (alloc(co, [P, 8, 256]), alloc(co, [P, 8, 256]), alloc(co, [P, 2, 4, P]),
                           alloc(co, [P, 4, P]), alloc(co, [P, 8, P]))
    sc, m8, mx, sm = alloc(co, [P, 2, 256]), alloc(co, [P, 8]), alloc(co, [P, 8]), alloc(co, [P, 2, 8])
    ya = co.lg[:, :].rearrange("p (t n) -> p t n", t=2)
    conv_y = co.lb[:, :].rearrange("p (k n) -> p k n", k=4)
    zt = alloc(co, [P, 4, 258])
    cw = alloc(co, [12, P])
    cwt = alloc(co, [P, 12])
    dep = {}
    co.po.wait_ge(fe)
    dep["w"] = (load_small(co, wuk[:, :, :], A["w_uk"][l].rearrange("(a b) d c -> (b d) a c", b=2)),
                load_small(co, wuv[:, :, :], A["w_uv"][l].rearrange("h c d -> c h d")),
                load_small(co, kvg[:, :], A["kv_norm_g"][l:l + 1, :].to_broadcast([P, P])),
                load_small(co, cw[:, :], A["conv_w"][l].rearrange("w (k p) -> (w k) p", p=P)))
    skew = bass.AP(tensor=A["t5"].tensor, offset=A["t5"].offset + 127, ap=[[511, P], [P * 512, 8], [1, 256]])
    co.po.wait_ge(fe, co.t5)
    dep["b1"] = load_small(co, b1[:, :, :], skew)

    def on_qa(s, tok):
        dep["qa"] = t32(co, lambda k, t: s[:, t, k * P:(k + 1) * P], 4, qat[:, :, :], tok, fe)
        return pe_mark(co)

    def on_mid(s, tok):
        dep["iq0"] = t32(co, lambda k, t: s[:, t, P + k * P:P + (k + 1) * P], 3, iqt[:, :, :], tok, fe)
        p = pe_mark(co)
        done = []
        co.ac.wait_ge(tok, fe)
        for t in range(2):
            co.ac.wait_ge(done)
            a = co.ac.activation(sq[:, :], s[:, t, 0:P], ACT.Square, accum_out=ss[:, t, 0:1]).then_inc(co.s_ac)
            done = a
            co.dv.wait_ge(a)
            a = co.dv.tensor_scalar(ss[:, t, 0:1], ss[:, t, 0:1], 1.0 / P, 1e-5, ALU.mult, ALU.add).then_inc(co.s_dv)
            co.po.wait_ge(a)
            a = co.po.tensor_tensor(ss[:, t, 1:2], ss[:, t, 0:1], minus_half(co, ss[:, t, 0:1]), ALU.pow).then_inc(co.s_po)
            co.dv.wait_ge(a, dep["w"])
            a = co.dv.scalar_tensor_tensor(ckv[:, t, :], s[:, t, 0:P], ss[:, t, 1:2], kvg[:, :], ALU.mult, ALU.mult).then_inc(co.s_dv)
        dep["ckv"] = a
        return (p, a)

    def on_last(s, tok):
        dep["iq1"] = t32(co, lambda k, t: s[:, t, 0:P], 1, iqt[:, 3:4, :], tok, fe)
        p = pe_mark(co)
        co.dv.wait_ge(tok, fe)
        a = co.dv.tensor_scalar(iw[:, :, :], s[:, :, 192:200], (8 ** -0.5) * (64 ** -0.5), None, ALU.mult).then_inc(co.s_dv)
        co.dv.wait_ge(tok, fe)
        for r in range(2):
            b = co.dv.tensor_copy(ik2[:, :, r * 64:(r + 1) * 64], s[:, :, 128:192]).then_inc(co.s_dv)
        dep["iw"] = a
        dep["ik"] = t32(co, lambda k, t: ik2[:, t, :], 1, ikt[:, :, :], b, fe)
        dep["ckvt"] = t32(co, lambda k, t: ckv[:, t, :], 1, ckvt[:, :, :], dep["ckv"], fe)
        return (p, b)

    def ev(then, n=512):
        return lambda banks, tok: tokens_of(banks, tok, n, then)

    gemm(co, xt, co.xdep, w, 0, 512, ev(on_qa))
    gemm(co, xt, co.xdep, w, 512, 512, ev(on_mid))
    gemm(co, xt, co.xdep, w, 1024, 200, ev(on_last, 200))

    def dsa():
        yield
        yield
        Lfree = scfree = ptfree = olfree = qlfree = smfree = None
        for t in range(2):
            nk = (t + 1) * P
            ts_ = slice(t * P, (t + 1) * P)
            ql = []
            for g in range(2):
                b = next_bank(co)
                co.pe.wait_ge(dep['qa'], dep['w'], b.drained)
                for i in range(4):
                    tok = co.pe.matmul(b.ap[:, i * P:(i + 1) * P], wuk[64 * g:64 * g + 64, i, :], qat[64 * g:64 * g + 64, i, ts_], skip_group_check=True, start=True, stop=True).then_inc(co.s_pe, i == 3)
                co.ac.wait_ge(tok, qlfree, fe)
                b.drained = co.ac.activation(qlt[:, 4 * g:4 * g + 4, :], b.ap.rearrange("p (h n) -> p h n", h=4), ACT.Copy, scale=0.125).then_inc(co.s_ac)
                ql.append(b.drained)
            rel = []
            for g in range(4):
                b = next_bank(co)
                r = slice(64 * (g // 2), 64 * (g // 2) + 64)
                co.pe.wait_ge(dep['iq0'], dep['iq1'], dep['ik'], b.drained)
                for i in range(2):
                    tok = co.pe.matmul(b.ap[:, i * nk:(i + 1) * nk], iqt[r, HP[2 * g + i] // 2, ts_], ikt[r, 0, 0:nk], skip_group_check=True, start=True, stop=True).then_inc(co.s_pe, i == 1)
                co.ac.wait_ge(tok, Lfree, fe)
                b.drained = co.ac.activation(L[:, 2 * g:2 * g + 2, 0:nk], b.ap[:, 0:2 * nk].rearrange("p (h n) -> p h n", h=2), ACT.Relu).then_inc(co.s_ac)
                rel.append(b.drained)
            yield
            neg = co.cst[:, C_NEG + 256 - nk:C_NEG + 256]
            tok = scfree
            co.dv.wait_ge(dep['iw'], fe)
            for h in range(8):
                co.dv.wait_ge(rel[h // 2], tok)
                tok = co.dv.scalar_tensor_tensor(sc[:, 0, 0:nk], L[:, h, 0:nk], iw[:, t, HP[h]:HP[h] + 1], neg if h == 0 else sc[:, 0, 0:nk], ALU.mult, ALU.add).then_inc(co.s_dv)
            yield
            for r in range(8):
                v, o = sc[:, r % 2, 0:nk], sc[:, (r + 1) % 2, 0:nk]
                co.dv.wait_ge(tok)
                tok = co.dv.max(m8[:, :], v).then_inc(co.s_dv)
                co.dv.wait_ge(tok)
                tok = co.dv.match_replace(o, m8[:, :], v, -3.3e38).then_inc(co.s_dv)
                if r == 3:
                    yield
            s0 = sc[:, 0, 0:nk]
            co.dv.wait_ge(tok)
            tok = co.dv.tensor_scalar(s0, s0, -3.2e38, -BIG, ALU.is_gt, ALU.mult).then_inc(co.s_dv)
            co.dv.wait_ge(tok)
            tok = co.dv.tensor_tensor(s0, s0, neg, ALU.min).then_inc(co.s_dv)
            Lv = L[:, :, 0:nk]
            co.dv.wait_ge(tok, dep["b1"], fe)
            tok = co.dv.tensor_tensor(Lv, b1[:, :, 256 - nk:256], s0.unsqueeze(1).to_broadcast([P, 8, nk]), ALU.add).then_inc(co.s_dv)
            yield
            lt = []
            for g in range(4):
                b = next_bank(co)
                co.pe.wait_ge(dep['ckvt'], b.drained)
                for h in (2 * g, 2 * g + 1):
                    co.pe.wait_ge(ql[h // 4])
                    m = co.pe.matmul(b.ap[:, (h % 2) * nk:(h % 2 + 1) * nk], qlt[:, h, :], ckvt[:, 0, 0:nk], skip_group_check=True, start=True, stop=True).then_inc(co.s_pe, h % 2 == 1)
                v = L[:, 2 * g:2 * g + 2, 0:nk]
                co.dv.wait_ge(m, tok)
                b.drained = co.dv.tensor_tensor(v, b.ap[:, 0:2 * nk].rearrange("p (h n) -> p h n", h=2), v, ALU.add).then_inc(co.s_dv)
                lt.append(b.drained)
            qlfree = m
            co.dv.wait_ge(tuple(lt))
            tok = co.dv.tensor_reduce(mx[:, :], Lv, AX, ALU.max).then_inc(co.s_dv)
            co.dv.wait_ge(tok)
            tok = co.dv.tensor_scalar(mx[:, :], mx[:, :], -1.0, None, ALU.mult).then_inc(co.s_dv)
            yield
            es = []
            co.ac.wait_ge(tok, smfree, fe)
            for h in range(8):
                es.append(co.ac.activation(L[:, h, 0:nk], L[:, h, 0:nk], ACT.Exp, bias=mx[:, h:h + 1], accum_out=sm[:, t, h:h + 1]).then_inc(co.s_ac))
            co.dv.wait_ge(tuple(es))
            rc = co.dv.reciprocal(sm[:, t, :], sm[:, t, :]).then_inc(co.s_dv)
            yb = next_bank(co, hold=True)
            for g in range(2):
                cps = []
                for s in range(t + 1):
                    b = next_bank(co)
                    co.pe.wait_ge(b.drained)
                    for h in range(4):
                        co.pe.wait_ge(es[4 * g + h])
                        m = co.pe.transpose(b.ap[:, h * P:(h + 1) * P], L[:, 4 * g + h, s * P:(s + 1) * P], ident(co, L[:, 4 * g + h, s * P:(s + 1) * P])).then_inc(co.s_pe, h == 3)
                    o, i = pt[:, s, :, :], b.ap.rearrange("p (h n) -> p h n", h=4)
                    q = co.ac if s == 0 else co.dv
                    q.wait_ge(m, ptfree, fe)
                    b.drained = q.copy(o, i).then_inc(co.s_ac if q is co.ac else co.s_dv)
                    cps.append(b.drained)
                yield
                b = next_bank(co)
                co.pe.wait_ge(dep['ckv'], b.drained)
                for s in range(t + 1):
                    co.pe.wait_ge(cps[s])
                    m = co.pe.matmul(b.ap, ckv[:, s, :], pt[:, s, :, :].rearrange("p h n -> p (h n)"), start=s == 0, stop=s == t, skip_group_check=True).then_inc(co.s_pe, s == t)
                ptfree = m
                co.dv.wait_ge(m, olfree, fe)
                b.drained = c = co.dv.tensor_copy(olt[:, :, :], b.ap.rearrange("p (h n) -> p h n", h=4)).then_inc(co.s_dv)
                yield
                for h in range(4):
                    hh = 4 * g + h
                    co.pe.wait_ge(c, yb.drained, dep["w"])
                    m = co.pe.matmul(yb.ap[:, hh * 64:(hh + 1) * 64], olt[:, h, :], wuv[:, HP[hh], :], skip_group_check=True, start=True, stop=True).then_inc(co.s_pe, h == 3)
                olfree = m
            Lfree = m
            scfree = m
            co.dv.wait_ge(m, rc, fe)
            for g in range(2):
                yb.drained = co.dv.tensor_tensor(ya[:, t, :].rearrange("p (a b d) -> p b a d", a=4, b=2)[:, g], yb.ap.rearrange("p (b a d) -> p b a d", a=4, b=2)[:, g], sm[:, t, 4 * g:4 * g + 4].unsqueeze(2).to_broadcast([P, 4, 64]), ALU.mult).then_inc(co.s_dv)
            yb.held = False
            dep[f"ya{t}"] = yb.drained
            yield
        ydep[0] = to_t(co, lambda t, k: ya[:, t, k * P:(k + 1) * P], 4, yt[0], (dep["ya0"], dep["ya1"]), fe)

    spawn(co, dsa())

    def on_cc(s, tok):
        dep["cc"] = (s, tok)
        return None

    def conv_z(banks, tok):
        s, ctok = dep["cc"]
        i = turn[0] % 2
        turn[0] += 1
        z = tk[i]

        def gen():
            co.dv.wait_ge(tok, ctok, tkfree[i])
            for t in range(2):
                m = co.dv.tensor_tensor(z[:, t, :], banks[t].ap[:, :], s[:, t, :], ALU.mult).then_inc(co.s_dv)
                banks[t].drained = m
            tkfree[1 - i] = m
            co.dv.wait_ge(fe)
            a = co.dv.memset(zt[:, :, 0:2], 0.0).then_inc(co.s_dv)
            yield
            got = t32(co, lambda k, t: z[:, t, k * P:(k + 1) * P], 4, zt[:, :, 2:258], m, fe)
            tkfree[i] = pe_mark(co)
            b = next_bank(co)
            co.pe.wait_ge(dep["w"], b.drained)
            m = co.pe.transpose(b.ap[:, 0:12], cw[:, :], ident(co, cw[:, :])).then_inc(co.s_pe)
            co.dv.wait_ge(m, fe)
            b.drained = m = co.dv.tensor_copy(cwt[:, :], b.ap[:, 0:12]).then_inc(co.s_dv)
            dep["z"] = (got, a, m)
        spawn(co, gen())

    def conv_b(s, tok):
        c = conv_y
        bt = dep["y"]
        hi, lo = yt[2]
        out = []
        for k0 in (0, 2):
            b = next_bank(co)
            co.pe.wait_ge(tok, b.drained)
            for k in (k0, k0 + 1):
                for t in range(2):
                    m = co.pe.transpose(b.ap[:, (k - k0) * 256 + t * P:(k - k0) * 256 + (t + 1) * P], s[:, t, k * P:(k + 1) * P], ident(co, s[:, t, k * P:(k + 1) * P])).then_inc(co.s_pe, t == 1)
            v = c[:, k0:k0 + 2, :]
            co.dv.wait_ge(m, bt)
            b.drained = m = co.dv.tensor_tensor(v, b.ap.rearrange("p (k n) -> p k n", k=2), v, ALU.mult).then_inc(co.s_dv)
            co.ac.wait_ge(m, fe)
            a = co.ac.activation(hi[:, k0:k0 + 2, :], v, ACT.Copy).then_inc(co.s_ac)
            co.dv.wait_ge(a)
            out.append((a, co.dv.tensor_tensor(lo[:, k0:k0 + 2, :], v, hi[:, k0:k0 + 2, :].bitcast(F32), ALU.subtract).then_inc(co.s_dv)))
        ydep[2] = out
        return pe_mark(co)

    def conv():
        yield
        co.dv.wait_ge(dep['z'], fe)
        for k in range(4):
            a = co.dv.tensor_scalar(conv_y[:, k, :], zt[:, k, 2:258], cwt[:, 8 + k:9 + k], None, ALU.mult).then_inc(co.s_dv)
            co.dv.wait_ge(a)
            a = co.dv.scalar_tensor_tensor(conv_y[:, k, :], zt[:, k, 1:257], cwt[:, 4 + k:5 + k], conv_y[:, k, :], ALU.mult, ALU.add).then_inc(co.s_dv)
            co.dv.wait_ge(a)
            a = co.dv.scalar_tensor_tensor(conv_y[:, k, :], zt[:, k, 0:256], cwt[:, k:k + 1], conv_y[:, k, :], ALU.mult, ALU.add).then_inc(co.s_dv)
        dep["y"] = a

    gemm(co, xt, co.xdep, w, 3272, 512, ev(on_cc))
    gemm(co, xt, co.xdep, w, 3784, 512, conv_z)
    spawn(co, conv())
    gemm(co, xt, co.xdep, w, 2760, 512, ev(conv_b))

    def on_qs(s, tok):
        dep["qs"] = t32(co, lambda k, t: s[:, t, k * P:(k + 1) * P], 4, qst[:, :, :], tok, fe, scale=0.125)
        return pe_mark(co)

    def on_ks(s, tok):
        dep["ks"] = t32(co, lambda k, t: s[:, t, k * P:(k + 1) * P], 4, kst[:, :, :], tok, fe)
        return pe_mark(co)

    def on_vs(banks, tok):
        dep["vs"] = pair(co, vs[:, :, :], banks, tok, 0, 512, fe)

    gemm(co, xt, co.xdep, w, 1224, 512, ev(on_qs))
    gemm(co, xt, co.xdep, w, 1736, 512, ev(on_ks))
    gemm(co, xt, co.xdep, w, 2248, 512, on_vs)
    flush(co)
    co.base = low
    yt[1] = (alloc(co, [P, 4, 256], F32R), alloc(co, [P, 4, 256], F32R))
    sg = alloc(co, [P, 2, 3, D])
    bb = [alloc(co, [P, 512]) for _ in range(2)]
    low = co.base
    fe2 = counts(co)
    zs = [alloc(co, [P, 8, P]) for _ in range(2)]
    sp11, sp0 = alloc(co, [P, 8, P]), alloc(co, [P, 8, P])
    tmp = co.lg[:, :].rearrange("p (t n) -> p t n", t=2)
    cs = co.cst

    def stick():
        sp_done = {}
        zfree = {0: fe2, 1: fe2}
        tfree = {0: fe2, 1: fe2}
        spfree = fe2
        yb = {}
        for i, (s, t) in enumerate(((0, 0), (1, 1), (0, 1))):
            z = zs[i % 2]
            sp = sp11 if (s, t) == (1, 1) else sp0
            toks = []
            for g in range(2):
                b = next_bank(co)
                r = slice(64 * g, 64 * g + 64)
                co.pe.wait_ge(dep['qs'], dep['ks'], b.drained)
                for h in range(4):
                    m = co.pe.matmul(b.ap[:, h * P:(h + 1) * P], kst[r, h, s * P:(s + 1) * P], qst[r, h, t * P:(t + 1) * P], skip_group_check=True, start=True, stop=True).then_inc(co.s_pe, h == 3)
                zg, spg, tg = z[:, 4 * g:4 * g + 4, :], sp[:, 4 * g:4 * g + 4, :], tmp[:, g, :].rearrange(
                    "p (h n) -> p h n", h=4)
                co.ac.wait_ge(m, zfree[i % 2])
                b.drained = c = co.ac.activation(zg, b.ap.rearrange("p (h n) -> p h n", h=4), ACT.Copy).then_inc(co.s_ac)
                co.dv.wait_ge(c, tfree[g])
                a = co.dv.scalar_tensor_tensor(tg, zg, -1.0, zg, ALU.mult, ALU.max).then_inc(co.s_dv)
                co.ac.wait_ge(a)
                a = co.ac.activation(tg, tg, ACT.Exp, scale=-1.0).then_inc(co.s_ac)
                co.ac.wait_ge(a)
                a = co.ac.activation(tg, tg, ACT.Ln, bias=1.0).then_inc(co.s_ac)
                co.dv.wait_ge(a, spfree)
                a = co.dv.scalar_tensor_tensor(spg, zg, 0.0, tg, ALU.max, ALU.add).then_inc(co.s_dv)
                tfree[g] = a
                if s == t:
                    co.dv.wait_ge(a)
                    a = co.dv.tensor_tensor(spg, spg, cs[:, C_SM:C_SM + P].unsqueeze(1).to_broadcast([P, 4, P]), ALU.mult).then_inc(co.s_dv)
                    co.dv.wait_ge(c, a)
                    c = co.dv.tensor_tensor(zg, zg, cs[:, C_SN:C_SN + P].unsqueeze(1).to_broadcast([P, 4, P]), ALU.add).then_inc(co.s_dv)
                toks.append((a, c))
            sp_done[(s, t)] = toks
            yield
            yield
            at = []
            for g in range(2):
                b = next_bank(co)
                f = lambda v: v[:, 4 * g:4 * g + 4, :].rearrange("p h n -> p (h n)")
                co.pe.wait_ge(toks[g], b.drained)
                m = co.pe.matmul(b.ap, cs[:, C_TRI:C_TRI + P], f(sp), stop=s == t, skip_group_check=True, start=True).then_inc(co.s_pe)
                if s != t:
                    co.pe.wait_ge(sp_done[(1, 1)][g])
                    m = co.pe.matmul(b.ap, cs[:, C_ONE:C_ONE + P], f(sp11), start=False, skip_group_check=True, stop=True).then_inc(co.s_pe)
                spfree = m
                zg = z[:, 4 * g:4 * g + 4, :]
                co.dv.wait_ge(m, toks[g])
                b.drained = a = co.dv.tensor_tensor(zg, zg, b.ap.rearrange("p (h n) -> p h n", h=4), ALU.subtract).then_inc(co.s_dv)
                co.ac.wait_ge(a)
                at.append(co.ac.activation(zg, zg, ACT.Exp).then_inc(co.s_ac))
            yield
            if t not in yb:
                yb[t] = next_bank(co, hold=True)
            first = s == t
            last = (s, t) != (1, 1)
            co.pe.wait_ge(dep['vs'], yb[t].drained)
            for h in range(8):
                co.pe.wait_ge(at[h // 4])
                m = co.pe.matmul(yb[t].ap[:, HP[h] * 64:(HP[h] + 1) * 64], z[:, h, :], vs[:, s, HP[h] * 64:(HP[h] + 1) * 64], start=first and h == 0, stop=last, skip_group_check=True).then_inc(co.s_pe, h == 7)
            zfree[i % 2] = m
            if last:
                o = tk[0][:, t, :]
                co.ac.wait_ge(m, tkfree[0])
                yb[t].drained = c = co.ac.activation(o, yb[t].ap, ACT.Copy).then_inc(co.s_ac)
                yb[t].held = False
                dep[f"yb{t}"] = c
            yield
        ydep[1] = to_t(co, lambda t, k: tk[0][:, t, k * P:(k + 1) * P], 4, yt[1], (dep["yb0"], dep["yb1"]), fe2)

    spawn(co, stick())
    bfree = [fe2, fe2]
    sgd = {}
    for i in range(3):
        for c in range(2):
            n = 2 * i + c
            co.po.wait_ge(bfree[n % 2])
            bd = load_small(co, bb[n % 2][:, :], A["b_gate"][l, i:i + 1, c * 512:(c + 1) * 512].to_broadcast([P, 512]))

            def evac(banks, tok):
                for t in range(2):
                    o = sg[:, t, i, c * 512:(c + 1) * 512]
                    co.dv.wait_ge(tok, bd, fe2)
                    banks[t].drained = a = co.dv.tensor_tensor(o, banks[t].ap, bb[n % 2][:, :], ALU.add).then_inc(co.s_dv)
                    co.ac.wait_ge(a)
                    sgd[(i, c, t)] = co.ac.activation(o, o, ACT.Sigmoid).then_inc(co.s_ac)
                bfree[n % 2] = a
            gemm(co, xt, co.xdep, w, 4296 + n * 512, 512, evac)
    flush(co)
    co.xtfree = pe_mark(co)
    co.base = low
    mg, y = alloc(co, [P, 2, D]), co.y
    assert co.base <= co.top - 8192
    fe3 = counts(co)
    load_ln(co, l, 1, fe3)
    mgd = [[None, None], [None, None]]
    for i in (0, 2, 1):
        for c in range(2):
            def evac(banks, tok):
                for t in range(2):
                    s, o = sg[:, t, i, c * 512:(c + 1) * 512], mg[:, t, c * 512:(c + 1) * 512]
                    co.dv.wait_ge(tok, sgd[(i, c, t)], fe3)
                    a = co.dv.tensor_tensor(o if i == 0 else s, banks[t].ap, s, ALU.mult).then_inc(co.s_dv)
                    banks[t].drained = a
                    if i:
                        co.dv.wait_ge(a, mgd[c][t])
                        a = co.dv.tensor_tensor(o, o, s, ALU.add).then_inc(co.s_dv)
                    mgd[c][t] = a
            gemm(co, yt[i], ydep[i], A["w_branch"][l, i], c * 512, 512, evac)
    mdep = to_t(co, lambda t, k: mg[:, t, k * P:(k + 1) * P], 8, xt, tuple(mgd[0] + mgd[1]), co.xtfree)
    got = [None] * 4
    res = residual(co, y, ALPHA, got, fe3)
    for c in range(2):
        gemm(co, xt, mdep, A["w_mix_out"][l], c * 512, 512, res(c * 512, 512))
    co.xtfree = pe_mark(co)
    spawn(co, layer_norm(co, y, got[0:2], got[2:4], 1e-5, nxt))
    co.base = start


def cross(co, l, nxt):
    A = co.A
    start = co.base
    kt, v = alloc(co, [P, 4, 256]), alloc(co, [P, 2, 512])
    kept = co.base
    mem, mh, ml = alloc(co, [P, 2, D]), alloc(co, [P, 8, 256], F32R), alloc(co, [P, 8, 256], F32R)
    fe = counts(co)
    co.po.wait_ge(fe)
    md = load_small(co, mem[:, :, :], A["mem"][0].rearrange("(t p) d -> p t d", p=P))
    mdep = to_t(co, lambda t, k: mem[:, t, k * P:(k + 1) * P], 8, (mh, ml), md, fe)
    dep = {}
    w = A["xa_wkv"][l]

    def on_k(banks, tok):
        def gen():
            s = pair(co, mem[:, :, 0:512], banks, tok, 0, 512, md, mdep)
            yield
            dep["k"] = t32(co, lambda k, t: mem[:, t, k * P:(k + 1) * P], 4, kt[:, :, :], s, fe)
        spawn(co, gen())

    def on_v(banks, tok):
        dep["v"] = pair(co, v[:, :, :], banks, tok, 0, 512, fe)

    gemm(co, (mh, ml), mdep, w, 0, 512, on_k)
    gemm(co, (mh, ml), mdep, w, 512, 512, on_v)
    flush(co)
    co.base = kept
    qt, L, pt = alloc(co, [P, 4, 256]), alloc(co, [P, 2, 4, 256]), alloc(co, [P, 2, 4, 256])
    q, y, mx, sm = alloc(co, [P, 2, 512]), co.y, alloc(co, [P, 2, 4]), alloc(co, [P, 2, 4])
    mt = mod_tiles(co)
    oh, ol = alloc(co, [P, 4, 256], F32R), alloc(co, [P, 4, 256], F32R)
    fe = counts(co)

    def on_q(banks, tok):
        dep["qs"] = pair(co, q[:, :, :], banks, tok, 0, 512, fe)

    gemm(co, (co.xh, co.xl), co.xdep, A["xa_wq"][l], 0, 512, on_q)
    co.xtfree = pe_mark(co)
    dep["q"] = t32(co, lambda k, t: q[:, t, k * P:(k + 1) * P], 4, qt[:, :, :], dep["qs"], fe)
    cps, nm = {}, {}
    for t in range(2):
        lt = []
        for g in range(2):
            b = next_bank(co)
            co.pe.wait_ge(dep['q'], dep['k'], b.drained)
            for h in (2 * g, 2 * g + 1):
                m = co.pe.matmul(b.ap[:, (h % 2) * 256:(h % 2 + 1) * 256], qt[:, h, t * P:(t + 1) * P], kt[:, h, :], skip_group_check=True, start=True, stop=True).then_inc(co.s_pe, h % 2 == 1)
            co.ac.wait_ge(m, fe)
            b.drained = co.ac.activation(L[:, t, 2 * g:2 * g + 2, :], b.ap.rearrange("p (h n) -> p h n", h=2), ACT.Copy, scale=128 ** -0.5).then_inc(co.s_ac)
            lt.append(b.drained)
        co.dv.wait_ge(tuple(lt))
        a = co.dv.tensor_reduce(mx[:, t, :], L[:, t, :, :], AX, ALU.max).then_inc(co.s_dv)
        co.dv.wait_ge(a)
        a = co.dv.tensor_scalar(mx[:, t, :], mx[:, t, :], -1.0, None, ALU.mult).then_inc(co.s_dv)
        co.ac.wait_ge(a)
        es = [co.ac.activation(L[:, t, h, :], L[:, t, h, :], ACT.Exp, bias=mx[:, t, h:h + 1], accum_out=sm[:, t, h:h + 1]).then_inc(co.s_ac)
              for h in range(4)]
        co.dv.wait_ge(tuple(es))
        a = co.dv.reciprocal(sm[:, t, :], sm[:, t, :]).then_inc(co.s_dv)
        co.dv.wait_ge(a)
        nm[t] = [co.dv.tensor_scalar(L[:, t, h, :], L[:, t, h, :], sm[:, t, h:h + 1], None, ALU.mult).then_inc(co.s_dv) for h in range(4)]
    mod_groups(co, MOD_EARLY[8 * l + 2:][:2], mt)
    for t in range(2):
        for s in range(2):
            b = next_bank(co)
            co.pe.wait_ge(b.drained)
            for h in range(4):
                co.pe.wait_ge(nm[t][h])
                m = co.pe.transpose(b.ap[:, h * P:(h + 1) * P], L[:, t, h, s * P:(s + 1) * P], ident(co, L[:, t, h, s * P:(s + 1) * P])).then_inc(co.s_pe, h == 3)
            q = co.ac if s == 0 else co.dv
            q.wait_ge(m, fe)
            b.drained = q.copy(pt[:, s, :, t * P:(t + 1) * P], b.ap.rearrange("p (h n) -> p h n", h=4)).then_inc(co.s_ac if q is co.ac else co.s_dv)
            cps[(s, t)] = b.drained
    odep = []
    for g in range(2):
        b = next_bank(co)
        co.pe.wait_ge(dep['v'], b.drained)
        for h in (2 * g, 2 * g + 1):
            for s in range(2):
                co.pe.wait_ge(cps[s, 0], cps[s, 1])
                m = co.pe.matmul(b.ap[:, (h % 2) * 256:(h % 2 + 1) * 256], v[:, s, h * P:(h + 1) * P], pt[:, s, h, :], start=s == 0, stop=s == 1, skip_group_check=True).then_inc(co.s_pe, s == 1)
        ps = b.ap.rearrange("p (h n) -> p h n", h=2)
        co.ac.wait_ge(m, fe)
        a = co.ac.activation(oh[:, 2 * g:2 * g + 2, :], ps, ACT.Copy).then_inc(co.s_ac)
        co.dv.wait_ge(m, a)
        c = co.dv.tensor_tensor(ol[:, 2 * g:2 * g + 2, :], ps, oh[:, 2 * g:2 * g + 2, :].bitcast(F32), ALU.subtract).then_inc(co.s_dv)
        b.drained = (a, c)
        odep.append((a, c))
    got = [None] * 4
    res = residual(co, y, ALPHA, got, fe)
    for c in range(2):
        gemm(co, (oh, ol), odep, A["xa_wo"][l], c * 512, 512, res(c * 512, 512))
    spawn(co, layer_norm(co, y, got[0:2], got[2:4], 1e-5, nxt))
    mod_groups(co, MOD_EARLY[8 * l + 4:][:2], mt)
    co.base = start


"""The second block. A stream is one of x and ctx: its tile, when it stands, who read it last."""


def begin(co):
    A = co.A
    co.base = co.lgbase
    co.top -= 8192
    co.ctx_t = alloc(co, [P, 2, D])
    co.gb = alloc(co, [P, D])
    fe = counts(co)
    co.gbfree = fe
    co.yfree = fe
    co.po.wait_ge(fe)
    co.cready = load_small(co, co.ctx_t[:, :, :], A["ctx_2"][0].rearrange("(t p) d -> p t d", p=P))
    co.tile = [co.x, co.ctx_t]
    co.ready = [co.xready, co.cready]


def prenorm(co, l, s, f):
    src, y, rs = co.tile[s], co.y, co.rs
    if s == 1 or l == 1 and f == 1:
        co.gaindep = mod_gain(co, l, f)
    norm = []
    co.ac.wait_ge(co.ready[s], co.yfree, co.rsfree)
    for t in range(2):
        a = co.ac.activation(y[:, t, :], src[:, t, :], ACT.Square, accum_out=rs[:, t, 0:1]).then_inc(co.s_ac)
        co.dv.wait_ge(a)
        a = co.dv.tensor_scalar(rs[:, t, 0:1], rs[:, t, 0:1], 1.0 / D, 1e-6, ALU.mult, ALU.add).then_inc(co.s_dv)
        co.po.wait_ge(a)
        a = co.po.tensor_tensor(rs[:, t, 1:2], rs[:, t, 0:1], minus_half(co, rs[:, t, 0:1]), ALU.pow).then_inc(co.s_po)
        co.dv.wait_ge(a)
        norm.append(co.dv.tensor_scalar(y[:, t, :], src[:, t, :], rs[:, t, 1:2], None, ALU.mult).then_inc(co.s_dv))
    co.rsfree = norm[1]
    yield
    out = []
    hi, lo, tmp = co.xh, co.xl, co.gb
    wfree = [co.gbfree, co.gbfree]
    for k0 in range(0, 8, 2):
        b = next_bank(co)
        co.pe.wait_ge(b.drained)
        for k in (0, 1):
            for t in range(2):
                co.pe.wait_ge(norm[t])
                m = co.pe.transpose(b.ap[:, k * 256 + t * P:k * 256 + (t + 1) * P], y[:, t, (k0 + k) * P:(k0 + k + 1) * P], ident(co, y[:, t, (k0 + k) * P:(k0 + k + 1) * P])).then_inc(co.s_pe, k == 1 and t == 1)
        j = k0 // 2 % 2
        w = tmp[:, 512 * j:512 * j + 512]
        for k in (0, 1):
            sc, sh = co.mgain[:, l, f, k0 + k, s:s + 1], co.mc[:, l, 3 * f, k0 + k, s:s + 1]
            co.dv.wait_ge(m, co.gaindep, wfree[j])
            v = co.dv.tensor_scalar(w[:, k * 256:(k + 1) * 256], b.ap[:, k * 256:(k + 1) * 256], sc, sh, ALU.mult, ALU.add).then_inc(co.s_dv)
        b.drained = v
        w2 = w.rearrange("p (k n) -> p k n", k=2)
        co.ac.wait_ge(v, co.xtfree)
        a = co.ac.activation(hi[:, k0:k0 + 2, :], w2, ACT.Copy).then_inc(co.s_ac)
        co.dv.wait_ge(a, co.xtfree)
        v = co.dv.tensor_tensor(lo[:, k0:k0 + 2, :], w2, hi[:, k0:k0 + 2, :].bitcast(F32), ALU.subtract).then_inc(co.s_dv)
        wfree[j] = v
        out.append(v)
    co.gbfree = v
    co.yfree = pe_mark(co)
    co.xdep = out


def gate_rows(co, l, s, f):
    co.po.wait_ge(co.gated_at[l, f, 0], co.gated_at[l, f, 1], co.gbfree)
    co.gbdep = load_small(co, co.gb[:, :], co.A["gates"][l, f, s:s + 1, :].to_broadcast([P, D]))


def gated(co, s):
    got = []
    x = co.tile[s]

    def make(c0, n):
        def evac(banks, tok):
            for t in range(2):
                g, p = co.gb[:, c0:c0 + n], banks[t].ap[:, 0:n]
                w, o = co.y[:, t, c0:c0 + n], x[:, t, c0:c0 + n]
                co.dv.wait_ge(tok, co.gbdep, co.yfree)
                a = co.dv.tensor_tensor(w, p, g, ALU.mult).then_inc(co.s_dv)
                banks[t].drained = a
                co.dv.wait_ge(a, co.ready[s])
                got.append(co.dv.tensor_tensor(o, o, w, ALU.add).then_inc(co.s_dv))
        return evac
    return make, got


def ffn2(co, l, s):
    A = co.A
    start = co.base
    spawn(co, prenorm(co, l, s, 1))
    flush(co)
    gate_rows(co, l, s, 1)
    make, got = gated(co, s)
    ffn(co, A["ffn_w_in_2"][l], A["ffn_w_out_2"][l], make)
    co.yfree = co.gbfree = tuple(got)
    co.ready[s] = tuple(got)
    co.base = start


def out_proj(co, l, s, ydep):
    flush(co)
    dep = to_t(co, lambda t, k: co.y[:, t, k * P:(k + 1) * P], 8, (co.xh, co.xl), ydep, co.xtfree)
    co.yfree = pe_mark(co)
    gate_rows(co, l, s, 0)
    make, got = gated(co, s)
    for c in range(2):
        gemm(co, (co.xh, co.xl), dep, co.A["w_out_2"][l], c * 512, 512, make(c * 512, 512))
    co.xtfree = pe_mark(co)
    co.yfree = co.gbfree = tuple(got)
    co.ready[s] = tuple(got)


def groups(co, v, w, n, g, gain, dep, wfree):
    a = v.shape[1]
    ss, ss2 = co.gs[:, 0, 0:a * g], co.gs[:, 1, 0:a * g]
    v3 = ss.rearrange("p (a g) -> p a g", a=a)
    co.dv.wait_ge(dep, wfree)
    tok = co.dv.tensor_tensor(w, v, v, ALU.mult).then_inc(co.s_dv)
    co.dv.wait_ge(tok, co.gsfree)
    tok = co.dv.tensor_reduce(v3, w, AX, ALU.add).then_inc(co.s_dv)
    co.dv.wait_ge(tok)
    tok = co.dv.tensor_scalar(ss, ss, 1.0 / n, 1e-6, ALU.mult, ALU.add).then_inc(co.s_dv)
    co.po.wait_ge(tok)
    tok = co.po.tensor_tensor(ss2, ss, minus_half(co, ss), ALU.pow).then_inc(co.s_po)
    r3 = ss2.rearrange("p (a g) -> p a g", a=a)
    co.dv.wait_ge(tok)
    for i in range(a):
        b = co.dv.tensor_tensor(v[:, i], v[:, i], r3[:, i].unsqueeze(2).to_broadcast([P, g, n]), ALU.mult).then_inc(co.s_dv)
        co.dv.wait_ge(b)
        b = co.dv.tensor_tensor(v[:, i], v[:, i], gain.unsqueeze(1).to_broadcast([P, g, n]), ALU.mult).then_inc(co.s_dv)
    co.gsfree = b
    return b


def rope(co, v, w, w2, g, dep):
    for t in range(2):
        c = co.rt[:, t, 0:64].unsqueeze(1).to_broadcast([P, g, 64])
        co.dv.wait_ge(dep)
        a = co.dv.tensor_tensor(w[:, t], v[:, t], c, ALU.mult).then_inc(co.s_dv)
        for h in range(2):
            o = w2[:, t].rearrange("p g (a h n) -> p g a h n", a=2, h=2)[:, :, :, h]
            i = v[:, t].rearrange("p g (a h n) -> p g a h n", a=2, h=2)[:, :, :, 1 - h]
            s = co.rt[:, t, 64:128].rearrange("p (a h n) -> p a h n", a=2, h=2)[:, :, h].unsqueeze(1)\
                .to_broadcast([P, g, 2, 16])
            co.dv.wait_ge(dep)
            b = co.dv.tensor_tensor(o, i, s, ALU.mult).then_inc(co.s_dv)
        co.dv.wait_ge(a, b)
        a = co.dv.tensor_tensor(v[:, t], w[:, t], w2[:, t], ALU.add).then_inc(co.s_dv)
    return a


def even(co):
    A, l = co.A, 0
    start = co.base
    W = A["ev_w_in_2"][0]
    dkt, dv = alloc(co, [P, 4, 512]), alloc(co, [P, 4, 512])
    knt, krt, mv = alloc(co, [P, 4, 512]), alloc(co, [64, 512]), alloc(co, [P, 4, 512])
    dqt, qnt, qrt = alloc(co, [P, 4, 256]), alloc(co, [P, 4, 256]), alloc(co, [64, 4, 256])
    co.rt, co.gs = alloc(co, [P, 2, P]), alloc(co, [P, 2, 32])
    gn = alloc(co, [P, 1152])
    lam = alloc(co, [P, 4])
    low = co.base
    tk, w1, w2 = alloc(co, [P, 2, 512]), alloc(co, [P, 2, 512]), alloc(co, [P, 2, 512])
    cqh, cql = alloc(co, [P, 2, 256], F32R), alloc(co, [P, 2, 256], F32R)
    ckh, ckl = alloc(co, [P, 1, 256], F32R), alloc(co, [P, 1, 256], F32R)
    lv = alloc(co, [P, 4, 64])
    fe = counts(co)
    co.gsfree = fe
    spawn(co, prenorm(co, l, 1, 0))
    co.po.wait_ge(fe)
    gd, at = [load_small(co, co.rt[:, :, :], A["rope"][:, :, :])], 0
    gains = {}
    for n, w in (("da_q_g_2", 64), ("da_k_g_2", 64), ("mla_q_a_g_2", 256), ("mla_kv_a_g_2", 128),
                 ("mla_q_g_2", 192), ("mla_k_g_2", 128), ("mla_kr_g_2", 64), ("da_out_g_2", 128)):
        gains[n] = gn[:, at:at + w]
        co.po.wait_ge(fe)
        gd.append(load_small(co, gn[:, at:at + w], A[n].to_broadcast([P, w])))
        at += w
    co.po.wait_ge(fe)
    for i, n in enumerate(("da_lq1_2", "da_lk1_2", "da_lq2_2", "da_lk2_2")):
        gd.append(load_small(co, lv[:, i, :], A[n].to_broadcast([P, 64])))
    gd = tuple(gd)
    free = {"tk": fe}
    dep = {}

    def view(v, n, w):
        return v[:, :, 0:n * w].rearrange("p t (g n) -> p t g n", n=w)

    def project(s):
        xt = (co.xh, co.xl)
        roped = s == 0
        k0 = 256 if s == 0 else 0
        ks = slice(k0, k0 + 256)
        kfree = None if s == 1 else ()

        def on_heads(gname, dst, key, cols):
            def evac(banks, tok):
                def gen():
                    a = pair(co, tk[:, :, :], banks, tok, 0, 512, free["tk"])
                    yield
                    a = groups(co, view(tk, 8, 64), view(w1, 8, 64), 64, 8, gains[gname], (a, gd), fe)
                    if roped:
                        a = rope(co, view(tk, 8, 64), view(w1, 8, 64), view(w2, 8, 64), 8, a)
                    yield
                    dep[key, s] = t32(co, lambda k, t: tk[:, t, k * P:(k + 1) * P], 4, dst[:, :, cols], a,
                                           (fe, dep.get("qfree")))
                    free["tk"] = pe_mark(co)
                flush(co)
                spawn(co, gen())
            return evac

        def on_dv(banks, tok):
            for t in range(2):
                o = dv[:, k0 // P + t, :]
                q = co.ac if t else co.dv
                q.wait_ge(tok, fe)
                banks[t].drained = q.copy(o, banks[t].ap).then_inc(co.s_ac if q is co.ac else co.s_dv)
                dep["dv", s, t] = banks[t].drained

        def on_mla(banks, tok):
            def gen():
                a = pair(co, tk[:, :, 0:448], banks, tok, 0, 448, free["tk"])
                yield
                c = groups(co, tk[:, :, 0:256].unsqueeze(2), w1[:, :, 0:256].unsqueeze(2), 256, 1,
                                gains["mla_q_a_g_2"], (a, gd), fe)
                d = groups(co, tk[:, :, 256:384].unsqueeze(2), w1[:, :, 256:384].unsqueeze(2), 128, 1,
                                gains["mla_kv_a_g_2"], (a, gd), fe)
                kr = tk[:, :, 384:448].unsqueeze(2)
                e = groups(co, kr, w1[:, :, 384:448].unsqueeze(2), 64, 1, gains["mla_kr_g_2"], (a, gd), fe)
                if roped:
                    e = rope(co, kr, w1[:, :, 384:448].unsqueeze(2), w2[:, :, 384:448].unsqueeze(2), 1, e)
                yield
                dep["cq"] = to_t(co, lambda t, k: tk[:, t, k * P:(k + 1) * P], 2, (cqh, cql), c,
                                      (fe, dep.get("cqfree")))
                dep["ck"] = to_t(co, lambda t, k: tk[:, t, 256:384], 1, (ckh, ckl), d, (fe, dep.get("cqfree")))
                dep["kr", s] = t32(co, lambda k, t: tk[:, t, 384:448], 1, krt[:, ks].unsqueeze(1), e, fe)
                free["tk"] = pe_mark(co)
            flush(co)
            spawn(co, gen())

        def on_kv(c):
            def evac(banks, tok):
                def gen():
                    a = pair(co, tk[:, :, :], banks, tok, 0, 512, free["tk"])
                    yield
                    kn = tk[:, :, :].rearrange("p t (g n) -> p t g n", n=256)[:, :, :, 0:128]
                    k1 = w1[:, :, :].rearrange("p t (g n) -> p t g n", n=256)[:, :, :, 0:128]
                    e = groups(co, kn, k1, 128, 2, gains["mla_k_g_2"], (a, gd), fe)
                    for t in range(2):
                        v = tk[:, t, :].rearrange("p (g n) -> p g n", n=256)[:, :, 128:256]
                        o = mv[:, k0 // P + t, 256 * c:256 * c + 256].rearrange("p (g n) -> p g n", n=128)
                        co.ac.wait_ge(a, fe)
                        m = co.ac.activation(o, v, ACT.Copy).then_inc(co.s_ac)
                    dep["mv", s, c] = m
                    yield
                    dep["kn", s, c] = t32(co, lambda k, t: tk[:, t, 256 * k:256 * k + 128], 2,
                                               knt[:, 2 * c:2 * c + 2, ks], e, fe)
                    free["tk"] = (pe_mark(co), m)
                flush(co)
                spawn(co, gen())
            return evac

        def on_q(c):
            def evac(banks, tok):
                def gen():
                    a = pair(co, tk[:, :, 0:384], banks, tok, 0, 384, free["tk"])
                    yield
                    e = groups(co, view(tk, 2, 192), view(w1, 2, 192), 192, 2, gains["mla_q_g_2"], (a, gd), fe)
                    if roped:
                        e = rope(co, *(view(v, 2, 192)[:, :, :, 128:192] for v in (tk, w1, w2)), 2, e)
                    yield
                    qf = (fe, dep.get("qfree"))
                    dep["qn", s, c] = t32(co, lambda k, t: tk[:, t, 192 * k:192 * k + 128], 2,
                                               qnt[:, 2 * c:2 * c + 2, :], e, qf)
                    dep["qr", s, c] = t32(co, lambda k, t: tk[:, t, 192 * k + 128:192 * k + 192], 2,
                                               qrt[:, 2 * c:2 * c + 2, :], e, qf)
                    free["tk"] = pe_mark(co)
                flush(co)
                spawn(co, gen())
            return evac

        gemm(co, xt, co.xdep, W, 1536, 448, on_mla)
        gemm(co, xt, co.xdep, W, 512, 512, on_heads("da_k_g_2", dkt, "dk", ks))
        gemm(co, xt, co.xdep, W, 1024, 512, on_dv)
        gemm(co, (ckh, ckl), dep["ck"], A["mla_w_ukv_2"][0], 0, 512, on_kv(0))
        flush(co)
        gemm(co, (ckh, ckl), dep["ck"], A["mla_w_ukv_2"][0], 512, 512, on_kv(1))
        flush(co)
        gemm(co, xt, co.xdep, W, 0, 512, on_heads("da_q_g_2", dqt, "dq", slice(0, 256)))
        co.xtfree = pe_mark(co)
        gemm(co, (cqh, cql), dep["cq"], A["mla_w_uq_2"][0], 0, 384, on_q(0))
        flush(co)
        gemm(co, (cqh, cql), dep["cq"], A["mla_w_uq_2"][0], 384, 384, on_q(1))
        dep["cqfree"] = pe_mark(co)
        flush(co)

    def lambdas():
        co.dv.wait_ge(gd)
        a = co.dv.tensor_scalar(gains["da_out_g_2"], gains["da_out_g_2"], 1.0 - (0.8 - 0.6 * math.exp(0.0)), None, ALU.mult).then_inc(co.s_dv)
        co.dv.wait_ge(gd)
        for i in range(2):
            a = co.dv.tensor_tensor(lv[:, 2 * i, :], lv[:, 2 * i, :], lv[:, 2 * i + 1, :], ALU.mult).then_inc(co.s_dv)
            co.dv.wait_ge(a, fe)
            a = co.dv.tensor_reduce(lam[:, i:i + 1], lv[:, 2 * i, :], AX, ALU.add).then_inc(co.s_dv)
        co.ac.wait_ge(a)
        a = co.ac.activation(lam[:, 0:2], lam[:, 0:2], ACT.Exp).then_inc(co.s_ac)
        co.dv.wait_ge(a)
        a = co.dv.tensor_tensor(lam[:, 2:3], lam[:, 1:2], lam[:, 0:1], ALU.subtract).then_inc(co.s_dv)
        co.dv.wait_ge(a)
        dep["lam"] = co.dv.tensor_scalar(lam[:, 2:3], lam[:, 2:3], -(0.8 - 0.6 * math.exp(0.0)), None, ALU.add).then_inc(co.s_dv)

    def attend(s, pr, at_, sm, mx, fe, done):
        nk = 512 if s == 0 else 256
        ns = nk // P
        streams = (1, 0) if s == 0 else (1,)
        y = co.y
        kdep = tuple(v for k, v in dep.items() if isinstance(k, tuple) and k[0] in ("dk", "dv", "kn", "kr", "mv")
                     and k[1] in streams)
        qdep = tuple(v for k, v in dep.items() if isinstance(k, tuple) and k[0] in ("dq", "qn", "qr")
                     and k[1] == s)
        pfree, afree, smfree = [fe] * 4, [fe] * 2, [fe] * 4
        items = [(t, h) for t in range(2) for h in range(8)]
        yb = {}
        st = {}
        rdep = {}
        for i in range(len(items) + 3):
            if 2 <= i < len(items) + 2 and items[i - 2][1] < 4:
                r = (i - 2) % 4
                p = pr[r]
                co.dv.wait_ge(st[i - 2])
                a = co.dv.reciprocal(mx[:, r, 2:4], mx[:, r, 2:4]).then_inc(co.s_dv)
                co.dv.wait_ge(a, dep["lam"])
                a = co.dv.tensor_scalar(mx[:, r, 3:4], mx[:, r, 3:4], lam[:, 2:3], None, ALU.mult).then_inc(co.s_dv)
                b = co.dv.tensor_scalar(p[:, 0, 0:nk], p[:, 0, 0:nk], mx[:, r, 2:3], None, ALU.mult).then_inc(co.s_dv)
                co.dv.wait_ge(a, b)
                st[i - 2] = co.dv.scalar_tensor_tensor(p[:, 0, 0:nk], p[:, 1, 0:nk], mx[:, r, 3:4], p[:, 0, 0:nk], ALU.mult, ALU.add).then_inc(co.s_dv)
            scores = []
            if i < len(items):
                t, h = items[i]
                ts_ = slice(t * P, (t + 1) * P)
                for j in range(2 if h < 4 else 1):
                    b = next_bank(co)
                    co.pe.wait_ge(kdep, qdep, b.drained)
                    if h < 4:
                        m = co.pe.matmul(b.ap[:, 0:nk], dqt[64 * j:64 * j + 64, h, ts_], dkt[64 * j:64 * j + 64, h, 0:nk], skip_group_check=True, start=True, stop=True).then_inc(co.s_pe)
                    else:
                        co.pe.matmul(b.ap[:, 0:nk], qnt[:, h - 4, ts_], knt[:, h - 4, 0:nk], stop=False, skip_group_check=True, start=True)
                        m = co.pe.matmul(b.ap[:, 0:nk], qrt[:, h - 4, ts_], krt[:, 0:nk], start=False, skip_group_check=True, stop=True).then_inc(co.s_pe)
                    scores.append((b, m))
            if 2 <= i < len(items) + 2:
                r, q = (i - 2) % 4, i % 2
                p, es = pr[r], st[i - 2]
                b = next_bank(co)
                co.pe.wait_ge(es, b.drained)
                for k in range(ns):
                    m = co.pe.transpose(b.ap[:, k * P:(k + 1) * P], p[:, 0, k * P:(k + 1) * P], ident(co, p[:, 0, k * P:(k + 1) * P])).then_inc(co.s_pe, k == ns - 1)
                pfree[r] = m
                smfree[r] = (m, es)
                co.ac.wait_ge(m, afree[q])
                b.drained = co.ac.activation(at_[q][:, 0:ns, :], b.ap[:, 0:nk].rearrange("p (k n) -> p k n", n=P), ACT.Copy).then_inc(co.s_ac)
                st[i - 2] = b.drained
            if i < len(items):
                t, h = items[i]
                r = i % 4
                p, es = pr[r], []
                sc = 64 ** -0.5 if h < 4 else 192 ** -0.5
                for j, (b, m) in enumerate(scores):
                    co.dv.wait_ge(m, smfree[r])
                    a = co.dv.tensor_reduce(mx[:, r, j:j + 1], b.ap[:, 0:nk], AX, ALU.max).then_inc(co.s_dv)
                    co.dv.wait_ge(a)
                    a = co.dv.tensor_scalar(mx[:, r, j:j + 1], mx[:, r, j:j + 1], -sc, None, ALU.mult).then_inc(co.s_dv)
                    acc = sm[:, t, h - 4:h - 3] if h >= 4 else mx[:, r, 2 + j:3 + j]
                    co.ac.wait_ge(a, pfree[r])
                    b.drained = co.ac.activation(p[:, j, 0:nk], b.ap[:, 0:nk], ACT.Exp, scale=sc, bias=mx[:, r, j:j + 1], accum_out=acc).then_inc(co.s_ac)
                    es.append(b.drained)
                st[i] = tuple(es)
            yield
            if i >= 3:
                t, h = items[i - 3]
                q = (i - 1) % 2
                if h % 4 == 0:
                    yb[h // 4] = next_bank(co, hold=True)
                b = yb[h // 4]
                v = dv if h < 4 else mv
                hh = h % 4
                co.pe.wait_ge(st[i - 3], b.drained)
                for k in range(ns):
                    m = co.pe.matmul(b.ap[:, hh * P:(hh + 1) * P], at_[q][:, k, :], v[:, k, hh * P:(hh + 1) * P], start=k == 0, stop=k == ns - 1, skip_group_check=True).then_inc(co.s_pe, k == ns - 1)
                afree[q] = m
                if h == 3:
                    o = y[:, t, 0:512]
                    co.ac.wait_ge(m, co.yfree)
                    b.drained = a = co.ac.activation(o, b.ap, ACT.Copy).then_inc(co.s_ac)
                    b.held = False
                    ov = y[:, t:t + 1, 0:512].rearrange("p t (g n) -> p t g n", n=P)
                    wv = co.gb[:, 0:512].unsqueeze(1).rearrange("p t (g n) -> p t g n", n=P)
                    a = groups(co, ov, wv, 128, 4, gains["da_out_g_2"], (a, gd), co.gbfree)
                    co.gbfree = a
                    done.append(a)
                if h == 7:
                    co.dv.wait_ge(m)
                    a = co.dv.reciprocal(sm[:, t, :], sm[:, t, :]).then_inc(co.s_dv)
                    co.dv.wait_ge(a, co.yfree)
                    b.drained = a = co.dv.tensor_tensor(y[:, t, 512:1024].rearrange("p (g n) -> p g n", n=P), b.ap.rearrange("p (g n) -> p g n", n=P), sm[:, t, :].unsqueeze(2).to_broadcast([P, 4, P]), ALU.mult).then_inc(co.s_dv)
                    b.held = False
                    done.append(a)
        dep["qfree"] = pe_mark(co)

    for s in (1, 0):
        if s == 0:
            spawn(co, prenorm(co, l, s, 0))
        flush(co)
        fe = counts(co)
        free["tk"] = fe
        project(s)
        if s == 1:
            lambdas()
        mark = co.base
        co.base = low
        pr = [alloc(co, [P, 2, 512]) for _ in range(4)]
        at_ = [alloc(co, [P, 4, P]) for _ in range(2)]
        sm, mx = alloc(co, [P, 2, 4]), alloc(co, [P, 4, 4])
        fa = counts(co)
        done = []
        spawn(co, attend(s, pr, at_, sm, mx, fa, done))
        flush(co)
        co.base = mark
        out_proj(co, l, s, tuple(done))
    co.base = start


def rpb_scratch(co):
    A = co.A
    z = alloc(co, [P, 1792])
    fe = counts(co)
    co.dv.wait_ge(fe)
    a = co.dv.memset(z[:, :], 0.0).then_inc(co.s_dv)
    flat = A["na"].rearrange("c r h w -> (c r h w)").rearrange("(q p n) -> q p n", p=P, n=1792)
    co.po.wait_ge(a)
    d = tuple(load_small(co, flat[q], z[:, :]) for q in range(4))
    out = []
    for r in range(7):
        src = A["na_rpb_2"][0, :, r + 4, :]
        src = bass.AP(tensor=src.tensor, offset=src.offset, ap=[[0, 64]] + [list(v) for v in src.ap])
        co.po.wait_ge(d)
        out.append(load_small(co, A["na"][:, r, :, 48:79], src))
    co.nadep = tuple(out)


def odd(co):
    A, l = co.A, 1
    start = co.base
    W = A["od_w_in_2"][0]
    kt, v, qt = alloc(co, [P, 8, 512]), alloc(co, [P, 4, D]), alloc(co, [P, 8, 256])
    co.gs = alloc(co, [P, 2, 32])
    gn = alloc(co, [P, 2, 64])
    nb = alloc(co, [P, 16, 384])
    low = co.base
    tk, w1 = alloc(co, [P, 2, 512]), alloc(co, [P, 2, 512])
    fe = counts(co)
    co.gsfree = fe
    co.po.wait_ge(fe)
    gd = (load_small(co, gn[:, 0, :], A["na_q_g_2"].to_broadcast([P, 64])),
          load_small(co, gn[:, 1, :], A["na_k_g_2"].to_broadcast([P, 64])))
    ld = []
    co.po.wait_ge(co.nadep)
    for r2 in range(2):
        for i in range(6):
            src = A["na"][:, 1 - r2 + i, :, :]
            src = bass.AP(tensor=src.tensor, offset=src.offset + 63, ap=[[7 * 16 * P - 1, 64], [P, 16], [1, 64]])
            ld.append(load_small(co, nb[64 * r2:64 * r2 + 64, :, 64 * i:64 * i + 64], src))
    free = {"tk": fe}
    dep = {"k": [], "v": [], "q": []}

    def on_heads(which, dst, c, cols):
        def evac(banks, tok):
            def gen():
                a = pair(co, tk[:, :, :], banks, tok, 0, 512, free["tk"])
                yield
                f = lambda t: t[:, :, :].rearrange("p t (g n) -> p t g n", n=64)
                a = groups(co, f(tk), f(w1), 64, 8, gn[:, which, :], (a, gd), fe)
                yield
                dep["qk"[which]].append(t32(co, lambda k, t: tk[:, t, k * P:(k + 1) * P], 4,
                                                 dst[:, 4 * c:4 * c + 4, cols], a, fe))
                free["tk"] = pe_mark(co)
            flush(co)
            spawn(co, gen())
        return evac

    def on_v(c, s0):
        def evac(banks, tok):
            for t in range(2):
                q = co.ac if t else co.dv
                q.wait_ge(tok, fe)
                banks[t].drained = q.copy(v[:, s0 + t, c * 512:(c + 1) * 512], banks[t].ap).then_inc(co.s_ac if q is co.ac else co.s_dv)
                dep["v"].append(banks[t].drained)
        return evac

    for s in (1, 0):
        spawn(co, prenorm(co, l, s, 0))
        flush(co)
        xt = (co.xh, co.xl)
        for c in range(2):
            gemm(co, xt, co.xdep, W, 1024 + c * 512, 512, on_heads(1, kt, c, slice(256 * s, 256 * s + 256)))
            gemm(co, xt, co.xdep, W, 2048 + c * 512, 512, on_v(c, 2 * s))
        if s == 0:
            for c in range(2):
                gemm(co, xt, co.xdep, W, c * 512, 512, on_heads(0, qt, c, slice(0, 256)))
        co.xtfree = pe_mark(co)
        flush(co)
    co.base = low
    pr = [alloc(co, [P, 512]) for _ in range(4)]
    at_ = [alloc(co, [P, 4, P]) for _ in range(2)]
    sm, mx = co.gs[:, 1, :].rearrange("p (t h) -> p t h", t=2), co.gs[:, 0, 0:4].unsqueeze(2)
    fa = counts(co)
    mt = ([co.gb[:, 0:512]] * 2, [co.gb[:, 512:1024]] * 2, [fa], [fa])
    kd, done = tuple(dep["k"] + dep["v"] + dep["q"]), []

    def attend():
        pfree, afree, mfree = [fa] * 4, [fa] * 2, [fa] * 4
        o = nb[:, :, :].rearrange("p h (i n) -> p (h i) n", n=64)
        na = co.cst[:, C_NA:C_NA + 64].unsqueeze(1).to_broadcast([P, 96, 64])
        co.dv.wait_ge(ld)
        nd = co.dv.tensor_tensor(o, o, na, ALU.add).then_inc(co.s_dv)
        items = [(t, h) for t in range(2) for h in range(16)]
        yb, st = {}, {}
        for i in range(len(items) + 4):
            if 1 <= i < len(items) + 1:
                r = (i - 1) % 4
                co.dv.wait_ge(st[i - 1], mfree[r])
                a = co.dv.tensor_reduce(mx[:, r, :], pr[r][:, :], AX, ALU.max).then_inc(co.s_dv)
                co.dv.wait_ge(a)
                shift = co.dv.tensor_scalar(mx[:, r, :], mx[:, r, :], -1.0, None, ALU.mult).then_inc(co.s_dv)
            if i < len(items):
                t, h = items[i]
                r = i % 4
                b = next_bank(co)
                rr = slice(64 * (h % 2), 64 * (h % 2) + 64)
                co.pe.wait_ge(kd, b.drained)
                m = co.pe.matmul(b.ap, qt[rr, h // 2, t * P:(t + 1) * P], kt[rr, h // 2, :], skip_group_check=True, start=True, stop=True).then_inc(co.s_pe)
                co.dv.wait_ge(m, nd, pfree[r])
                a = co.dv.scalar_tensor_tensor(pr[r][:, 0:256], b.ap[:, 0:256], 0.125, nb[:, h, 128 * (1 - t):128 * (1 - t) + 256], ALU.mult, ALU.add).then_inc(co.s_dv)
                score = (a, b)
            if 1 <= i < len(items) + 1:
                t, h = items[i - 1]
                r = (i - 1) % 4
                co.ac.wait_ge(shift, fa)
                st[i - 1] = mfree[r] = co.ac.activation(pr[r][:, :], pr[r][:, :], ACT.Exp, bias=mx[:, r, :], accum_out=sm[:, t, h:h + 1]).then_inc(co.s_ac)
            if 3 <= i < len(items) + 3:
                r, q = (i - 3) % 4, i % 2
                p = pr[r]
                b = next_bank(co)
                co.pe.wait_ge(st[i - 3], b.drained)
                for k in range(4):
                    m = co.pe.transpose(b.ap[:, k * P:(k + 1) * P], p[:, k * P:(k + 1) * P], ident(co, p[:, k * P:(k + 1) * P])).then_inc(co.s_pe, k == 3)
                pfree[r] = m
                co.ac.wait_ge(m, afree[q])
                b.drained = st[i - 3] = co.ac.activation(at_[q][:, :, :], b.ap.rearrange("p (k n) -> p k n", n=P), ACT.Copy).then_inc(co.s_ac)
            if i < len(items):
                r = i % 4
                a, b = score
                co.ac.wait_ge(a, pfree[r])
                c = co.ac.activation(pr[r][:, 256:512], b.ap[:, 256:512], ACT.Copy, scale=0.125).then_inc(co.s_ac)
                b.drained = st[i] = (a, c)
            yield
            if i >= 4:
                t, h = items[i - 4]
                q = (i - 1) % 2
                if h % 8 == 0:
                    yb[h // 8] = next_bank(co, hold=True)
                b = yb[h // 8]
                co.pe.wait_ge(st[i - 4], b.drained)
                for k in range(4):
                    m = co.pe.matmul(b.ap[:, (h % 8) * 64:(h % 8 + 1) * 64], at_[q][:, k, :], v[:, k, h * 64:(h + 1) * 64], start=k == 0, stop=k == 3, skip_group_check=True).then_inc(co.s_pe, k == 3)
                afree[q] = m
                if h % 8 == 7:
                    c = h // 8
                    rc = sm[:, t, 8 * c:8 * c + 8]
                    co.dv.wait_ge(m)
                    a = co.dv.reciprocal(rc, rc).then_inc(co.s_dv)
                    co.dv.wait_ge(a, co.yfree)
                    b.drained = e = co.dv.tensor_tensor(co.y[:, t, c * 512:(c + 1) * 512].rearrange("p (g n) -> p g n", n=64), b.ap.rearrange("p (g n) -> p g n", n=64), rc.unsqueeze(2).to_broadcast([P, 8, 64]), ALU.mult).then_inc(co.s_dv)
                    b.held = False
                    done.append(e)
    spawn(co, attend())
    mod_groups(co, MOD_LATE, mt, quiet=False)
    co.gbfree = (mt[2][0], mt[3][0])
    flush(co)
    co.base = start
    out_proj(co, l, 0, tuple(done))


def first_and_second_block(nc, A, out):
    A["t5"] = nc.dram_tensor("t5_rows", [8, P, 512], F32).ap()
    A["na"] = nc.dram_tensor("rpb_rows", [64, 7, 16, P], F32).ap()
    A["gates"] = nc.dram_tensor("gate_rows", [2, 2, 2, D], F32).ap()
    with ExitStack() as ctx:
        co = new_core(nc, A, ctx, first_plan(A) + second_plan(A))
        setup(co)
        for l in range(2):
            ffn1(co, l, 0, None)
            mixer(co, l, (l, 2))
            cross(co, l, (l, 3))
            ffn1(co, l, 1, (1, 0) if l == 0 else None)
        flush(co)
        begin(co)
        even(co)
        ffn2(co, 0, 1)
        ffn2(co, 0, 0)
        odd(co)
        ffn2(co, 1, 0)
        flush(co)
        co.xready = co.ready[0]
        finish_out(co, out)
        emit(co)


_INS = ["x", "mem", "ln_g", "ln_b", "ffn_w_in", "ffn_w_out", "w_mix_in", "b_gate", "kv_norm_g", "w_uk", "w_uv",
        "conv_w", "w_branch", "w_mix_out", "xa_wq", "xa_wkv", "xa_wo", "rel_bias", "c_2", "ctx_2", "c_ctx_2",
        "mod_w_2", "mod_b_2", "norm_mix_g_2", "norm_ffn_g_2", "w_out_2", "ffn_w_in_2", "ffn_w_out_2", "ev_w_in_2",
        "da_q_g_2", "da_k_g_2", "da_lq1_2", "da_lk1_2", "da_lq2_2", "da_lk2_2", "da_out_g_2", "mla_q_a_g_2",
        "mla_w_uq_2", "mla_kv_a_g_2", "mla_w_ukv_2", "mla_q_g_2", "mla_k_g_2", "mla_kr_g_2", "od_w_in_2",
        "na_q_g_2", "na_k_g_2", "na_rpb_2"]


def kernel(**inputs):
    import concourse.bacc as _bacc
    from concourse.bass_utils import run_bass_kernel_spmd as _run

    nc = _bacc.Bacc("TRN2", target_bir_lowering=False, num_devices=1)
    arrays, aps = {}, {}
    given = {n: np.ascontiguousarray(inputs[n]) for n in _INS}
    given["consts"], given["buckets"], given["rope"] = constants(), bucket_table(), rope_table()
    for name, a in given.items():
        arrays[f"in_{name}"] = a
        aps[name] = nc.dram_tensor(f"in_{name}", a.shape, mybir.dt.from_np(a.dtype), kind="ExternalInput").ap()
    out = nc.dram_tensor("out_0", (1, 256, D), F32, kind="ExternalOutput").ap()
    first_and_second_block(nc, aps, out[0])
    r = _run(nc, [arrays], core_ids=[0])
    return r.results[0]["out_0"]
```

```python
from contextlib import ExitStack
import math

import numpy as np

import concourse.bass as bass
from concourse import mybir

F32 = mybir.dt.float32
F32R = mybir.dt.float32r
ALU = mybir.AluOpType
ACT = mybir.ActivationFunctionType
AX = mybir.AxisListType.X
P = 128
HP = [0, 2, 4, 6, 1, 3, 5, 7]
D = 1024
F = 2816
BIG = 1e30
ALPHA = 4 ** 0.25

NRAW, NSPL, AHEAD = 3, 3, 2
UW = 2048

C_ID, C_TRI, C_ONE, C_NEG, C_SM, C_SN, C_HALF, C_S0, C_S1, C_NA, C_END = (
    0, 128, 256, 384, 640, 768, 896, 928, 1056, 1184, 1440)


def constants():
    c = np.zeros((P, C_END), np.float32)
    p = np.arange(P)[:, None]
    c[:, C_ID:C_ID + P] = np.eye(P)
    c[:, C_TRI:C_TRI + P] = p >= np.arange(P)[None]
    c[:, C_ONE:C_ONE + P] = 1
    c[:, C_NEG:C_NEG + 256] = np.where(np.arange(256)[None] > 128 + p, -3e38, 0)
    c[:, C_SM:C_SM + P] = p < np.arange(P)[None]
    c[:, C_SN:C_SN + P] = np.where(p < np.arange(P)[None], 0, -BIG)
    c[:, C_HALF:C_HALF + 32] = -0.5
    c[0, C_S0:C_S0 + P] = 1
    c[64, C_S1:C_S1 + P] = 1
    col = p % 64
    start = np.clip(col - 8, 0, 48)
    w = np.arange(256)[None] % 64
    c[:, C_NA:C_NA + 256] = np.where((w >= start) & (w < start + 16), 0, -BIG)
    return c


def bucket_table():
    n = np.maximum(255 - np.arange(512), 0)
    nf = np.maximum(n, 1).astype(np.float32)
    large = 16 + (np.log(nf / np.float32(16)) / np.float32(math.log(8.0)) * np.float32(16)).astype(np.int32)
    b = np.where(n < 16, n, np.minimum(large, 31))
    return (b[None] == np.arange(32)[:, None]).astype(np.float32)


def rope_table():
    t = np.arange(256)
    inv = (10000.0 ** (-np.arange(0, 32, 2, dtype=np.float32) / np.float32(32))).astype(np.float32)
    ar = (t // 64).astype(np.float32)[:, None] * inv
    ac = (t % 64).astype(np.float32)[:, None] * inv
    out = np.zeros((256, 2, 2, 2, 16), np.float32)
    for a, ang in enumerate((ar, ac)):
        out[:, 0, a, :] = np.cos(ang)[:, None]
        out[:, 1, a, 0] = -np.sin(ang)
        out[:, 1, a, 1] = np.sin(ang)
    return out.reshape(2, 128, 128).transpose(1, 0, 2).copy()


class Count:

    def __init__(self, sem):
        self.sem, self.n = sem, 0

    def mark(self, back=0):
        return (self, self.n - back)


class Step:

    def __init__(self, make):
        self.make, self.inc = make, None

    def then_inc(self, count, when=True, by=1):
        if not when:
            return None
        self.inc = (count.sem, by)
        count.n += by
        return count.mark()

    def play(self, e):
        ins = self.make(e)
        if self.inc:
            ins.then_inc(*self.inc)


class Wait:
    inc = True

    def __init__(self, sem, value):
        self.sem, self.value = sem, value

    def play(self, e):
        e.wait_ge(self.sem, self.value)


class Queue:

    def __init__(self):
        self.steps = []

    def step(self, make):
        self.steps.append(Step(make))
        return self.steps[-1]

    def wait_ge(self, *marks):
        for m in marks:
            if isinstance(m, (list, tuple)) and not (m and isinstance(m[0], Count)):
                self.wait_ge(*m)
            elif m is not None and m[1] > 0:
                self.steps.append(Wait(m[0].sem, m[1]))

    def dma_start(self, out, in_):
        return self.step(lambda e: e.dma_start(out, in_))

    def tensor_tensor(self, out, a, b, op):
        return self.step(lambda e: e.tensor_tensor(out, a, b, op))

    def play(self, e):
        for s in self.steps:
            s.play(e)


class VectorQueue(Queue):
    def tensor_scalar(self, out, a, s1, s2, op0, op1=None):
        if op1 is None:
            return self.step(lambda e: e.tensor_scalar(out, a, s1, None, op0))
        return self.step(lambda e: e.tensor_scalar(out, a, s1, s2, op0, op1))

    def scalar_tensor_tensor(self, out, a, s, b, op0, op1):
        return self.step(lambda e: e.scalar_tensor_tensor(out, a, s, b, op0, op1))

    def tensor_copy(self, out, a):
        return self.step(lambda e: e.tensor_copy(out, a))

    def tensor_reduce(self, out, a, axis, op):
        return self.step(lambda e: e.tensor_reduce(out, a, axis, op))

    def reciprocal(self, out, a):
        return self.step(lambda e: e.reciprocal(out, a))

    def bn_stats(self, out, a):
        return self.step(lambda e: e.bn_stats(out, a))

    def bn_aggr(self, out, a):
        return self.step(lambda e: e.bn_aggr(out, a))

    def max(self, out, a):
        return self.step(lambda e: e.max(out, a))

    def match_replace(self, out, eight, a, v):
        return self.step(lambda e: e.match_replace(out, eight, a, v))

    def memset(self, out, v):
        return self.step(lambda e: e.memset(out, v))

    copy = tensor_copy


class ScalarQueue(Queue):
    def activation(self, out, a, f, **k):
        return self.step(lambda e: e.activation(out, a, f, **k))

    def copy(self, out, a):
        return self.activation(out, a, ACT.Copy)


class TensorQueue(Queue):
    def matmul(self, out, lhs, rhs, **k):
        return self.step(lambda e: e.matmul(out, lhs, rhs, **k))

    def transpose(self, out, a, ident):
        return self.step(lambda e: e.transpose(out, a, ident))


def blocks(w, c0, n, plain=False):
    kts = w.shape[0] // P
    return [(w, k0, min(4, kts - k0), c0, n, plain) for k0 in range(0, kts, 4)]


def same(a, b):
    return a[0].tensor.name == b[0].tensor.name and a[0].offset == b[0].offset and a[1:] == b[1:]


def ffn_blocks(w_in, w_out):
    out = []
    for c in range(0, F, 512):
        n = min(512, F - c)
        out += blocks(w_in, c, n) + blocks(w_in, F + c, n)
    return out + blocks(w_out, 0, 512) + blocks(w_out, 512, 512)


MOD_PARTS = [1, 5, 2, 1, 1, 1, 5, 2, 1, 0, 3, 2]
MOD_GROUPS = [(l, j) for l in range(2) for j in range(12)]
assert sum(MOD_PARTS) == len(MOD_GROUPS)


def mod_part(l, i):
    a = sum(MOD_PARTS[:5 * l + i])
    return MOD_GROUPS[a:a + MOD_PARTS[5 * l + i]]


def mod_blocks(A, groups):
    return [b for l, j in groups for b in blocks(A["mod_w_2"][l], j * 512, 512, plain=True)]


def first_plan(A):
    out = []
    for l in range(2):
        early = [mod_blocks(A, mod_part(l, i)) for i in range(5)]
        out += ffn_blocks(A["ffn_w_in"][l, 0], A["ffn_w_out"][l, 0]) + early[0]
        for c, n in [(0, 512), (512, 512), (1024, 200), (3272, 512), (3784, 512), (2760, 512), (1224, 512),
                     (1736, 512), (2248, 512)]:
            out += blocks(A["w_mix_in"][l], c, n)
        out += early[1]
        for i in range(6):
            out += blocks(A["w_mix_in"][l], 4296 + i * 512, 512)
        for i in (0, 2, 1):
            for c in (0, 512):
                out += blocks(A["w_branch"][l, i], c, 512)
        for w in ("w_mix_out", "xa_wkv"):
            for c in (0, 512):
                out += blocks(A[w][l], c, 512)
        out += blocks(A["xa_wq"][l], 0, 512) + early[2]
        for c in (0, 512):
            out += blocks(A["xa_wo"][l], c, 512)
        out += early[3] + ffn_blocks(A["ffn_w_in"][l, 1], A["ffn_w_out"][l, 1])
        out += early[4]
    return out


def second_plan(A):
    def w_out(l):
        return blocks(A["w_out_2"][l], 0, 512) + blocks(A["w_out_2"][l], 512, 512)

    def ffn(l):
        return ffn_blocks(A["ffn_w_in_2"][l], A["ffn_w_out_2"][l])

    ev, od, ukv, uq = A["ev_w_in_2"][0], A["od_w_in_2"][0], A["mla_w_ukv_2"][0], A["mla_w_uq_2"][0]
    out = []
    for s in range(2):
        late = mod_blocks(A, mod_part(2, s))
        out += blocks(ev, 1536, 448) + blocks(ev, 512, 512) + blocks(ev, 0, 512)
        out += blocks(ukv, 0, 512) + blocks(uq, 0, 384) + blocks(ev, 1024, 512)
        out += blocks(ukv, 512, 512) + blocks(uq, 384, 384) + late + w_out(0)
    out += ffn(0) + ffn(0)
    for s in range(2):
        for c in (0, 512):
            out += blocks(od, 1024 + c, 512) + blocks(od, 2048 + c, 512)
    out += blocks(od, 0, 512) + blocks(od, 512, 512)
    return out + w_out(1) + ffn(1)


class Bank:
    def __init__(self, ap):
        self.ap, self.drained, self.held = ap[:, :], None, False


class Core:
    pass


def new_core(nc, A, ctx, plan):
    co = Core()
    co.nc, co.A, co.ctx, co.plan = nc, A, ctx, plan
    sem = lambda n: Count(ctx.enter_context(nc.semaphore(n)))
    co.pe, co.dv, co.ac, co.po, co.sp = TensorQueue(), VectorQueue(), ScalarQueue(), Queue(), Queue()
    co.s_pe, co.s_dv, co.s_ac, co.s_po = sem("s_pe"), sem("s_dv"), sem("s_ac"), sem("s_po")
    co.s_hi, co.s_lo, co.s_use = sem("s_hi"), sem("s_lo"), sem("s_use")
    co.s_out = sem("s_out")
    co.s_raw = [sem(f"s_raw{i}") for i in range(NRAW)]
    co.s_par = [sem(f"s_par{i}") for i in range(12)]
    co.npar = 0
    co.nuse = 0
    co.nth, n = [], 0
    for b in plan:
        co.nth.append(-1 if b[5] else n)
        n += not b[5]
    co.bg = []
    co.base = 16512
    co.top = 229344
    co.y = nc.alloc_sbuf_tensor_at("y", [P, 2, D], F32, offset=co.top - 8192)
    co.names = 0
    co.raw = [alloc(co, [P, UW]) for _ in range(NRAW)]
    co.whi = [alloc(co, [P, UW], F32R) for _ in range(NSPL)]
    co.wlo = [alloc(co, [P, UW], F32R) for _ in range(NSPL)]
    co.banks = [Bank(ctx.enter_context(nc.psum_tensor(f"bank{i}", [P, 512], F32))) for i in range(8)]
    co.bi = 0
    for u in range(AHEAD):
        stage(co, u)
    return co




def alloc(co, shape, dt=F32):
    n = 4
    for s in shape[1:]:
        n *= s
    n = (n + 31) // 32 * 32
    co.names += 1
    assert co.base + n <= co.top, (co.base, n, co.top)
    t = co.nc.alloc_sbuf_tensor_at(f"m{co.names}", shape, dt, offset=co.base)
    co.base += n
    return t


def counts(co):
    return (pe_mark(co), co.s_dv.mark(), co.s_ac.mark(), co.s_po.mark(),
            tuple(s.mark() for s in co.s_par if s.n))


def pe_mark(co):
    assert not co.pe.steps or co.pe.steps[-1].inc
    return (co.s_pe.mark(), co.s_use.mark())


def next_bank(co, hold=False):
    while co.banks[co.bi].held:
        co.bi = (co.bi + 1) % 8
    b = co.banks[co.bi]
    co.bi = (co.bi + 1) % 8
    b.held = hold
    return b




def load_small(co, out, in_):
    s = co.s_par[co.npar % len(co.s_par)]
    co.npar += 1
    if s.n:
        co.po.wait_ge(s.mark())
    return co.po.dma_start(out, in_).then_inc(s, by=16)


def ident(co, a):
    n = a.shape[0]
    return co.cst[0:n, C_ID:C_ID + n]


def minus_half(co, v):
    return co.cst[:, C_HALF:C_HALF + v.shape[-1]]




def spawn(co, gen):
    if next(gen, StopIteration) is not StopIteration:
        co.bg.append(gen)


def advance(co):
    co.bg = [g for g in co.bg if next(g, StopIteration) is not StopIteration]


def flush(co):
    while co.bg:
        advance(co)




def slot(co, ring, u, nk, n):
    return ring[u % len(ring)][:, 0:nk * n].rearrange("p (k n) -> p k n", k=nk)


def stage(co, u):
    if u >= len(co.plan):
        return
    w, k0, nk, c0, n, plain = co.plan[u]
    v = co.nth[u]
    raw = slot(co, co.raw, u, nk, n)
    landed = co.s_raw[u % NRAW]
    if u >= NRAW:
        if co.plan[u - NRAW][5]:
            co.sp.wait_ge((co.s_use, u - NRAW + 1))
        else:
            co.sp.wait_ge((co.s_hi, co.nth[u - NRAW] + 1))
            co.sp.wait_ge((co.s_lo, co.nth[u - NRAW] + 1))
    co.sp.dma_start(raw, w[k0 * P:(k0 + nk) * P, c0:c0 + n].rearrange("(k p) n -> p k n", p=P))\
        .then_inc(landed, by=16)
    if plain:
        return

    hi, lo = slot(co, co.whi, v, nk, n), slot(co, co.wlo, v, nk, n)
    co.ac.wait_ge(landed.mark())
    if v >= NSPL:
        co.ac.wait_ge((co.s_use, co.nth.index(v - NSPL) + 1))
    co.ac.activation(hi, raw, ACT.Copy).then_inc(co.s_hi)

    co.dv.wait_ge(landed.mark())
    co.dv.wait_ge((co.s_hi, v + 1))
    if v >= NSPL:
        co.dv.wait_ge((co.s_use, co.nth.index(v - NSPL) + 1))
    co.dv.tensor_tensor(lo, raw, hi.bitcast(F32), ALU.subtract).then_inc(co.s_lo)


def next_block(co, w, k0, nk, c0, n, plain):
    u = co.nuse
    co.nuse += 1
    assert same(co.plan[u], (w, k0, nk, c0, n, plain)), u
    stage(co, u + AHEAD)
    return u


def gemm(co, xt, xdep, w, c0, n, evac, quiet=False):
    hi, lo = xt
    kts = w.shape[0] // P
    banks = [next_bank(co, hold=True) for _ in range(2)]
    for k0 in range(0, kts, 4):
        nk = min(4, kts - k0)
        u = next_block(co, w, k0, nk, c0, n, False)
        v = co.nth[u]
        wh, wl = slot(co, co.whi, v, nk, n), slot(co, co.wlo, v, nk, n)
        co.pe.wait_ge((co.s_hi, v + 1))
        co.pe.wait_ge((co.s_lo, v + 1))
        co.pe.wait_ge(xdep[k0 // 2:(k0 + nk + 1) // 2] if isinstance(xdep, list) else xdep)
        for t in range(2):
            out = banks[t].ap[:, 0:n]
            co.pe.wait_ge(banks[t].drained)
            for k in range(nk):
                xh = hi[:, k0 + k, t * P:(t + 1) * P]
                xl = lo[:, k0 + k, t * P:(t + 1) * P]
                co.pe.matmul(out, xh, wh[:, k, :], start=k0 + k == 0, stop=False, skip_group_check=True)
                co.pe.matmul(out, xh, wl[:, k, :], start=False, stop=False, skip_group_check=True)
                used = co.pe.matmul(out, xl, wh[:, k, :], start=False, stop=k0 + k == kts - 1, skip_group_check=True)\
                    .then_inc(co.s_use, t == 1 and k == nk - 1)
        if not quiet:
            advance(co)
    evac(banks, used)
    for b in banks:
        b.held = False


def gemm_t(co, xt, xdep, w, c0, n, evac):
    hi, lo = xt
    kts = w.shape[0] // P
    banks = [next_bank(co, hold=True) for _ in range((n // P + 1) // 2)]
    for k0 in range(0, kts, 4):
        nk = min(4, kts - k0)
        u = next_block(co, w, k0, nk, c0, n, False)
        v = co.nth[u]
        wh, wl = slot(co, co.whi, v, nk, n), slot(co, co.wlo, v, nk, n)
        co.pe.wait_ge((co.s_hi, v + 1))
        co.pe.wait_ge((co.s_lo, v + 1))
        co.pe.wait_ge(xdep[k0 // 2:(k0 + nk + 1) // 2] if isinstance(xdep, list) else xdep)
        for b in range(n // P):
            out = banks[b // 2].ap[:, 256 * (b % 2):256 * (b % 2) + 256]
            cs = slice(b * P, (b + 1) * P)
            co.pe.wait_ge(banks[b // 2].drained)
            for k in range(nk):
                xh, xl = hi[:, k0 + k, :], lo[:, k0 + k, :]
                co.pe.matmul(out, wh[:, k, cs], xh, start=k0 + k == 0 and b % 2 == 0, stop=False, skip_group_check=True)
                co.pe.matmul(out, wh[:, k, cs], xl, start=False, stop=False, skip_group_check=True)
                used = co.pe.matmul(out, wl[:, k, cs], xh, start=False, stop=k0 + k == kts - 1, skip_group_check=True)\
                    .then_inc(co.s_use, b == n // P - 1 and k == nk - 1)
        advance(co)
    evac(banks, used)
    for b in banks:
        b.held = False


def plain_gemm(co, xt, xdep, w, c0, evac, quiet):
    kts = w.shape[0] // P
    bank = next_bank(co, hold=True)
    co.pe.wait_ge(xdep, bank.drained)
    for k0 in range(0, kts, 4):
        u = next_block(co, w, k0, 4, c0, 512, True)
        raw = slot(co, co.raw, u, 4, 512)
        co.pe.wait_ge((co.s_raw[u % NRAW], 16 * (u // NRAW + 1)))
        for k in range(4):
            used = co.pe.matmul(bank.ap[0:xt.shape[2], :], xt[:, k0 + k, :], raw[:, k, :], start=k0 + k == 0,
                                stop=k0 + k == kts - 1, skip_group_check=True).then_inc(co.s_use, k == 3)
        if not quiet:
            advance(co)
    evac(bank, used)
    bank.held = False


def finish_out(co, out):
    co.sp.wait_ge(co.xready)
    done = co.sp.dma_start(out.rearrange("(t p) d -> p t d", p=P), co.x[:, :, :]).then_inc(co.s_out, by=16)
    co.sp.wait_ge(done)
    co.sp.wait_ge([s.mark() for s in co.s_par if s.n])


def emit(co):
    block = co.ctx.enter_context(co.nc.Block())

    @block.sync
    def _(e):
        co.sp.play(e)

    @block.scalar
    def _(e):
        co.ac.play(e)

    @block.gpsimd
    def _(e):
        co.po.play(e)

    @block.vector
    def _(e):
        co.dv.play(e)

    @block.tensor
    def _(e):
        co.pe.play(e)




def to_t(co, src, kt, dst, dep, free=None):
    hi, lo = dst
    out = []
    for k0 in range(0, kt, 2):
        nk = min(2, kt - k0)
        b = next_bank(co)
        co.pe.wait_ge(dep, b.drained)
        for k in range(nk):
            for t in range(2):
                tok = co.pe.transpose(b.ap[:, k * 256 + t * P:k * 256 + (t + 1) * P], src(t, k0 + k), ident(co, src(t, k0 + k))).then_inc(co.s_pe, k == nk - 1 and t == 1)
        ps = b.ap[:, 0:nk * 256].rearrange("p (k n) -> p k n", k=nk)
        co.ac.wait_ge(tok, free)
        a = co.ac.activation(hi[:, k0:k0 + nk, :], ps, ACT.Copy).then_inc(co.s_ac)
        co.dv.wait_ge(tok, a, free)
        v = co.dv.tensor_tensor(lo[:, k0:k0 + nk, :], ps, hi[:, k0:k0 + nk, :].bitcast(F32), ALU.subtract).then_inc(co.s_dv)
        b.drained = (a, v)
        out.append((a, v))
    return out


def t32(co, src, n, dst, dep, free=None, scale=1.0):
    toks = []
    for k0 in range(0, n, 2):
        nk = min(2, n - k0)
        b = next_bank(co)
        for k in range(nk):
            for t in range(2):
                s = src(k0 + k, t)
                m = s.shape[-1]
                co.pe.wait_ge(dep, b.drained)
                tok = co.pe.transpose(b.ap[0:m, k * 256 + t * P:k * 256 + (t + 1) * P], s, ident(co, s)).then_inc(co.s_pe, k == nk - 1 and t == 1)
        m = dst.shape[0]
        ps = b.ap[0:m, 0:nk * 256].rearrange("p (k n) -> p k n", k=nk)
        co.ac.wait_ge(tok, free)
        a = co.ac.activation(dst[:, k0:k0 + nk, :], ps, ACT.Copy, scale=scale).then_inc(co.s_ac)
        b.drained = a
        toks.append(a)
    return tuple(toks)


def load_ln(co, l, i, *deps):
    A = co.A
    co.po.wait_ge(deps)
    co.lnpar = (load_small(co, co.lg[:, :], A["ln_g"][l, i:i + 1, :].to_broadcast([P, D])),
                  load_small(co, co.lb[:, :], A["ln_b"][l, i:i + 1, :].to_broadcast([P, D])))


def norm_stats(co, y, t, c, dep):
    co.dv.wait_ge(dep, co.rsfree)
    return co.dv.bn_stats(co.st[:, t, c, :], y[:, t, c * 512:(c + 1) * 512]).then_inc(co.s_dv)


def layer_norm(co, y, ydep, stats, eps, nxt):
    st, mv, rs, par = co.st, co.mv, co.rs, co.lnpar
    norm, cen = [], []
    for t in range(2):
        co.dv.wait_ge(stats[t])
        tok = co.dv.bn_aggr(mv[:, t, :], st[:, t, :, :].rearrange("p c s -> p (c s)")).then_inc(co.s_dv)
        co.dv.wait_ge(tok)
        tok = co.dv.tensor_scalar(rs[:, t, 0:1], mv[:, t, 1:2], eps, None, ALU.add).then_inc(co.s_dv)
        co.po.wait_ge(tok)
        norm.append(co.po.tensor_tensor(rs[:, t, 1:2], rs[:, t, 0:1], minus_half(co, rs[:, t, 0:1]), ALU.pow).then_inc(co.s_po))
        co.dv.wait_ge(tok, ydep[t], par)
        cen.append(co.dv.scalar_tensor_tensor(y[:, t, :], y[:, t, :], mv[:, t, 0:1], co.lg[:, :], ALU.subtract, ALU.mult).then_inc(co.s_dv))
    yield
    out = {}
    co.dv.wait_ge(co.xfree, par)
    for c in range(2):
        for t in range(2):
            cs = slice(c * 512, (c + 1) * 512)
            co.dv.wait_ge(norm[t], cen[t])
            out[t, c] = co.dv.scalar_tensor_tensor(co.x[:, t, cs], y[:, t, cs], rs[:, t, 1:2], co.lb[:, cs], ALU.mult, ALU.add).then_inc(co.s_dv)
    tok = out[1, 1]
    if nxt:
        load_ln(co, nxt[0], nxt[1], tok)
    co.rsfree = tok
    co.xready = (out[0, 1], tok)
    yield
    if nxt is None:
        return
    hi, lo = co.xh, co.xl
    co.xdep = []
    for c in range(2):
        co.xdep += to_t(co, lambda t, k: co.x[:, t, (4 * c + k) * P:(4 * c + k + 1) * P], 4,
                        (hi[:, 4 * c:, :], lo[:, 4 * c:, :]), (out[0, c], out[1, c]), co.xtfree)
    co.xfree = pe_mark(co)


def mod_setup(co, rows, cs, fe):
    A = co.A
    co.po.wait_ge(fe)
    d = [load_small(co, rows[0:8, :], A["c_2"][0].rearrange("(k p) -> k p", p=P)),
         load_small(co, rows[8:16, :], A["c_ctx_2"].rearrange("(k p) -> k p", p=P)),
         load_small(co, rows[16:32, :], A["norm_mix_g_2"].rearrange("l (k p) -> (l k) p", p=P)),
         load_small(co, rows[32:48, :], A["norm_ffn_g_2"].rearrange("l (k p) -> (l k) p", p=P))]
    b = next_bank(co)
    co.pe.wait_ge(d, co.cdep, b.drained)
    m = co.pe.transpose(b.ap[:, 0:48], rows[:, :], ident(co, rows[:, :])).then_inc(co.s_pe)
    co.dv.wait_ge(m, fe)
    g = co.dv.tensor_copy(co.gcol[:, :], b.ap[:, 0:48]).then_inc(co.s_dv)
    co.ac.wait_ge(g, fe)
    s = co.ac.activation(cs[:, :], b.ap[:, 0:16], ACT.Silu).then_inc(co.s_ac)
    b.drained = (g, s)
    co.ac.wait_ge(s)
    co.chdep = co.ac.activation(co.ch[:, :, :], cs[:, :].rearrange("p (a k) -> p k a", a=2), ACT.Copy).then_inc(co.s_ac)
    co.gcdep = g


def mod_tiles(co):
    t = [alloc(co, [P, 512]) for _ in range(4)]
    fe = counts(co)
    return t[0:2], t[2:4], [fe, fe], [fe, fe]


def mod_groups(co, groups, tiles, quiet=True):
    A = co.A
    mb, rt, bfree, rfree = tiles
    for l, j in groups:
        blk, half, i, ib = j // 2, j % 2, j % len(rfree), j % len(bfree)
        co.po.wait_ge(bfree[ib])
        bd = load_small(co, mb[ib][0:2, :], A["mod_b_2"][l:l + 1, j * 512:(j + 1) * 512].to_broadcast([2, 512]))

        def evac(bank, tok):
            co.dv.wait_ge(tok, bd, rfree[i])
            a = co.dv.tensor_tensor(rt[i][0:2, :], bank.ap[0:2, :], mb[ib][0:2, :], ALU.add).then_inc(co.s_dv)
            bank.drained = bfree[ib] = a
            if blk in (2, 5):
                co.po.wait_ge(a)
                rfree[i] = co.gated_at[l, blk // 3, half] = load_small(
                    co, A["gates"][l, blk // 3, :, half * 512:(half + 1) * 512], rt[i][0:2, :])
            else:
                spawn(co, columns(l, blk, half, i, a))

        def columns(l, blk, half, i, a):
            yield
            b = next_bank(co)
            co.pe.wait_ge(a, b.drained)
            for k in range(4):
                r = rt[i][0:2, k * P:(k + 1) * P]
                m = co.pe.transpose(b.ap[:, 2 * k:2 * k + 2], r, ident(co, r)).then_inc(co.s_pe, k == 3)
            rfree[i] = m
            co.dv.wait_ge(m)
            b.drained = co.mcd[l, blk, half] = co.dv.tensor_copy(co.mc[:, l, blk, 4 * half:4 * half + 4, :], b.ap[:, 0:8].rearrange("p (k a) -> p k a", k=4)).then_inc(co.s_dv)

        plain_gemm(co, co.ch, co.chdep, A["mod_w_2"][l], j * 512, evac, quiet)
        if quiet and (l, j) != groups[-1]:
            advance(co)


def mod_gain(co, l, f):
    v = co.mgain[:, l, f, :, :]
    c = 16 + 16 * f + 8 * l
    shift, scale = (co.mcd[l, 3 * f, 0], co.mcd[l, 3 * f, 1]), (co.mcd[l, 3 * f + 1, 0], co.mcd[l, 3 * f + 1, 1])
    co.dv.wait_ge(scale, co.gcdep)
    a = co.dv.tensor_scalar(v, co.mc[:, l, 3 * f + 1, :, :], 1.0, None, ALU.add).then_inc(co.s_dv)
    co.dv.wait_ge(a)
    a = co.dv.tensor_tensor(v, v, co.gcol[:, c:c + 8].unsqueeze(2).to_broadcast([P, 8, 2]), ALU.mult).then_inc(co.s_dv)
    return (a, shift)


def residual(co, y, scale, got, fe):
    def make(c0, n):
        def evac(banks, tok):
            for t in range(2):
                o = y[:, t, c0:c0 + n]
                co.dv.wait_ge(tok, co.xready, fe)
                r = co.dv.scalar_tensor_tensor(o, co.x[:, t, c0:c0 + n], scale, banks[t].ap[:, 0:n], ALU.mult, ALU.add).then_inc(co.s_dv)
                banks[t].drained = r
                got[t] = r
            for t in range(2):
                got[2 + t] = norm_stats(co, y, t, c0 // 512, got[t])
        return evac
    return make


def ffn(co, w_in, w_out, resid, between=None):
    xt, xdep = (co.xh, co.xl), co.xdep
    base = co.base
    uh, ul = alloc(co, [P, 22, 256], F32R), alloc(co, [P, 22, 256], F32R)
    sa = alloc(co, [P, 2, 512])
    ut = [alloc(co, [P, 2, 512]) for _ in range(2)]
    fe = counts(co)
    free = {"sa": fe, 0: fe, 1: fe}
    udep = []
    for j in range(6):
        c, n = j * 512, min(512, F - j * 512)
        hold = []

        def evac_a(banks, tok):
            co.ac.wait_ge(tok, free["sa"])
            for i, b in enumerate(banks):
                b.drained = co.ac.activation(sa[:, i, :], b.ap, ACT.Silu).then_inc(co.s_ac)
                hold.append(b.drained)

        def evac_b(banks, tok):
            spawn(co, rest(banks, tok, j, n, hold))

        def rest(banks, tok, j, n, sat):
            u = ut[j % 2]
            got = []
            co.dv.wait_ge(tok, free[j % 2])
            for i, b in enumerate(banks):
                co.dv.wait_ge(sat[i])
                b.drained = co.dv.tensor_tensor(u[:, i, :], b.ap, sa[:, i, :], ALU.mult).then_inc(co.s_dv)
                got.append(b.drained)
            free["sa"] = got[-1]
            yield
            co.ac.wait_ge(fe)
            co.dv.wait_ge(fe)
            for i in range(len(banks)):
                k = 4 * j + 2 * i
                hi, lo = (v[:, k:k + 2, :].rearrange("p k n -> p (k n)") for v in (uh, ul))
                co.ac.wait_ge(got[i])
                a = co.ac.activation(hi, u[:, i, :], ACT.Copy).then_inc(co.s_ac)
                co.dv.wait_ge(a)
                udep.append((a, co.dv.tensor_tensor(lo, u[:, i, :], hi.bitcast(F32), ALU.subtract).then_inc(co.s_dv)))
            free[j % 2] = udep[-1]

        gemm_t(co, xt, xdep, w_in, c, n, evac_a)
        gemm_t(co, xt, xdep, w_in, F + c, n, evac_b)
    flush(co)
    co.xtfree = pe_mark(co)
    if between is not None:
        spawn(co, between)
    for c in range(2):
        gemm(co, (uh, ul), udep, w_out, c * 512, 512, resid(c * 512, 512))
    co.base = base


"""The first block's sublayers."""


def setup(co):
    A = co.A
    co.cst = alloc(co, [P, C_END])
    co.x = alloc(co, [P, 2, D])
    co.xh, co.xl = alloc(co, [P, 8, 256], F32R), alloc(co, [P, 8, 256], F32R)
    co.st, co.mv, co.rs = alloc(co, [P, 2, 2, 6]), alloc(co, [P, 2, 2]), alloc(co, [P, 2, 2])
    co.ch = alloc(co, [P, 8, 2])
    co.gcol, co.mc, co.mgain = alloc(co, [P, 48]), alloc(co, [P, 2, 6, 8, 2]), alloc(co, [P, 2, 2, 8, 2])
    co.mcd, co.gated_at = {}, {}
    co.lgbase = co.base
    co.lg, co.lb = alloc(co, [P, D]), alloc(co, [P, D])
    co.xfree = co.rsfree = co.xtfree = None
    cdep = co.cdep = load_small(co, co.cst[:, :], A["consts"][:, :])
    co.xready = load_small(co, co.x[:, :, :], A["x"][0].rearrange("(t p) d -> p t d", p=P))
    load_ln(co, 0, 0)
    co.xdep = to_t(co, lambda t, k: co.x[:, t, k * P:(k + 1) * P], 8, (co.xh, co.xl),
                          (co.xready, cdep))


def side_setup(co, fe):
    A = co.A
    rows, cs = alloc(co, [48, P]), alloc(co, [P, 16])
    e, rb, rep, row = alloc(co, [32, 512]), alloc(co, [32, 8]), alloc(co, [32, 8, P]), alloc(co, [P, 8, 512])
    co.po.wait_ge(fe)
    d = (load_small(co, e[:, :], A["buckets"][:, :]), load_small(co, rb[:, :], A["rel_bias"][:, :]))

    def gen():
        mod_setup(co, rows, cs, fe)
        yield
        outs = []
        co.dv.wait_ge(d, fe)
        co.ac.wait_ge(fe)
        for h in range(8):
            t = co.dv.tensor_scalar(rep[:, h, :], co.cst[0:32, C_ONE:C_ONE + P], rb[:, HP[h]:HP[h] + 1], None, ALU.mult).then_inc(co.s_dv)
            b = next_bank(co)
            co.pe.wait_ge(t, b.drained)
            t = co.pe.matmul(b.ap[:, :], rep[:, h, :], e[:, :], skip_group_check=True, start=True, stop=True).then_inc(co.s_pe)
            co.ac.wait_ge(t)
            b.drained = co.ac.activation(row[:, h, :], b.ap[:, :], ACT.Copy).then_inc(co.s_ac)
            outs.append(b.drained)
            if h % 2:
                yield
        co.po.wait_ge(tuple(outs))
        co.t5 = load_small(co, A["t5"].rearrange("h p s -> p h s"), row[:, :, :])
    return gen()


def ffn1(co, l, i, nxt):
    A = co.A
    flush(co)
    w = 0 if i == 0 else 1
    mark = co.base
    got = [None] * 4
    y = co.y
    between = None
    if (l, i) == (1, 1):
        second_tiles(co)
        mark = co.base
        y2 = alloc(co, [P, 2, D])
        between = prenorm(co, 0, 1, 0, y2)
        at = co.base
        co.pn = alloc(co, [P, D])
        co.base = at
    mt = mod_tiles(co)
    fe = counts(co)
    if (l, i) == (0, 0):
        between = side_setup(co, fe)
    if (l, i) == (0, 1):
        between = rpb_scratch(co, alloc(co, [P, 1792]), fe)
    ffn(co, A["ffn_w_in"][l, w], A["ffn_w_out"][l, w], residual(co, y, 2 * ALPHA, got, fe), between)
    if (l, i) == (1, 1):
        mt[2][:] = [co.pnfree, co.pnfree]
    spawn(co, layer_norm(co, y, got[0:2], got[2:4], 4e-5, nxt))
    mod_groups(co, mod_part(l, 4 if i else 0), mt)
    co.base = mark


def pair(co, dst, banks, tok, a, n, *deps):
    co.ac.wait_ge(tok, deps)
    t0 = co.ac.activation(dst[:, 0, :], banks[0].ap[:, a:a + n], ACT.Copy).then_inc(co.s_ac)
    co.dv.wait_ge(tok, deps)
    t1 = co.dv.tensor_copy(dst[:, 1, :], banks[1].ap[:, a:a + n]).then_inc(co.s_dv)
    banks[0].drained, banks[1].drained = (banks[0].drained, t0), (banks[1].drained, t1)
    return (t0, t1)


def columns_of(co, dst, banks, tok, scale, *deps):
    a, b = (v.ap.rearrange("p (k n) -> p k n", k=2) for v in banks)
    co.ac.wait_ge(tok, deps)
    banks[0].drained = co.ac.activation(dst[:, 0:2, :], a, ACT.Copy, scale=scale).then_inc(co.s_ac)
    co.dv.wait_ge(tok, deps)
    banks[1].drained = co.dv.tensor_scalar(dst[:, 2:4, :], b, scale, None, ALU.mult).then_inc(co.s_dv)
    return (banks[0].drained, banks[1].drained)


def mixer(co, l, nxt):
    A = co.A
    flush(co)
    w = A["w_mix_in"][l]
    xt = (co.xh, co.xl)
    start = co.base
    yt = {i: (alloc(co, [P, 4, 256], F32R), alloc(co, [P, 4, 256], F32R)) for i in (0, 2)}
    tkbase = co.base
    tk = [alloc(co, [P, 2, 512]) for _ in range(2)]
    fe = counts(co)
    tkfree = [fe, fe]
    ydep = {}
    turn = [0]

    def tokens_of(banks, tok, n, then):
        i = turn[0] % 2
        turn[0] += 1

        def gen():
            s = pair(co, tk[i][:, :, 0:n], banks, tok, 0, n, tkfree[i])
            yield
            tkfree[i] = then(tk[i], s)
        spawn(co, gen())

    qst, kst, vs = alloc(co, [P, 4, 256]), alloc(co, [P, 4, 256]), alloc(co, [P, 2, 512])
    low = co.base
    qat, iqt, ikt = alloc(co, [P, 4, 256]), alloc(co, [P, 4, 256]), alloc(co, [P, 1, 256])
    ckv, ckvt, iw = alloc(co, [P, 2, P]), alloc(co, [P, 1, 256]), alloc(co, [P, 2, 8])
    ik2, kvg, sq, ss = alloc(co, [P, 2, P]), alloc(co, [P, P]), alloc(co, [P, P]), alloc(co, [P, 2, 2])
    wuk, wuv = alloc(co, [P, 4, P]), alloc(co, [P, 8, 64])
    b1, L, pt, olt, qlt = (alloc(co, [P, 8, 256]), alloc(co, [P, 8, 256]), alloc(co, [P, 2, 4, P]),
                           alloc(co, [P, 4, P]), alloc(co, [P, 8, P]))
    sc, m8, mx, sm = alloc(co, [P, 2, 256]), alloc(co, [P, 8]), alloc(co, [P, 8]), alloc(co, [P, 2, 8])
    ya = co.lg[:, :].rearrange("p (t n) -> p t n", t=2)
    conv_y = co.lb[:, :].rearrange("p (k n) -> p k n", k=4)
    zt = alloc(co, [P, 4, 258])
    cw = alloc(co, [12, P])
    cwt = alloc(co, [P, 12])
    dep = {}
    co.po.wait_ge(fe)
    dep["w"] = (load_small(co, wuk[:, :, :], A["w_uk"][l].rearrange("(a b) d c -> (b d) a c", b=2)),
                load_small(co, wuv[:, :, :], A["w_uv"][l].rearrange("h c d -> c h d")),
                load_small(co, kvg[:, :], A["kv_norm_g"][l:l + 1, :].to_broadcast([P, P])),
                load_small(co, cw[:, :], A["conv_w"][l].rearrange("w (k p) -> (w k) p", p=P)))
    skew = bass.AP(tensor=A["t5"].tensor, offset=A["t5"].offset + 127, ap=[[511, P], [P * 512, 8], [1, 256]])
    co.po.wait_ge(fe, co.t5)
    dep["b1"] = load_small(co, b1[:, :, :], skew)

    def on_qa(banks, tok):
        dep["qa"] = columns_of(co, qat, banks, tok, 1.0, fe)

    def on_mid(s, tok):
        dep["iq0"] = t32(co, lambda k, t: s[:, t, P + k * P:P + (k + 1) * P], 3, iqt[:, :, :], tok, fe)
        p = pe_mark(co)
        done = []
        co.ac.wait_ge(tok, fe)
        for t in range(2):
            co.ac.wait_ge(done)
            a = co.ac.activation(sq[:, :], s[:, t, 0:P], ACT.Square, accum_out=ss[:, t, 0:1]).then_inc(co.s_ac)
            done = a
            co.dv.wait_ge(a)
            a = co.dv.tensor_scalar(ss[:, t, 0:1], ss[:, t, 0:1], 1.0 / P, 1e-5, ALU.mult, ALU.add).then_inc(co.s_dv)
            co.po.wait_ge(a)
            a = co.po.tensor_tensor(ss[:, t, 1:2], ss[:, t, 0:1], minus_half(co, ss[:, t, 0:1]), ALU.pow).then_inc(co.s_po)
            co.dv.wait_ge(a, dep["w"])
            a = co.dv.scalar_tensor_tensor(ckv[:, t, :], s[:, t, 0:P], ss[:, t, 1:2], kvg[:, :], ALU.mult, ALU.mult).then_inc(co.s_dv)
        dep["ckv"] = a
        return (p, a)

    def on_last(s, tok):
        dep["iq1"] = t32(co, lambda k, t: s[:, t, 0:P], 1, iqt[:, 3:4, :], tok, fe)
        p = pe_mark(co)
        co.dv.wait_ge(tok, fe)
        a = co.dv.tensor_scalar(iw[:, :, :], s[:, :, 192:200], (8 ** -0.5) * (64 ** -0.5), None, ALU.mult).then_inc(co.s_dv)
        co.dv.wait_ge(tok, fe)
        for r in range(2):
            b = co.dv.tensor_copy(ik2[:, :, r * 64:(r + 1) * 64], s[:, :, 128:192]).then_inc(co.s_dv)
        dep["iw"] = a
        dep["ik"] = t32(co, lambda k, t: ik2[:, t, :], 1, ikt[:, :, :], b, fe)
        dep["ckvt"] = t32(co, lambda k, t: ckv[:, t, :], 1, ckvt[:, :, :], dep["ckv"], fe)
        return (p, b)

    def ev(then, n=512):
        return lambda banks, tok: tokens_of(banks, tok, n, then)

    gemm_t(co, xt, co.xdep, w, 0, 512, on_qa)
    gemm(co, xt, co.xdep, w, 512, 512, ev(on_mid))
    gemm(co, xt, co.xdep, w, 1024, 200, ev(on_last, 200))

    def dsa():
        yield
        yield
        Lfree = scfree = ptfree = olfree = qlfree = smfree = None
        for t in range(2):
            nk = (t + 1) * P
            ts_ = slice(t * P, (t + 1) * P)
            ql = []
            for g in range(2):
                b = next_bank(co)
                co.pe.wait_ge(dep['qa'], dep['w'], b.drained)
                for i in range(4):
                    tok = co.pe.matmul(b.ap[:, i * P:(i + 1) * P], wuk[64 * g:64 * g + 64, i, :], qat[64 * g:64 * g + 64, i, ts_], skip_group_check=True, start=True, stop=True).then_inc(co.s_pe, i == 3)
                co.ac.wait_ge(tok, qlfree, fe)
                b.drained = co.ac.activation(qlt[:, 4 * g:4 * g + 4, :], b.ap.rearrange("p (h n) -> p h n", h=4), ACT.Copy, scale=0.125).then_inc(co.s_ac)
                ql.append(b.drained)
            rel = []
            for g in range(4):
                b = next_bank(co)
                r = slice(64 * (g // 2), 64 * (g // 2) + 64)
                co.pe.wait_ge(dep['iq0'], dep['iq1'], dep['ik'], b.drained)
                for i in range(2):
                    tok = co.pe.matmul(b.ap[:, i * nk:(i + 1) * nk], iqt[r, HP[2 * g + i] // 2, ts_], ikt[r, 0, 0:nk], skip_group_check=True, start=True, stop=True).then_inc(co.s_pe, i == 1)
                co.ac.wait_ge(tok, Lfree, fe)
                b.drained = co.ac.activation(L[:, 2 * g:2 * g + 2, 0:nk], b.ap[:, 0:2 * nk].rearrange("p (h n) -> p h n", h=2), ACT.Relu).then_inc(co.s_ac)
                rel.append(b.drained)
            yield
            neg = co.cst[:, C_NEG + 256 - nk:C_NEG + 256]
            tok = scfree
            co.dv.wait_ge(dep['iw'], fe)
            for h in range(8):
                co.dv.wait_ge(rel[h // 2], tok)
                tok = co.dv.scalar_tensor_tensor(sc[:, 0, 0:nk], L[:, h, 0:nk], iw[:, t, HP[h]:HP[h] + 1], neg if h == 0 else sc[:, 0, 0:nk], ALU.mult, ALU.add).then_inc(co.s_dv)
            yield
            for r in range(8):
                v, o = sc[:, r % 2, 0:nk], sc[:, (r + 1) % 2, 0:nk]
                co.dv.wait_ge(tok)
                tok = co.dv.max(m8[:, :], v).then_inc(co.s_dv)
                co.dv.wait_ge(tok)
                tok = co.dv.match_replace(o, m8[:, :], v, -3.3e38).then_inc(co.s_dv)
                if r == 3:
                    yield
            s0 = sc[:, 0, 0:nk]
            co.dv.wait_ge(tok)
            tok = co.dv.tensor_scalar(s0, s0, -3.2e38, -BIG, ALU.is_gt, ALU.mult).then_inc(co.s_dv)
            co.dv.wait_ge(tok)
            tok = co.dv.tensor_tensor(s0, s0, neg, ALU.min).then_inc(co.s_dv)
            Lv = L[:, :, 0:nk]
            co.dv.wait_ge(tok, dep["b1"], fe)
            tok = co.dv.tensor_tensor(Lv, b1[:, :, 256 - nk:256], s0.unsqueeze(1).to_broadcast([P, 8, nk]), ALU.add).then_inc(co.s_dv)
            yield
            lt = []
            for g in range(4):
                b = next_bank(co)
                co.pe.wait_ge(dep['ckvt'], b.drained)
                for h in (2 * g, 2 * g + 1):
                    co.pe.wait_ge(ql[h // 4])
                    m = co.pe.matmul(b.ap[:, (h % 2) * nk:(h % 2 + 1) * nk], qlt[:, h, :], ckvt[:, 0, 0:nk], skip_group_check=True, start=True, stop=True).then_inc(co.s_pe, h % 2 == 1)
                v = L[:, 2 * g:2 * g + 2, 0:nk]
                co.dv.wait_ge(m, tok)
                b.drained = co.dv.tensor_tensor(v, b.ap[:, 0:2 * nk].rearrange("p (h n) -> p h n", h=2), v, ALU.add).then_inc(co.s_dv)
                lt.append(b.drained)
            qlfree = m
            co.dv.wait_ge(tuple(lt))
            tok = co.dv.tensor_reduce(mx[:, :], Lv, AX, ALU.max).then_inc(co.s_dv)
            co.dv.wait_ge(tok)
            tok = co.dv.tensor_scalar(mx[:, :], mx[:, :], -1.0, None, ALU.mult).then_inc(co.s_dv)
            yield
            es = []
            co.ac.wait_ge(tok, smfree, fe)
            for h in range(8):
                es.append(co.ac.activation(L[:, h, 0:nk], L[:, h, 0:nk], ACT.Exp, bias=mx[:, h:h + 1], accum_out=sm[:, t, h:h + 1]).then_inc(co.s_ac))
            co.dv.wait_ge(tuple(es))
            rc = co.dv.reciprocal(sm[:, t, :], sm[:, t, :]).then_inc(co.s_dv)
            yb = next_bank(co, hold=True)
            for g in range(2):
                cps = []
                for s in range(t + 1):
                    b = next_bank(co)
                    co.pe.wait_ge(b.drained)
                    for h in range(4):
                        co.pe.wait_ge(es[4 * g + h])
                        m = co.pe.transpose(b.ap[:, h * P:(h + 1) * P], L[:, 4 * g + h, s * P:(s + 1) * P], ident(co, L[:, 4 * g + h, s * P:(s + 1) * P])).then_inc(co.s_pe, h == 3)
                    o, i = pt[:, s, :, :], b.ap.rearrange("p (h n) -> p h n", h=4)
                    q = co.ac if s == 0 else co.dv
                    q.wait_ge(m, ptfree, fe)
                    b.drained = q.copy(o, i).then_inc(co.s_ac if q is co.ac else co.s_dv)
                    cps.append(b.drained)
                yield
                b = next_bank(co)
                co.pe.wait_ge(dep['ckv'], b.drained)
                for s in range(t + 1):
                    co.pe.wait_ge(cps[s])
                    m = co.pe.matmul(b.ap, ckv[:, s, :], pt[:, s, :, :].rearrange("p h n -> p (h n)"), start=s == 0, stop=s == t, skip_group_check=True).then_inc(co.s_pe, s == t)
                ptfree = m
                co.dv.wait_ge(m, olfree, fe)
                b.drained = c = co.dv.tensor_copy(olt[:, :, :], b.ap.rearrange("p (h n) -> p h n", h=4)).then_inc(co.s_dv)
                yield
                for h in range(4):
                    hh = 4 * g + h
                    co.pe.wait_ge(c, yb.drained, dep["w"])
                    m = co.pe.matmul(yb.ap[:, hh * 64:(hh + 1) * 64], olt[:, h, :], wuv[:, HP[hh], :], skip_group_check=True, start=True, stop=True).then_inc(co.s_pe, h == 3)
                olfree = m
            Lfree = m
            scfree = m
            co.dv.wait_ge(m, rc, fe)
            for g in range(2):
                yb.drained = co.dv.tensor_tensor(ya[:, t, :].rearrange("p (a b d) -> p b a d", a=4, b=2)[:, g], yb.ap.rearrange("p (b a d) -> p b a d", a=4, b=2)[:, g], sm[:, t, 4 * g:4 * g + 4].unsqueeze(2).to_broadcast([P, 4, 64]), ALU.mult).then_inc(co.s_dv)
            yb.held = False
            dep[f"ya{t}"] = yb.drained
            yield
        ydep[0] = to_t(co, lambda t, k: ya[:, t, k * P:(k + 1) * P], 4, yt[0], (dep["ya0"], dep["ya1"]), fe)

    spawn(co, dsa())

    def on_cc(banks, tok):
        i = turn[0] % 2
        turn[0] += 1
        dep["cc"] = (i, pair(co, tk[i], banks, tok, 0, 512, tkfree[i]))

    def conv_z(banks, tok):
        i, ctok = dep["cc"]
        got = []
        co.dv.wait_ge(tok, ctok, fe)
        for k, b in enumerate(banks):
            c = tk[i][:, k, :].rearrange("p (k n) -> p k n", k=2)
            b.drained = co.dv.tensor_tensor(zt[:, 2 * k:2 * k + 2, 2:258], b.ap.rearrange("p (k n) -> p k n", k=2), c, ALU.mult).then_inc(co.s_dv)
            got.append(b.drained)
        tkfree[i] = got[-1]
        got.append(co.dv.memset(zt[:, :, 0:2], 0.0).then_inc(co.s_dv))
        b = next_bank(co)
        co.pe.wait_ge(dep["w"], b.drained)
        m = co.pe.transpose(b.ap[:, 0:12], cw[:, :], ident(co, cw[:, :])).then_inc(co.s_pe)
        co.dv.wait_ge(m)
        b.drained = co.dv.tensor_copy(cwt[:, :], b.ap[:, 0:12]).then_inc(co.s_dv)
        dep["z"] = (got, b.drained)

    def conv_b(banks, tok):
        def gen():
            hi, lo = yt[2]
            got, out = [], []
            co.dv.wait_ge(tok, dep["y"])
            for k, b in enumerate(banks):
                v = conv_y[:, 2 * k:2 * k + 2, :]
                b.drained = co.dv.tensor_tensor(v, b.ap.rearrange("p (k n) -> p k n", k=2), v, ALU.mult).then_inc(co.s_dv)
                got.append(b.drained)
            yield
            co.ac.wait_ge(fe)
            for k in range(2):
                h, v = hi[:, 2 * k:2 * k + 2, :], conv_y[:, 2 * k:2 * k + 2, :]
                co.ac.wait_ge(got[k])
                a = co.ac.activation(h, v, ACT.Copy).then_inc(co.s_ac)
                co.dv.wait_ge(a)
                out.append((a, co.dv.tensor_tensor(lo[:, 2 * k:2 * k + 2, :], v, h.bitcast(F32), ALU.subtract).then_inc(co.s_dv)))
            ydep[2] = out
        spawn(co, gen())

    def conv():
        yield
        co.dv.wait_ge(dep['z'], fe)
        for k in range(4):
            a = co.dv.tensor_scalar(conv_y[:, k, :], zt[:, k, 2:258], cwt[:, 8 + k:9 + k], None, ALU.mult).then_inc(co.s_dv)
            co.dv.wait_ge(a)
            a = co.dv.scalar_tensor_tensor(conv_y[:, k, :], zt[:, k, 1:257], cwt[:, 4 + k:5 + k], conv_y[:, k, :], ALU.mult, ALU.add).then_inc(co.s_dv)
            co.dv.wait_ge(a)
            a = co.dv.scalar_tensor_tensor(conv_y[:, k, :], zt[:, k, 0:256], cwt[:, k:k + 1], conv_y[:, k, :], ALU.mult, ALU.add).then_inc(co.s_dv)
        dep["y"] = a

    gemm_t(co, xt, co.xdep, w, 3272, 512, on_cc)
    gemm_t(co, xt, co.xdep, w, 3784, 512, conv_z)
    spawn(co, conv())
    gemm_t(co, xt, co.xdep, w, 2760, 512, conv_b)

    def on_qs(banks, tok):
        dep["qs"] = columns_of(co, qst, banks, tok, 0.125, fe)

    def on_ks(banks, tok):
        dep["ks"] = columns_of(co, kst, banks, tok, 1.0, fe)

    def on_vs(banks, tok):
        dep["vs"] = pair(co, vs[:, :, :], banks, tok, 0, 512, fe)

    gemm_t(co, xt, co.xdep, w, 1224, 512, on_qs)
    gemm_t(co, xt, co.xdep, w, 1736, 512, on_ks)
    gemm(co, xt, co.xdep, w, 2248, 512, on_vs)
    halves = [[v[:, 0, :], v[:, 1, :]] for v in tk]
    mod_groups(co, mod_part(l, 1), (halves[0], halves[1], [tkfree[0]] * 2, [tkfree[1]] * 2), quiet=False)
    flush(co)
    co.base = low
    yt[1] = (alloc(co, [P, 4, 256], F32R), alloc(co, [P, 4, 256], F32R))
    sg = alloc(co, [P, 2, 3, D])
    bb = [alloc(co, [P, 512]) for _ in range(2)]
    low = co.base
    fe2 = counts(co)
    tkfree[:] = [fe2, fe2]
    zs = [alloc(co, [P, 8, P]) for _ in range(2)]
    sp11, sp0 = alloc(co, [P, 8, P]), alloc(co, [P, 8, P])
    tmp = co.lg[:, :].rearrange("p (t n) -> p t n", t=2)
    cs = co.cst

    def stick():
        sp_done = {}
        zfree = {0: fe2, 1: fe2}
        tfree = {0: fe2, 1: fe2}
        spfree = fe2
        yb = {}
        for i, (s, t) in enumerate(((0, 0), (1, 1), (0, 1))):
            z = zs[i % 2]
            sp = sp11 if (s, t) == (1, 1) else sp0
            toks = []
            for g in range(2):
                b = next_bank(co)
                r = slice(64 * g, 64 * g + 64)
                co.pe.wait_ge(dep['qs'], dep['ks'], b.drained)
                for h in range(4):
                    m = co.pe.matmul(b.ap[:, h * P:(h + 1) * P], kst[r, h, s * P:(s + 1) * P], qst[r, h, t * P:(t + 1) * P], skip_group_check=True, start=True, stop=True).then_inc(co.s_pe, h == 3)
                zg, spg, tg = z[:, 4 * g:4 * g + 4, :], sp[:, 4 * g:4 * g + 4, :], tmp[:, g, :].rearrange(
                    "p (h n) -> p h n", h=4)
                co.ac.wait_ge(m, zfree[i % 2])
                b.drained = c = co.ac.activation(zg, b.ap.rearrange("p (h n) -> p h n", h=4), ACT.Copy).then_inc(co.s_ac)
                co.dv.wait_ge(c, tfree[g])
                a = co.dv.scalar_tensor_tensor(tg, zg, -1.0, zg, ALU.mult, ALU.max).then_inc(co.s_dv)
                co.ac.wait_ge(a)
                a = co.ac.activation(tg, tg, ACT.Exp, scale=-1.0).then_inc(co.s_ac)
                co.ac.wait_ge(a)
                a = co.ac.activation(tg, tg, ACT.Ln, bias=1.0).then_inc(co.s_ac)
                co.dv.wait_ge(a, spfree)
                a = co.dv.scalar_tensor_tensor(spg, zg, 0.0, tg, ALU.max, ALU.add).then_inc(co.s_dv)
                tfree[g] = a
                if s == t:
                    co.dv.wait_ge(a)
                    a = co.dv.tensor_tensor(spg, spg, cs[:, C_SM:C_SM + P].unsqueeze(1).to_broadcast([P, 4, P]), ALU.mult).then_inc(co.s_dv)
                    co.dv.wait_ge(c, a)
                    c = co.dv.tensor_tensor(zg, zg, cs[:, C_SN:C_SN + P].unsqueeze(1).to_broadcast([P, 4, P]), ALU.add).then_inc(co.s_dv)
                toks.append((a, c))
            sp_done[(s, t)] = toks
            yield
            yield
            at = []
            for g in range(2):
                b = next_bank(co)
                f = lambda v: v[:, 4 * g:4 * g + 4, :].rearrange("p h n -> p (h n)")
                co.pe.wait_ge(toks[g], b.drained)
                m = co.pe.matmul(b.ap, cs[:, C_TRI:C_TRI + P], f(sp), stop=s == t, skip_group_check=True, start=True).then_inc(co.s_pe)
                if s != t:
                    co.pe.wait_ge(sp_done[(1, 1)][g])
                    m = co.pe.matmul(b.ap, cs[:, C_ONE:C_ONE + P], f(sp11), start=False, skip_group_check=True, stop=True).then_inc(co.s_pe)
                spfree = m
                zg = z[:, 4 * g:4 * g + 4, :]
                co.dv.wait_ge(m, toks[g])
                b.drained = a = co.dv.tensor_tensor(zg, zg, b.ap.rearrange("p (h n) -> p h n", h=4), ALU.subtract).then_inc(co.s_dv)
                co.ac.wait_ge(a)
                at.append(co.ac.activation(zg, zg, ACT.Exp).then_inc(co.s_ac))
            yield
            if t not in yb:
                yb[t] = next_bank(co, hold=True)
            first = s == t
            last = (s, t) != (1, 1)
            co.pe.wait_ge(dep['vs'], yb[t].drained)
            for h in range(8):
                co.pe.wait_ge(at[h // 4])
                m = co.pe.matmul(yb[t].ap[:, HP[h] * 64:(HP[h] + 1) * 64], z[:, h, :], vs[:, s, HP[h] * 64:(HP[h] + 1) * 64], start=first and h == 0, stop=last, skip_group_check=True).then_inc(co.s_pe, h == 7)
            zfree[i % 2] = m
            if last:
                o = tk[0][:, t, :]
                co.ac.wait_ge(m, tkfree[0])
                yb[t].drained = c = co.ac.activation(o, yb[t].ap, ACT.Copy).then_inc(co.s_ac)
                yb[t].held = False
                dep[f"yb{t}"] = c
            yield
        ydep[1] = to_t(co, lambda t, k: tk[0][:, t, k * P:(k + 1) * P], 4, yt[1], (dep["yb0"], dep["yb1"]), fe2)

    spawn(co, stick())
    bfree = [fe2, fe2]
    sgd = {}
    for i in range(3):
        for c in range(2):
            n = 2 * i + c
            co.po.wait_ge(bfree[n % 2])
            bd = load_small(co, bb[n % 2][:, :], A["b_gate"][l, i:i + 1, c * 512:(c + 1) * 512].to_broadcast([P, 512]))

            def evac(banks, tok):
                for t in range(2):
                    o = sg[:, t, i, c * 512:(c + 1) * 512]
                    co.dv.wait_ge(tok, bd, fe2)
                    banks[t].drained = a = co.dv.tensor_tensor(o, banks[t].ap, bb[n % 2][:, :], ALU.add).then_inc(co.s_dv)
                    co.ac.wait_ge(a)
                    sgd[(i, c, t)] = co.ac.activation(o, o, ACT.Sigmoid).then_inc(co.s_ac)
                bfree[n % 2] = a
            gemm(co, xt, co.xdep, w, 4296 + n * 512, 512, evac)
    flush(co)
    co.xtfree = pe_mark(co)
    co.base = low
    mg, y = alloc(co, [P, 2, D]), co.y
    assert co.base <= co.top - 8192
    fe3 = counts(co)
    load_ln(co, l, 1, fe3)
    co.base = tkbase
    co.mem = alloc(co, [P, 2, D])
    co.base = tkbase
    co.po.wait_ge(fe3)
    co.memdep = load_small(co, co.mem[:, :, :], A["mem"][0].rearrange("(t p) d -> p t d", p=P))
    mgd = [[None, None], [None, None]]
    for i in (0, 2, 1):
        for c in range(2):
            def evac(banks, tok):
                for t in range(2):
                    s, o = sg[:, t, i, c * 512:(c + 1) * 512], mg[:, t, c * 512:(c + 1) * 512]
                    co.dv.wait_ge(tok, sgd[(i, c, t)], fe3)
                    a = co.dv.tensor_tensor(o if i == 0 else s, banks[t].ap, s, ALU.mult).then_inc(co.s_dv)
                    banks[t].drained = a
                    if i:
                        co.dv.wait_ge(a, mgd[c][t])
                        a = co.dv.tensor_tensor(o, o, s, ALU.add).then_inc(co.s_dv)
                    mgd[c][t] = a
            gemm(co, yt[i], ydep[i], A["w_branch"][l, i], c * 512, 512, evac)
    mdep = to_t(co, lambda t, k: mg[:, t, k * P:(k + 1) * P], 8, xt, tuple(mgd[0] + mgd[1]), co.xtfree)
    got = [None] * 4
    res = residual(co, y, ALPHA, got, fe3)
    for c in range(2):
        gemm(co, xt, mdep, A["w_mix_out"][l], c * 512, 512, res(c * 512, 512))
    co.xtfree = pe_mark(co)
    spawn(co, layer_norm(co, y, got[0:2], got[2:4], 1e-5, nxt))
    co.base = start


def cross(co, l, nxt):
    A = co.A
    start = co.base
    kt, v = alloc(co, [P, 4, 256]), alloc(co, [P, 2, 512])
    kept = co.base
    mem, md = co.mem, co.memdep
    co.base = start + 16384 + 8192
    mh, ml = alloc(co, [P, 8, 256], F32R), alloc(co, [P, 8, 256], F32R)
    fe = counts(co)
    mdep = to_t(co, lambda t, k: mem[:, t, k * P:(k + 1) * P], 8, (mh, ml), md, fe)
    dep = {}
    w = A["xa_wkv"][l]

    def on_k(banks, tok):
        dep["k"] = columns_of(co, kt, banks, tok, 1.0, fe)

    def on_v(banks, tok):
        dep["v"] = pair(co, v[:, :, :], banks, tok, 0, 512, fe)

    gemm_t(co, (mh, ml), mdep, w, 0, 512, on_k)
    gemm(co, (mh, ml), mdep, w, 512, 512, on_v)
    flush(co)
    co.base = kept
    qt, L, pt = alloc(co, [P, 4, 256]), alloc(co, [P, 2, 4, 256]), alloc(co, [P, 2, 4, 256])
    y, mx, sm = co.y, alloc(co, [P, 2, 4]), alloc(co, [P, 2, 4])
    mt = mod_tiles(co)
    oh, ol = alloc(co, [P, 4, 256], F32R), alloc(co, [P, 4, 256], F32R)
    fe = counts(co)

    def on_q(banks, tok):
        dep["q"] = columns_of(co, qt, banks, tok, 128 ** -0.5, fe)

    gemm_t(co, (co.xh, co.xl), co.xdep, A["xa_wq"][l], 0, 512, on_q)
    co.xtfree = pe_mark(co)
    cps, nm = {}, {}
    for t in range(2):
        sb, lt = [], []
        for g in range(2):
            b = next_bank(co)
            sb.append(b)
            co.pe.wait_ge(dep['q'], dep['k'], b.drained)
            for h in (2 * g, 2 * g + 1):
                m = co.pe.matmul(b.ap[:, (h % 2) * 256:(h % 2 + 1) * 256], qt[:, h, t * P:(t + 1) * P], kt[:, h, :], skip_group_check=True, start=True, stop=True).then_inc(co.s_pe, h % 2 == 1)
            co.dv.wait_ge(m, fe)
            a = co.dv.tensor_reduce(mx[:, t, 2 * g:2 * g + 2], b.ap.rearrange("p (h n) -> p h n", h=2), AX, ALU.max).then_inc(co.s_dv)
            co.dv.wait_ge(a)
            lt.append(co.dv.tensor_scalar(mx[:, t, 2 * g:2 * g + 2], mx[:, t, 2 * g:2 * g + 2], -1.0, None, ALU.mult).then_inc(co.s_dv))
        es = []
        for h in range(4):
            b = sb[h // 2]
            co.ac.wait_ge(lt[h // 2], fe)
            b.drained = co.ac.activation(L[:, t, h, :], b.ap[:, (h % 2) * 256:(h % 2 + 1) * 256], ACT.Exp, bias=mx[:, t, h:h + 1], accum_out=sm[:, t, h:h + 1]).then_inc(co.s_ac)
            es.append(b.drained)
        co.dv.wait_ge(tuple(es))
        a = co.dv.reciprocal(sm[:, t, :], sm[:, t, :]).then_inc(co.s_dv)
        co.dv.wait_ge(a)
        nm[t] = [co.dv.tensor_scalar(L[:, t, h, :], L[:, t, h, :], sm[:, t, h:h + 1], None, ALU.mult).then_inc(co.s_dv) for h in range(4)]
    mod_groups(co, mod_part(l, 2), mt)
    for t in range(2):
        for s in range(2):
            b = next_bank(co)
            co.pe.wait_ge(b.drained)
            for h in range(4):
                co.pe.wait_ge(nm[t][h])
                m = co.pe.transpose(b.ap[:, h * P:(h + 1) * P], L[:, t, h, s * P:(s + 1) * P], ident(co, L[:, t, h, s * P:(s + 1) * P])).then_inc(co.s_pe, h == 3)
            q = co.ac if s == 0 else co.dv
            q.wait_ge(m, fe)
            b.drained = q.copy(pt[:, s, :, t * P:(t + 1) * P], b.ap.rearrange("p (h n) -> p h n", h=4)).then_inc(co.s_ac if q is co.ac else co.s_dv)
            cps[(s, t)] = b.drained
    odep = []
    for g in range(2):
        b = next_bank(co)
        co.pe.wait_ge(dep['v'], b.drained)
        for h in (2 * g, 2 * g + 1):
            for s in range(2):
                co.pe.wait_ge(cps[s, 0], cps[s, 1])
                m = co.pe.matmul(b.ap[:, (h % 2) * 256:(h % 2 + 1) * 256], v[:, s, h * P:(h + 1) * P], pt[:, s, h, :], start=s == 0, stop=s == 1, skip_group_check=True).then_inc(co.s_pe, s == 1)
        ps = b.ap.rearrange("p (h n) -> p h n", h=2)
        co.ac.wait_ge(m, fe)
        a = co.ac.activation(oh[:, 2 * g:2 * g + 2, :], ps, ACT.Copy).then_inc(co.s_ac)
        co.dv.wait_ge(m, a)
        c = co.dv.tensor_tensor(ol[:, 2 * g:2 * g + 2, :], ps, oh[:, 2 * g:2 * g + 2, :].bitcast(F32), ALU.subtract).then_inc(co.s_dv)
        b.drained = (a, c)
        odep.append((a, c))
    got = [None] * 4
    res = residual(co, y, ALPHA, got, fe)
    for c in range(2):
        gemm(co, (oh, ol), odep, A["xa_wo"][l], c * 512, 512, res(c * 512, 512))
    spawn(co, layer_norm(co, y, got[0:2], got[2:4], 1e-5, nxt))
    mod_groups(co, mod_part(l, 3), mt)
    co.base = start


"""The second block. A stream is one of x and ctx: its tile, when it stands, who read it last."""


def second_tiles(co):
    co.top -= 8192
    co.ctx_t = alloc(co, [P, 2, D])
    co.po.wait_ge(counts(co))
    co.ready = [None, load_small(co, co.ctx_t[:, :, :], co.A["ctx_2"][0].rearrange("(t p) d -> p t d", p=P))]
    co.tile = [co.x, co.ctx_t]
    co.gb, co.gbfree, co.pnfree, co.yfree = co.lg, None, None, None


def begin(co):
    fe = counts(co)
    co.ready[0] = co.xready
    co.pn = co.lb
    co.gbfree, co.pnfree, co.yfree = fe, fe, fe


def prenorm(co, l, s, f, y=None):
    src, rs = co.tile[s], co.rs
    yfree = counts(co) if y is not None else co.yfree
    y2, y = y, co.y if y is None else y
    if s == 1 or l == 1 and f == 1:
        co.gaindep = mod_gain(co, l, f)
    norm = []
    co.ac.wait_ge(co.ready[s], yfree, co.rsfree)
    for t in range(2):
        a = co.ac.activation(y[:, t, :], src[:, t, :], ACT.Square, accum_out=rs[:, t, 0:1]).then_inc(co.s_ac)
        co.dv.wait_ge(a)
        a = co.dv.tensor_scalar(rs[:, t, 0:1], rs[:, t, 0:1], 1.0 / D, 1e-6, ALU.mult, ALU.add).then_inc(co.s_dv)
        co.po.wait_ge(a)
        a = co.po.tensor_tensor(rs[:, t, 1:2], rs[:, t, 0:1], minus_half(co, rs[:, t, 0:1]), ALU.pow).then_inc(co.s_po)
        co.dv.wait_ge(a)
        norm.append(co.dv.tensor_scalar(y[:, t, :], src[:, t, :], rs[:, t, 1:2], None, ALU.mult).then_inc(co.s_dv))
    co.rsfree = norm[1]
    yield
    out = []
    hi, lo, tmp = co.xh, co.xl, co.pn
    wfree = [co.pnfree, co.pnfree]
    for k0 in range(0, 8, 2):
        b = next_bank(co)
        co.pe.wait_ge(b.drained)
        for k in (0, 1):
            for t in range(2):
                co.pe.wait_ge(norm[t])
                m = co.pe.transpose(b.ap[:, k * 256 + t * P:k * 256 + (t + 1) * P], y[:, t, (k0 + k) * P:(k0 + k + 1) * P], ident(co, y[:, t, (k0 + k) * P:(k0 + k + 1) * P])).then_inc(co.s_pe, k == 1 and t == 1)
        j = k0 // 2 % 2
        w = tmp[:, 512 * j:512 * j + 512]
        co.dv.wait_ge(m, co.gaindep, wfree[j])
        for k in (0, 1):
            sc, sh = co.mgain[:, l, f, k0 + k, s:s + 1], co.mc[:, l, 3 * f, k0 + k, s:s + 1]
            v = co.dv.tensor_scalar(w[:, k * 256:(k + 1) * 256], b.ap[:, k * 256:(k + 1) * 256], sc, sh, ALU.mult, ALU.add).then_inc(co.s_dv)
        b.drained = v
        w2 = w.rearrange("p (k n) -> p k n", k=2)
        co.ac.wait_ge(v, co.xtfree)
        a = co.ac.activation(hi[:, k0:k0 + 2, :], w2, ACT.Copy).then_inc(co.s_ac)
        co.dv.wait_ge(a, co.xtfree)
        v = co.dv.tensor_tensor(lo[:, k0:k0 + 2, :], w2, hi[:, k0:k0 + 2, :].bitcast(F32), ALU.subtract).then_inc(co.s_dv)
        wfree[j] = v
        out.append(v)
    co.pnfree = v
    if y2 is None:
        co.yfree = pe_mark(co)
    co.xdep = out


def gate_rows(co, l, s, f):
    co.po.wait_ge(co.gated_at[l, f, 0], co.gated_at[l, f, 1], co.gbfree)
    co.gbdep = load_small(co, co.gb[:, :], co.A["gates"][l, f, s:s + 1, :].to_broadcast([P, D]))


def gated(co, s, gw, gwfree):
    got = []
    x = co.tile[s]

    def make(c0, n):
        def evac(banks, tok):
            for t in range(2):
                g, p = co.gb[:, c0:c0 + n], banks[t].ap[:, 0:n]
                w, o = gw[:, t, c0:c0 + n], x[:, t, c0:c0 + n]
                co.dv.wait_ge(tok, co.gbdep, gwfree)
                a = co.dv.tensor_tensor(w, p, g, ALU.mult).then_inc(co.s_dv)
                banks[t].drained = a
                co.dv.wait_ge(a, co.ready[s])
                got.append(co.dv.tensor_tensor(o, o, w, ALU.add).then_inc(co.s_dv))
        return evac
    return make, got


def ffn2(co, l, s, normed, then):
    A = co.A
    start = co.base
    if not normed:
        spawn(co, prenorm(co, l, s, 1))
    flush(co)
    gate_rows(co, l, s, 1)
    gw = alloc(co, [P, 2, D])
    make, got = gated(co, s, gw, counts(co))
    ffn(co, A["ffn_w_in_2"][l], A["ffn_w_out_2"][l], make, prenorm(co, *then) if then else None)
    co.gbfree = tuple(got)
    co.ready[s] = tuple(got)
    co.base = start


def out_proj(co, l, s, ydep, then):
    flush(co)
    dep = to_t(co, lambda t, k: co.y[:, t, k * P:(k + 1) * P], 8, (co.xh, co.xl), ydep, co.xtfree)
    co.yfree = pe_mark(co)
    gate_rows(co, l, s, 0)
    mark = co.base
    gw = alloc(co, [P, 2, D])
    make, got = gated(co, s, gw, counts(co))
    if then is not None:
        following = prenorm(co, *then)
        next(following)
    for c in range(2):
        gemm(co, (co.xh, co.xl), dep, co.A["w_out_2"][l], c * 512, 512, make(c * 512, 512))
    co.xtfree = pe_mark(co)
    co.gbfree = tuple(got)
    co.ready[s] = tuple(got)
    if then is not None:
        co.bg.append(following)
    co.base = mark


def groups(co, v, w, n, g, gain, dep, wfree):
    a = v.shape[1]
    ss, ss2 = co.gs[:, 0, 0:a * g], co.gs[:, 1, 0:a * g]
    v3 = ss.rearrange("p (a g) -> p a g", a=a)
    co.ac.wait_ge(dep, wfree, co.gsfree)
    tok = co.ac.activation(w, v, ACT.Square).then_inc(co.s_ac)
    co.dv.wait_ge(dep, tok, co.gsfree)
    tok = co.dv.tensor_reduce(v3, w, AX, ALU.add).then_inc(co.s_dv)
    co.dv.wait_ge(tok)
    tok = co.dv.tensor_scalar(ss, ss, 1.0 / n, 1e-6, ALU.mult, ALU.add).then_inc(co.s_dv)
    co.po.wait_ge(tok)
    tok = co.po.tensor_tensor(ss2, ss, minus_half(co, ss), ALU.pow).then_inc(co.s_po)
    r3 = ss2.rearrange("p (a g) -> p a g", a=a)
    co.dv.wait_ge(tok)
    for i in range(a):
        b = co.dv.tensor_tensor(v[:, i], v[:, i], r3[:, i].unsqueeze(2).to_broadcast([P, g, n]), ALU.mult).then_inc(co.s_dv)
        co.dv.wait_ge(b)
        b = co.dv.tensor_tensor(v[:, i], v[:, i], gain.unsqueeze(1).to_broadcast([P, g, n]), ALU.mult).then_inc(co.s_dv)
    co.gsfree = b
    return b


def rope(co, v, w, w2, g, dep):
    for t in range(2):
        c = co.rt[:, t, 0:64].unsqueeze(1).to_broadcast([P, g, 64])
        co.dv.wait_ge(dep)
        a = co.dv.tensor_tensor(w[:, t], v[:, t], c, ALU.mult).then_inc(co.s_dv)
        for h in range(2):
            o = w2[:, t].rearrange("p g (a h n) -> p g a h n", a=2, h=2)[:, :, :, h]
            i = v[:, t].rearrange("p g (a h n) -> p g a h n", a=2, h=2)[:, :, :, 1 - h]
            s = co.rt[:, t, 64:128].rearrange("p (a h n) -> p a h n", a=2, h=2)[:, :, h].unsqueeze(1)\
                .to_broadcast([P, g, 2, 16])
            co.dv.wait_ge(dep)
            b = co.dv.tensor_tensor(o, i, s, ALU.mult).then_inc(co.s_dv)
        co.dv.wait_ge(a, b)
        a = co.dv.tensor_tensor(v[:, t], w[:, t], w2[:, t], ALU.add).then_inc(co.s_dv)
    co.gsfree = a
    return a


def even(co):
    A, l = co.A, 0
    start = co.base
    W = A["ev_w_in_2"][0]
    dkt, dv = alloc(co, [P, 4, 512]), alloc(co, [P, 4, 512])
    knt, krt, mv = alloc(co, [P, 4, 512]), alloc(co, [64, 512]), alloc(co, [P, 4, 512])
    dqt, qnt, qrt = alloc(co, [P, 4, 256]), alloc(co, [P, 4, 256]), alloc(co, [64, 4, 256])
    co.rt, co.gs = alloc(co, [P, 2, P]), alloc(co, [P, 2, 32])
    gn = alloc(co, [P, 1152])
    lam = alloc(co, [P, 4])
    low = co.base
    tks = [alloc(co, [P, 2, 512]) for _ in range(2)]
    w1, w2 = alloc(co, [P, 2, 512]), co.pn[:, :].rearrange("p (t n) -> p t n", t=2)
    cqh, cql = alloc(co, [P, 2, 256], F32R), alloc(co, [P, 2, 256], F32R)
    ckh, ckl = alloc(co, [P, 1, 256], F32R), alloc(co, [P, 1, 256], F32R)
    lv = co.gb[:, 512:768].rearrange("p (a n) -> p a n", n=64)
    fe = counts(co)
    co.gsfree = fe
    co.po.wait_ge(fe)
    gd, at = [load_small(co, co.rt[:, :, :], A["rope"][:, :, :])], 0
    gains = {}
    for n, w in (("da_q_g_2", 64), ("da_k_g_2", 64), ("mla_q_a_g_2", 256), ("mla_kv_a_g_2", 128),
                 ("mla_q_g_2", 192), ("mla_k_g_2", 128), ("mla_kr_g_2", 64), ("da_out_g_2", 128)):
        gains[n] = gn[:, at:at + w]
        co.po.wait_ge(fe)
        gd.append(load_small(co, gn[:, at:at + w], A[n].to_broadcast([P, w])))
        at += w
    co.po.wait_ge(fe)
    for i, n in enumerate(("da_lq1_2", "da_lk1_2", "da_lq2_2", "da_lk2_2")):
        gd.append(load_small(co, lv[:, i, :], A[n].to_broadcast([P, 64])))
    gd = tuple(gd)
    free = {"tk": [fe, fe]}
    busy, turn = [False, False], [0]

    def take():
        i = turn[0] % 2
        turn[0] += 1
        while busy[i]:
            advance(co)
        busy[i] = True
        return i, tks[i]

    def give(i, mark):
        free["tk"][i], busy[i] = mark, False

    dep = {}

    def view(v, n, w):
        return v[:, :, 0:n * w].rearrange("p t (g n) -> p t g n", n=w)

    def project(s):
        xt = (co.xh, co.xl)
        roped = s == 0
        k0 = 256 if s == 0 else 0
        ks = slice(k0, k0 + 256)
        kfree = None if s == 1 else ()

        def on_heads(gname, dst, key, cols):
            def evac(banks, tok):
                def gen():
                    a = pair(co, tk[:, :, :], banks, tok, 0, 512, free["tk"][i])
                    yield
                    a = groups(co, view(tk, 8, 64), view(w1, 8, 64), 64, 8, gains[gname], (a, gd), fe)
                    if roped:
                        a = rope(co, view(tk, 8, 64), view(w1, 8, 64), view(w2, 8, 64), 8, a)
                    yield
                    dep[key, s] = t32(co, lambda k, t: tk[:, t, k * P:(k + 1) * P], 4, dst[:, :, cols], a,
                                           (fe, dep.get("qfree")))
                    give(i, pe_mark(co))
                i, tk = take()
                spawn(co, gen())
            return evac

        def on_dv(banks, tok):
            for t in range(2):
                o = dv[:, k0 // P + t, :]
                q = co.ac if t else co.dv
                q.wait_ge(tok, fe)
                banks[t].drained = q.copy(o, banks[t].ap).then_inc(co.s_ac if q is co.ac else co.s_dv)
                dep["dv", s, t] = banks[t].drained

        def on_mla(banks, tok):
            def gen():
                a = pair(co, tk[:, :, 0:448], banks, tok, 0, 448, free["tk"][i])
                yield
                c = groups(co, tk[:, :, 0:256].unsqueeze(2), w1[:, :, 0:256].unsqueeze(2), 256, 1,
                                gains["mla_q_a_g_2"], (a, gd), fe)
                d = groups(co, tk[:, :, 256:384].unsqueeze(2), w1[:, :, 256:384].unsqueeze(2), 128, 1,
                                gains["mla_kv_a_g_2"], (a, gd), fe)
                kr = tk[:, :, 384:448].unsqueeze(2)
                e = groups(co, kr, w1[:, :, 384:448].unsqueeze(2), 64, 1, gains["mla_kr_g_2"], (a, gd), fe)
                if roped:
                    e = rope(co, kr, w1[:, :, 384:448].unsqueeze(2), w2[:, :, 384:448].unsqueeze(2), 1, e)
                yield
                dep["cq"] = to_t(co, lambda t, k: tk[:, t, k * P:(k + 1) * P], 2, (cqh, cql), c,
                                      (fe, dep.get("cqfree")))
                dep["ck"] = to_t(co, lambda t, k: tk[:, t, 256:384], 1, (ckh, ckl), d, (fe, dep.get("cqfree")))
                dep["kr", s] = t32(co, lambda k, t: tk[:, t, 384:448], 1, krt[:, ks].unsqueeze(1), e, fe)
                give(i, pe_mark(co))
            i, tk = take()
            spawn(co, gen())

        def on_kv(c):
            def evac(banks, tok):
                def gen():
                    a = pair(co, tk[:, :, :], banks, tok, 0, 512, free["tk"][i])
                    yield
                    kn = tk[:, :, :].rearrange("p t (g n) -> p t g n", n=256)[:, :, :, 0:128]
                    k1 = w1[:, :, :].rearrange("p t (g n) -> p t g n", n=256)[:, :, :, 0:128]
                    e = groups(co, kn, k1, 128, 2, gains["mla_k_g_2"], (a, gd), fe)
                    for t in range(2):
                        v = tk[:, t, :].rearrange("p (g n) -> p g n", n=256)[:, :, 128:256]
                        o = mv[:, k0 // P + t, 256 * c:256 * c + 256].rearrange("p (g n) -> p g n", n=128)
                        co.ac.wait_ge(a, fe)
                        m = co.ac.activation(o, v, ACT.Copy).then_inc(co.s_ac)
                    dep["mv", s, c] = m
                    yield
                    dep["kn", s, c] = t32(co, lambda k, t: tk[:, t, 256 * k:256 * k + 128], 2,
                                               knt[:, 2 * c:2 * c + 2, ks], e, fe)
                    give(i, (pe_mark(co), m))
                i, tk = take()
                spawn(co, gen())
            return evac

        def on_q(c):
            def evac(banks, tok):
                def gen():
                    a = pair(co, tk[:, :, 0:384], banks, tok, 0, 384, free["tk"][i])
                    yield
                    e = groups(co, view(tk, 2, 192), view(w1, 2, 192), 192, 2, gains["mla_q_g_2"], (a, gd), fe)
                    if roped:
                        e = rope(co, *(view(v, 2, 192)[:, :, :, 128:192] for v in (tk, w1, w2)), 2, e)
                    yield
                    qf = (fe, dep.get("qfree"))
                    dep["qn", s, c] = t32(co, lambda k, t: tk[:, t, 192 * k:192 * k + 128], 2,
                                               qnt[:, 2 * c:2 * c + 2, :], e, qf)
                    dep["qr", s, c] = t32(co, lambda k, t: tk[:, t, 192 * k + 128:192 * k + 192], 2,
                                               qrt[:, 2 * c:2 * c + 2, :], e, qf)
                    give(i, pe_mark(co))
                i, tk = take()
                spawn(co, gen())
            return evac

        gemm(co, xt, co.xdep, W, 1536, 448, on_mla)
        gemm(co, xt, co.xdep, W, 512, 512, on_heads("da_k_g_2", dkt, "dk", ks))
        gemm(co, xt, co.xdep, W, 0, 512, on_heads("da_q_g_2", dqt, "dq", slice(0, 256)))
        gemm(co, (ckh, ckl), dep["ck"], A["mla_w_ukv_2"][0], 0, 512, on_kv(0))
        gemm(co, (cqh, cql), dep["cq"], A["mla_w_uq_2"][0], 0, 384, on_q(0))
        gemm(co, xt, co.xdep, W, 1024, 512, on_dv)
        co.xtfree = pe_mark(co)
        gemm(co, (ckh, ckl), dep["ck"], A["mla_w_ukv_2"][0], 512, 512, on_kv(1))
        gemm(co, (cqh, cql), dep["cq"], A["mla_w_uq_2"][0], 384, 384, on_q(1))
        dep["cqfree"] = pe_mark(co)
        flush(co)

    def lambdas():
        co.dv.wait_ge(gd)
        a = co.dv.tensor_scalar(gains["da_out_g_2"], gains["da_out_g_2"], 1.0 - (0.8 - 0.6 * math.exp(0.0)), None, ALU.mult).then_inc(co.s_dv)
        co.dv.wait_ge(gd)
        for i in range(2):
            a = co.dv.tensor_tensor(lv[:, 2 * i, :], lv[:, 2 * i, :], lv[:, 2 * i + 1, :], ALU.mult).then_inc(co.s_dv)
            co.dv.wait_ge(a, fe)
            a = co.dv.tensor_reduce(lam[:, i:i + 1], lv[:, 2 * i, :], AX, ALU.add).then_inc(co.s_dv)
        co.ac.wait_ge(a)
        a = co.ac.activation(lam[:, 0:2], lam[:, 0:2], ACT.Exp).then_inc(co.s_ac)
        co.dv.wait_ge(a)
        a = co.dv.tensor_tensor(lam[:, 2:3], lam[:, 1:2], lam[:, 0:1], ALU.subtract).then_inc(co.s_dv)
        co.dv.wait_ge(a)
        dep["lam"] = co.dv.tensor_scalar(lam[:, 2:3], lam[:, 2:3], -(0.8 - 0.6 * math.exp(0.0)), None, ALU.add).then_inc(co.s_dv)

    def attend(s, pr, at_, sm, mx, fe, done):
        nk = 512 if s == 0 else 256
        ns = nk // P
        streams = (1, 0) if s == 0 else (1,)
        y = co.y
        kdep = tuple(v for k, v in dep.items() if isinstance(k, tuple) and k[0] in ("dk", "dv", "kn", "kr", "mv")
                     and k[1] in streams)
        qdep = tuple(v for k, v in dep.items() if isinstance(k, tuple) and k[0] in ("dq", "qn", "qr")
                     and k[1] == s)
        pfree, afree, smfree = [fe] * 4, [fe] * 2, [fe] * 4
        items = [(t, h) for t in range(2) for h in range(8)]
        yb = {}
        st = {}
        rdep = {}
        for i in range(len(items) + 3):
            if 2 <= i < len(items) + 2 and items[i - 2][1] < 4:
                r = (i - 2) % 4
                p = pr[r]
                co.dv.wait_ge(st[i - 2])
                a = co.dv.reciprocal(mx[:, r, 2:4], mx[:, r, 2:4]).then_inc(co.s_dv)
                co.dv.wait_ge(a, dep["lam"])
                a = co.dv.tensor_scalar(mx[:, r, 3:4], mx[:, r, 3:4], lam[:, 2:3], None, ALU.mult).then_inc(co.s_dv)
                b = co.dv.tensor_scalar(p[:, 0, 0:nk], p[:, 0, 0:nk], mx[:, r, 2:3], None, ALU.mult).then_inc(co.s_dv)
                co.dv.wait_ge(a, b)
                st[i - 2] = co.dv.scalar_tensor_tensor(p[:, 0, 0:nk], p[:, 1, 0:nk], mx[:, r, 3:4], p[:, 0, 0:nk], ALU.mult, ALU.add).then_inc(co.s_dv)
            scores = []
            if i < len(items):
                t, h = items[i]
                ts_ = slice(t * P, (t + 1) * P)
                for j in range(2 if h < 4 else 1):
                    b = next_bank(co)
                    co.pe.wait_ge(kdep, qdep, b.drained)
                    if h < 4:
                        m = co.pe.matmul(b.ap[:, 0:nk], dqt[64 * j:64 * j + 64, h, ts_], dkt[64 * j:64 * j + 64, h, 0:nk], skip_group_check=True, start=True, stop=True).then_inc(co.s_pe)
                    else:
                        co.pe.matmul(b.ap[:, 0:nk], qnt[:, h - 4, ts_], knt[:, h - 4, 0:nk], stop=False, skip_group_check=True, start=True)
                        m = co.pe.matmul(b.ap[:, 0:nk], qrt[:, h - 4, ts_], krt[:, 0:nk], start=False, skip_group_check=True, stop=True).then_inc(co.s_pe)
                    scores.append((b, m))
            if 2 <= i < len(items) + 2:
                r, q = (i - 2) % 4, i % 2
                p, es = pr[r], st[i - 2]
                b = next_bank(co)
                co.pe.wait_ge(es, b.drained)
                for k in range(ns):
                    m = co.pe.transpose(b.ap[:, k * P:(k + 1) * P], p[:, 0, k * P:(k + 1) * P], ident(co, p[:, 0, k * P:(k + 1) * P])).then_inc(co.s_pe, k == ns - 1)
                pfree[r] = m
                smfree[r] = (m, es)
                co.ac.wait_ge(m, afree[q])
                b.drained = co.ac.activation(at_[q][:, 0:ns, :], b.ap[:, 0:nk].rearrange("p (k n) -> p k n", n=P), ACT.Copy).then_inc(co.s_ac)
                st[i - 2] = b.drained
            if i < len(items):
                t, h = items[i]
                r = i % 4
                p, es = pr[r], []
                sc = 64 ** -0.5 if h < 4 else 192 ** -0.5
                for j, (b, m) in enumerate(scores):
                    co.dv.wait_ge(m, smfree[r])
                    a = co.dv.tensor_reduce(mx[:, r, j:j + 1], b.ap[:, 0:nk], AX, ALU.max).then_inc(co.s_dv)
                    co.dv.wait_ge(a)
                    a = co.dv.tensor_scalar(mx[:, r, j:j + 1], mx[:, r, j:j + 1], -sc, None, ALU.mult).then_inc(co.s_dv)
                    acc = sm[:, t, h - 4:h - 3] if h >= 4 else mx[:, r, 2 + j:3 + j]
                    co.ac.wait_ge(a, pfree[r])
                    b.drained = co.ac.activation(p[:, j, 0:nk], b.ap[:, 0:nk], ACT.Exp, scale=sc, bias=mx[:, r, j:j + 1], accum_out=acc).then_inc(co.s_ac)
                    es.append(b.drained)
                st[i] = tuple(es)
            yield
            if i >= 3:
                t, h = items[i - 3]
                q = (i - 1) % 2
                if h % 4 == 0:
                    yb[h // 4] = next_bank(co, hold=True)
                b = yb[h // 4]
                v = dv if h < 4 else mv
                hh = h % 4
                co.pe.wait_ge(st[i - 3], b.drained)
                for k in range(ns):
                    m = co.pe.matmul(b.ap[:, hh * P:(hh + 1) * P], at_[q][:, k, :], v[:, k, hh * P:(hh + 1) * P], start=k == 0, stop=k == ns - 1, skip_group_check=True).then_inc(co.s_pe, k == ns - 1)
                afree[q] = m
                if h == 3:
                    o = y[:, t, 0:512]
                    co.ac.wait_ge(m, co.yfree)
                    b.drained = a = co.ac.activation(o, b.ap, ACT.Copy).then_inc(co.s_ac)
                    b.held = False
                    ov = y[:, t:t + 1, 0:512].rearrange("p t (g n) -> p t g n", n=P)
                    wv = co.gb[:, 0:512].unsqueeze(1).rearrange("p t (g n) -> p t g n", n=P)
                    a = groups(co, ov, wv, 128, 4, gains["da_out_g_2"], (a, gd), co.gbfree)
                    co.gbfree = a
                    done.append(a)
                if h == 7:
                    co.dv.wait_ge(m)
                    a = co.dv.reciprocal(sm[:, t, :], sm[:, t, :]).then_inc(co.s_dv)
                    co.dv.wait_ge(a, co.yfree)
                    b.drained = a = co.dv.tensor_tensor(y[:, t, 512:1024].rearrange("p (g n) -> p g n", n=P), b.ap.rearrange("p (g n) -> p g n", n=P), sm[:, t, :].unsqueeze(2).to_broadcast([P, 4, P]), ALU.mult).then_inc(co.s_dv)
                    b.held = False
                    done.append(a)
        dep["qfree"] = pe_mark(co)

    for s in (1, 0):
        flush(co)
        fe = counts(co)
        free["tk"] = [fe, fe]
        project(s)
        co.pnfree = co.s_dv.mark()
        if s == 1:
            lambdas()
        mark = co.base
        co.base = low
        pr = [alloc(co, [P, 2, 512]) for _ in range(4)]
        at_ = [alloc(co, [P, 4, P]) for _ in range(2)]
        sm, mx = alloc(co, [P, 2, 4]), alloc(co, [P, 4, 4])
        fa = counts(co)
        done = []
        spawn(co, attend(s, pr, at_, sm, mx, fa, done))
        mt = ([co.gb[:, 512:1024]], [co.pn[:, 0:512], co.pn[:, 512:1024]], [fa], [fa, fa])
        mod_groups(co, mod_part(2, 1 - s), mt, quiet=False)
        flush(co)
        co.gbfree = (co.gbfree, mt[2])
        co.pnfree = (co.pnfree, mt[3])
        co.base = low
        out_proj(co, l, s, tuple(done), (l, 0, 0) if s == 1 else (l, 1, 1))
        co.base = mark
    co.base = start


def rpb_scratch(co, z, fe):
    A = co.A
    co.dv.wait_ge(fe)
    a = co.dv.memset(z[:, :], 0.0).then_inc(co.s_dv)
    flat = A["na"].rearrange("c r h w -> (c r h w)").rearrange("(q p n) -> q p n", p=P, n=1792)
    co.po.wait_ge(a)
    d = tuple(load_small(co, flat[q], z[:, :]) for q in range(4))
    out = []
    for r in range(7):
        src = A["na_rpb_2"][0, :, r + 4, :]
        src = bass.AP(tensor=src.tensor, offset=src.offset, ap=[[0, 64]] + [list(v) for v in src.ap])
        co.po.wait_ge(d)
        out.append(load_small(co, A["na"][:, r, :, 48:79], src))
    co.nadep = tuple(out)
    yield


def odd(co):
    A, l = co.A, 1
    start = co.base
    W = A["od_w_in_2"][0]
    kt, v, qt = alloc(co, [P, 8, 512]), alloc(co, [P, 4, D]), alloc(co, [P, 8, 256])
    co.gs = alloc(co, [P, 2, 32])
    gn = alloc(co, [P, 2, 64])
    nb = alloc(co, [P, 16, 384])
    low = co.base
    tks, w1 = [alloc(co, [P, 2, 512]) for _ in range(2)], co.gb[:, :].rearrange("p (t n) -> p t n", t=2)
    fe = counts(co)
    co.gsfree = fe
    co.po.wait_ge(fe)
    gd = (load_small(co, gn[:, 0, :], A["na_q_g_2"].to_broadcast([P, 64])),
          load_small(co, gn[:, 1, :], A["na_k_g_2"].to_broadcast([P, 64])))
    ld = []
    co.po.wait_ge(co.nadep)
    for r2 in range(2):
        for i in range(6):
            src = A["na"][:, 1 - r2 + i, :, :]
            src = bass.AP(tensor=src.tensor, offset=src.offset + 63, ap=[[7 * 16 * P - 1, 64], [P, 16], [1, 64]])
            ld.append(load_small(co, nb[64 * r2:64 * r2 + 64, :, 64 * i:64 * i + 64], src))
    free = {"tk": [fe, fe]}
    busy, turn = [False, False], [0]

    def take():
        i = turn[0] % 2
        turn[0] += 1
        while busy[i]:
            advance(co)
        busy[i] = True
        return i, tks[i]

    def give(i, mark):
        free["tk"][i], busy[i] = mark, False

    dep = {"k": [], "v": [], "q": []}

    def on_heads(which, dst, c, cols):
        def evac(banks, tok):
            def gen():
                a = pair(co, tk[:, :, :], banks, tok, 0, 512, free["tk"][i])
                yield
                f = lambda t: t[:, :, :].rearrange("p t (g n) -> p t g n", n=64)
                a = groups(co, f(tk), f(w1), 64, 8, gn[:, which, :], (a, gd), fe)
                yield
                dep["qk"[which]].append(t32(co, lambda k, t: tk[:, t, k * P:(k + 1) * P], 4,
                                                 dst[:, 4 * c:4 * c + 4, cols], a, fe))
                give(i, pe_mark(co))
            i, tk = take()
            spawn(co, gen())
        return evac

    def on_v(c, s0):
        def evac(banks, tok):
            for t in range(2):
                q = co.ac if t else co.dv
                q.wait_ge(tok, fe)
                banks[t].drained = q.copy(v[:, s0 + t, c * 512:(c + 1) * 512], banks[t].ap).then_inc(co.s_ac if q is co.ac else co.s_dv)
                dep["v"].append(banks[t].drained)
        return evac

    for s in (1, 0):
        if s == 0:
            o = nb[:, :, :].rearrange("p h (i n) -> p (h i) n", n=64)
            na = co.cst[:, C_NA:C_NA + 64].unsqueeze(1).to_broadcast([P, 96, 64])
            co.dv.wait_ge(ld)
            nd = co.dv.tensor_tensor(o, o, na, ALU.add).then_inc(co.s_dv)
            co.bg.append(xnorm)
        flush(co)
        xt = (co.xh, co.xl)
        for c in range(2):
            if s == 1 and c == 1:
                xnorm = prenorm(co, l, 0, 0)
                next(xnorm)
            gemm(co, xt, co.xdep, W, 1024 + c * 512, 512, on_heads(1, kt, c, slice(256 * s, 256 * s + 256)))
            gemm(co, xt, co.xdep, W, 2048 + c * 512, 512, on_v(c, 2 * s))
        if s == 0:
            for c in range(2):
                gemm(co, xt, co.xdep, W, c * 512, 512, on_heads(0, qt, c, slice(0, 256)))
        co.xtfree = pe_mark(co)
        flush(co)
    co.base = low
    pr = [alloc(co, [P, 512]) for _ in range(4)]
    at_ = [co.pn[:, 512 * i:512 * i + 512].rearrange("p (k n) -> p k n", n=P) for i in range(2)]
    sm, mx = co.gs[:, 1, :].rearrange("p (t h) -> p t h", t=2), co.gs[:, 0, 0:4].unsqueeze(2)
    fa = counts(co)
    kd, done = tuple(dep["k"] + dep["v"] + dep["q"]), []

    def attend():
        pfree, afree, mfree = [fa] * 4, [fa] * 2, [fa] * 4
        items = [(t, h) for t in range(2) for h in range(16)]
        yb, st = {}, {}
        for i in range(len(items) + 4):
            if 1 <= i < len(items) + 1:
                r = (i - 1) % 4
                co.dv.wait_ge(st[i - 1], mfree[r])
                a = co.dv.tensor_reduce(mx[:, r, :], pr[r][:, :], AX, ALU.max).then_inc(co.s_dv)
                co.dv.wait_ge(a)
                shift = co.dv.tensor_scalar(mx[:, r, :], mx[:, r, :], -1.0, None, ALU.mult).then_inc(co.s_dv)
            if i < len(items):
                t, h = items[i]
                r = i % 4
                b = next_bank(co)
                rr = slice(64 * (h % 2), 64 * (h % 2) + 64)
                co.pe.wait_ge(kd, b.drained)
                m = co.pe.matmul(b.ap, qt[rr, h // 2, t * P:(t + 1) * P], kt[rr, h // 2, :], skip_group_check=True, start=True, stop=True).then_inc(co.s_pe)
                co.dv.wait_ge(m, nd, pfree[r])
                a = co.dv.scalar_tensor_tensor(pr[r][:, 0:256], b.ap[:, 0:256], 0.125, nb[:, h, 128 * (1 - t):128 * (1 - t) + 256], ALU.mult, ALU.add).then_inc(co.s_dv)
                score = (a, b)
            if 1 <= i < len(items) + 1:
                t, h = items[i - 1]
                r = (i - 1) % 4
                co.ac.wait_ge(shift, fa)
                st[i - 1] = mfree[r] = co.ac.activation(pr[r][:, :], pr[r][:, :], ACT.Exp, bias=mx[:, r, :], accum_out=sm[:, t, h:h + 1]).then_inc(co.s_ac)
            if i < len(items):
                r = i % 4
                a, b = score
                co.ac.wait_ge(a, pfree[r])
                c = co.ac.activation(pr[r][:, 256:512], b.ap[:, 256:512], ACT.Copy, scale=0.125).then_inc(co.s_ac)
                b.drained = st[i] = (a, c)
            if 3 <= i < len(items) + 3:
                r, q = (i - 3) % 4, i % 2
                p = pr[r]
                b = next_bank(co)
                co.pe.wait_ge(st[i - 3], b.drained)
                for k in range(4):
                    m = co.pe.transpose(b.ap[:, k * P:(k + 1) * P], p[:, k * P:(k + 1) * P], ident(co, p[:, k * P:(k + 1) * P])).then_inc(co.s_pe, k == 3)
                pfree[r] = m
                co.ac.wait_ge(m, afree[q])
                b.drained = st[i - 3] = co.ac.activation(at_[q][:, :, :], b.ap.rearrange("p (k n) -> p k n", n=P), ACT.Copy).then_inc(co.s_ac)
            yield
            if i >= 4:
                t, h = items[i - 4]
                q = (i - 1) % 2
                if h % 8 == 0:
                    yb[h // 8] = next_bank(co, hold=True)
                b = yb[h // 8]
                co.pe.wait_ge(st[i - 4], b.drained)
                for k in range(4):
                    m = co.pe.matmul(b.ap[:, (h % 8) * 64:(h % 8 + 1) * 64], at_[q][:, k, :], v[:, k, h * 64:(h + 1) * 64], start=k == 0, stop=k == 3, skip_group_check=True).then_inc(co.s_pe, k == 3)
                afree[q] = m
                if h % 8 == 7:
                    c = h // 8
                    rc = sm[:, t, 8 * c:8 * c + 8]
                    co.dv.wait_ge(m)
                    a = co.dv.reciprocal(rc, rc).then_inc(co.s_dv)
                    co.dv.wait_ge(a, co.yfree)
                    b.drained = e = co.dv.tensor_tensor(co.y[:, t, c * 512:(c + 1) * 512].rearrange("p (g n) -> p g n", n=64), b.ap.rearrange("p (g n) -> p g n", n=64), rc.unsqueeze(2).to_broadcast([P, 8, 64]), ALU.mult).then_inc(co.s_dv)
                    b.held = False
                    done.append(e)
    spawn(co, attend())
    flush(co)
    co.base = low
    co.gbfree = fa
    out_proj(co, l, 0, tuple(done), None)
    co.base = start


def first_and_second_block(nc, A, out):
    A["t5"] = nc.dram_tensor("t5_rows", [8, P, 512], F32).ap()
    A["na"] = nc.dram_tensor("rpb_rows", [64, 7, 16, P], F32).ap()
    A["gates"] = nc.dram_tensor("gate_rows", [2, 2, 2, D], F32).ap()
    with ExitStack() as ctx:
        co = new_core(nc, A, ctx, first_plan(A) + second_plan(A))
        setup(co)
        for l in range(2):
            ffn1(co, l, 0, ())
            mixer(co, l, (l, 2))
            cross(co, l, (l, 3))
            ffn1(co, l, 1, (1, 0) if l == 0 else None)
        flush(co)
        begin(co)
        even(co)
        ffn2(co, 0, 1, True, (0, 0, 1))
        ffn2(co, 0, 0, True, (1, 1, 0))
        odd(co)
        ffn2(co, 1, 0, False, None)
        flush(co)
        co.xready = co.ready[0]
        finish_out(co, out)
        emit(co)


_INS = ["x", "mem", "ln_g", "ln_b", "ffn_w_in", "ffn_w_out", "w_mix_in", "b_gate", "kv_norm_g", "w_uk", "w_uv",
        "conv_w", "w_branch", "w_mix_out", "xa_wq", "xa_wkv", "xa_wo", "rel_bias", "c_2", "ctx_2", "c_ctx_2",
        "mod_w_2", "mod_b_2", "norm_mix_g_2", "norm_ffn_g_2", "w_out_2", "ffn_w_in_2", "ffn_w_out_2", "ev_w_in_2",
        "da_q_g_2", "da_k_g_2", "da_lq1_2", "da_lk1_2", "da_lq2_2", "da_lk2_2", "da_out_g_2", "mla_q_a_g_2",
        "mla_w_uq_2", "mla_kv_a_g_2", "mla_w_ukv_2", "mla_q_g_2", "mla_k_g_2", "mla_kr_g_2", "od_w_in_2",
        "na_q_g_2", "na_k_g_2", "na_rpb_2"]


def kernel(**inputs):
    import concourse.bacc as _bacc
    from concourse.bass_utils import run_bass_kernel_spmd as _run

    nc = _bacc.Bacc("TRN2", target_bir_lowering=False, num_devices=1)
    arrays, aps = {}, {}
    given = {n: np.ascontiguousarray(inputs[n]) for n in _INS}
    given["consts"], given["buckets"], given["rope"] = constants(), bucket_table(), rope_table()
    for name, a in given.items():
        arrays[f"in_{name}"] = a
        aps[name] = nc.dram_tensor(f"in_{name}", a.shape, mybir.dt.from_np(a.dtype), kind="ExternalInput").ap()
    out = nc.dram_tensor("out_0", (1, 256, D), F32, kind="ExternalOutput").ap()
    first_and_second_block(nc, aps, out[0])
    r = _run(nc, [arrays], core_ids=[0])
    return r.results[0]["out_0"]
```
